# Optimizing a Trainium2 kernel written in Bass

```python
import math
import jax, jax.numpy as jnp
from jax import lax
import numpy as np

D_MODEL = 1024
BATCH = 1
SEQ = 512
DEPTH = 2

GRID_W = 64
CTX_LEN = 256
HEAD_DIM = 64
ROPE_BASE = 10000.0
NORM_EPS = 1e-6
NEG_INF = -1e30
F32 = jnp.float32

A_HEADS = 4
A_KV_HEADS = 2
A_GROUP = A_HEADS // A_KV_HEADS
A_WINDOW = 128
A_BLOCK = 128
B_HEADS = 4
B_QK_DIM = 64
B_V_DIM = 2 * B_QK_DIM
B_BLOCK = 128
C_HEADS = 4
C_QK_DIM = 32
C_V_DIM = 2 * C_QK_DIM
C_CHUNK = 128

A_Q = A_HEADS * HEAD_DIM
A_KV = A_KV_HEADS * HEAD_DIM
B_QK = B_HEADS * 2 * B_QK_DIM
B_V = B_HEADS * B_V_DIM
C_QK = C_HEADS * C_QK_DIM
C_V = C_HEADS * C_V_DIM
SPLIT_SIZES = (A_Q, A_KV, A_KV, B_QK, B_QK, B_V, C_QK, C_QK, C_V, C_V)
IN_WIDTH = sum(SPLIT_SIZES)
SPLIT_POINTS = tuple(int(s) for s in np.cumsum(SPLIT_SIZES)[:-1])
MIX_WIDTH = A_Q + B_V + C_V

D_FF = 2816
CONV_W = 3
N_MOD = 6

kernel_name = "hybrid_parallel_groups_diffusion_trunk"

def rms_norm(x, g):
    xf = x.astype(F32)
    y = xf * lax.rsqrt(jnp.mean(xf * xf, axis=-1, keepdims=True) + NORM_EPS)
    return (y * g.astype(F32)).astype(x.dtype)

def modulate(h, shift, scale):
    return h * (1.0 + scale) + shift

def axial_rope_tables(n_tok, dim):
    n_rows = n_tok // GRID_W
    rows = jnp.repeat(jnp.arange(n_rows, dtype=F32), GRID_W)
    cols = jnp.tile(jnp.arange(GRID_W, dtype=F32), n_rows)
    n_freq = dim // 4
    inv = ROPE_BASE ** (-jnp.arange(n_freq, dtype=F32) / n_freq)
    ang = jnp.concatenate([rows[:, None] * inv, cols[:, None] * inv], axis=-1)
    return jnp.cos(ang), jnp.sin(ang)

def apply_rope(x, cos, sin):
    half = x.shape[-1] // 2
    shp = cos.shape[:1] + (1,) * (x.ndim - 3) + cos.shape[1:]
    c = cos.reshape(shp).astype(x.dtype)
    s = sin.reshape(shp).astype(x.dtype)
    x1, x2 = x[..., :half], x[..., half:]
    return jnp.concatenate([x1 * c - x2 * s, x1 * s + x2 * c], axis=-1)

def split_projection(p):
    bsz, n = p.shape[:2]
    qa, ka, va, qb, kb, vb, qr, kr, vr, gr = jnp.split(p, SPLIT_POINTS, axis=-1)
    qa = qa.reshape(bsz, n, A_HEADS, HEAD_DIM)
    ka = ka.reshape(bsz, n, A_KV_HEADS, HEAD_DIM)
    va = va.reshape(bsz, n, A_KV_HEADS, HEAD_DIM)
    qb = qb.reshape(bsz, n, B_HEADS, 2, B_QK_DIM)
    kb = kb.reshape(bsz, n, B_HEADS, 2, B_QK_DIM)
    vb = vb.reshape(bsz, n, B_HEADS, B_V_DIM)
    qr = qr.reshape(bsz, n, C_HEADS, C_QK_DIM)
    kr = kr.reshape(bsz, n, C_HEADS, C_QK_DIM) * (C_QK_DIM ** -0.5)
    vr = vr.reshape(bsz, n, C_HEADS, C_V_DIM)
    return qa, ka, va, qb, kb, vb, qr, kr, vr, gr

def softmax_with_sink(scores, sink):
    m = jnp.maximum(jnp.max(scores, axis=-1, keepdims=True), sink)
    e = jnp.exp(scores - m)
    return e / (jnp.sum(e, axis=-1, keepdims=True) + jnp.exp(sink - m))

def window_gqa_latent(q, k, v, kc, vc, sink):
    bsz, n, _, d = q.shape
    nb = n // A_BLOCK
    scale = d ** -0.5
    qb = q.reshape(bsz, nb, A_BLOCK, A_KV_HEADS, A_GROUP, d)
    pad = ((0, 0), (A_BLOCK, A_BLOCK), (0, 0), (0, 0))
    kp = jnp.pad(k, pad).reshape(bsz, nb + 2, A_BLOCK, A_KV_HEADS, d)
    vp = jnp.pad(v, pad).reshape(bsz, nb + 2, A_BLOCK, A_KV_HEADS, d)
    kband = jnp.concatenate([kp[:, :-2], kp[:, 1:-1], kp[:, 2:]], axis=2)
    vband = jnp.concatenate([vp[:, :-2], vp[:, 1:-1], vp[:, 2:]], axis=2)
    s_loc = jnp.einsum('bnqhgd,bnkhd->bhgnqk', qb, kband).astype(F32) * scale
    s_ctx = jnp.einsum('bnqhgd,blhd->bhgnql', qb, kc).astype(F32) * scale
    qi = jnp.arange(A_BLOCK)[:, None]
    kj = jnp.arange(3 * A_BLOCK)[None, :]
    rel = kj - A_BLOCK - qi
    kpos = jnp.arange(nb)[:, None, None] * A_BLOCK - A_BLOCK + kj
    valid = (jnp.abs(rel) <= A_WINDOW)[None] & (kpos >= 0) & (kpos < n)
    s_loc = jnp.where(valid, s_loc, NEG_INF)
    scores = jnp.concatenate([s_loc, s_ctx], axis=-1)
    sink_b = sink.astype(F32).reshape(A_KV_HEADS, A_GROUP)[None, :, :, None, None, None]
    p = softmax_with_sink(scores, sink_b).astype(v.dtype)
    p_loc, p_ctx = p[..., :3 * A_BLOCK], p[..., 3 * A_BLOCK:]
    out = (jnp.einsum('bhgnqk,bnkhd->bnqhgd', p_loc, vband)
           + jnp.einsum('bhgnql,blhd->bnqhgd', p_ctx, vc))
    return out.reshape(bsz, n, A_Q)

def gqa_context(q, k, v, sink):
    bsz, n, _, d = q.shape
    qg = q.reshape(bsz, n, A_KV_HEADS, A_GROUP, d)
    s = jnp.einsum('blhgd,bmhd->bhglm', qg, k).astype(F32) * (d ** -0.5)
    sink_b = sink.astype(F32).reshape(A_KV_HEADS, A_GROUP)[None, :, :, None, None]
    p = softmax_with_sink(s, sink_b).astype(v.dtype)
    return jnp.einsum('bhglm,bmhd->blhgd', p, v).reshape(bsz, n, A_Q)

def diff_attend(q, k, v, lam):
    s = jnp.einsum('bqhcd,bkhcd->bhcqk', q, k).astype(F32) * (B_QK_DIM ** -0.5)
    p = jax.nn.softmax(s, axis=-1)
    w = p[:, :, 0] - lam * p[:, :, 1]
    return jnp.einsum('bhqk,bkhd->bqhd', w.astype(v.dtype), v)

def diff_attention_latent(q, k, v, kc, vc, lam):
    bsz, n = q.shape[:2]
    k_all = jnp.concatenate([kc, k], axis=1)
    v_all = jnp.concatenate([vc, v], axis=1)
    qblocks = jnp.moveaxis(q.reshape(bsz, n // B_BLOCK, B_BLOCK, B_HEADS, 2, B_QK_DIM), 1, 0)
    out = lax.map(lambda qb: diff_attend(qb, k_all, v_all, lam), qblocks)
    return jnp.moveaxis(out, 0, 1).reshape(bsz, n, B_HEADS, B_V_DIM)

def diff_head_norm(o, g, lam_init):
    of = o.astype(F32)
    y = of * lax.rsqrt(jnp.mean(of * of, axis=-1, keepdims=True) + NORM_EPS)
    y = y * g.astype(F32) * (1.0 - lam_init)
    return y.reshape(o.shape[0], o.shape[1], B_V).astype(o.dtype)

def retention_chunked(q, k, v, log_gamma, state0, include_diag):
    bsz, nh, n, dk = q.shape
    dv = v.shape[-1]
    nc = n // C_CHUNK
    qc = q.astype(F32).reshape(bsz, nh, nc, C_CHUNK, dk)
    kc = k.astype(F32).reshape(bsz, nh, nc, C_CHUNK, dk)
    vc = v.astype(F32).reshape(bsz, nh, nc, C_CHUNK, dv)
    idx = jnp.arange(C_CHUNK, dtype=F32)
    lg = log_gamma.astype(F32)[:, None]
    diff = idx[:, None] - idx[None, :]
    mask = (diff >= 0) if include_diag else (diff > 0)
    decay = jnp.where(mask, jnp.exp(lg[:, :, None] * jnp.maximum(diff, 0.0)), 0.0)
    att = jnp.einsum('bhncd,bhnjd->bhncj', qc, kc) * decay[None, :, None]
    intra = jnp.einsum('bhncj,bhnje->bhnce', att, vc)
    q_decay = jnp.exp(lg * (idx + 1.0))
    k_decay = jnp.exp(lg * (C_CHUNK - 1.0 - idx))
    chunk_kv = jnp.einsum('bhnjd,bhnje->bhnde', kc * k_decay[None, :, None, :, None], vc)
    chunk_decay = jnp.exp(lg * C_CHUNK)[None, :, :, None]

    def step(state, kv):
        return chunk_decay * state + kv, state

    _, prev = lax.scan(step, state0, jnp.moveaxis(chunk_kv, 2, 0))
    prev = jnp.moveaxis(prev, 0, 2)
    cross = jnp.einsum('bhncd,bhnde->bhnce', qc * q_decay[None, :, None, :, None], prev)
    return (intra + cross).reshape(bsz, nh, n, dv)

def bidir_retention(q, k, v, lg_f, lg_b, s_f, s_b):
    y_f = retention_chunked(q, k, v, lg_f, s_f, True)
    flip = lambda t: jnp.flip(t, axis=2)
    y_b = flip(retention_chunked(flip(q), flip(k), flip(v), lg_b, s_b, False))
    return y_f + y_b

def context_final_states(k, v, lg_f, lg_b):
    n = k.shape[2]
    idx = jnp.arange(n, dtype=F32)
    wf = jnp.exp(lg_f[:, None] * (n - 1.0 - idx))
    wb = jnp.exp(lg_b[:, None] * idx)
    kf = k.astype(F32)
    vf = v.astype(F32)
    s_f = jnp.einsum('bhld,bhle->bhde', kf * wf[None, :, :, None], vf)
    s_b = jnp.einsum('bhld,bhle->bhde', kf * wb[None, :, :, None], vf)
    return s_f, s_b

def retention_out(y, gate):
    yc = y - jnp.mean(y, axis=-1, keepdims=True)
    yn = yc * lax.rsqrt(jnp.mean(yc * yc, axis=-1, keepdims=True) + NORM_EPS)
    yn = jnp.swapaxes(yn, 1, 2).reshape(gate.shape)
    return (jax.nn.silu(gate.astype(F32)) * yn).astype(gate.dtype)

def dwconv3(u, w, b):
    up = jnp.pad(u, ((0, 0), (1, 1), (0, 0)))
    return up[:, :-2] * w[0] + up[:, 1:-1] * w[1] + up[:, 2:] * w[2] + b

def gated_conv_ffn(h, w_up, conv_w, conv_b, w_down):
    u = dwconv3(h @ w_up, conv_w, conv_b)
    val, gate = jnp.split(u, 2, axis=-1)
    return (jax.nn.silu(gate) * val) @ w_down

def to_bhnd(t):
    return jnp.swapaxes(t, 1, 2)

def setup_inputs(seed: int = 0) -> dict:
    key = jax.random.key(seed)
    ks = jax.random.split(key, 20)
    nrm = lambda k, shape, s: jax.random.normal(k, shape, F32) * s
    gam = 1.0 - 2.0 ** (-5.0 - np.arange(C_HEADS))
    logit0 = jnp.asarray(np.log(gam / (1.0 - gam)).astype(np.float32))
    return {
        "x": nrm(ks[0], (BATCH, SEQ, D_MODEL), 1.0),
        "c": nrm(ks[1], (BATCH, D_MODEL), 1.0),
        "ctx": nrm(ks[2], (BATCH, CTX_LEN, D_MODEL), 1.0),
        "c_ctx": nrm(ks[3], (D_MODEL,), 1.0),
        "w_mod": nrm(ks[4], (DEPTH, D_MODEL, N_MOD * D_MODEL), D_MODEL ** -0.5),
        "b_mod": nrm(ks[5], (DEPTH, N_MOD * D_MODEL), 0.01),
        "norm1_g": 1.0 + nrm(ks[6], (DEPTH, D_MODEL), 0.01),
        "norm2_g": 1.0 + nrm(ks[7], (DEPTH, D_MODEL), 0.01),
        "w_in": nrm(ks[8], (DEPTH, D_MODEL, IN_WIDTH), D_MODEL ** -0.5),
        "w_out": nrm(ks[9], (DEPTH, MIX_WIDTH, D_MODEL), MIX_WIDTH ** -0.5),
        "attn_sink": nrm(ks[10], (DEPTH, A_HEADS), 0.5),
        "diff_lambda": nrm(ks[11], (DEPTH, 4, B_QK_DIM), 0.1),
        "diff_subln_g": 1.0 + nrm(ks[12], (DEPTH, B_V_DIM), 0.01),
        "ret_decay_logit": logit0[None, None, :] + nrm(ks[13], (DEPTH, 2, C_HEADS), 0.01),
        "w_up": nrm(ks[14], (DEPTH, D_MODEL, 2 * D_FF), D_MODEL ** -0.5),
        "conv_w": nrm(ks[15], (DEPTH, CONV_W, 2 * D_FF), CONV_W ** -0.5),
        "conv_b": nrm(ks[16], (DEPTH, 2 * D_FF), 0.01),
        "w_down": nrm(ks[17], (DEPTH, D_FF, D_MODEL), D_FF ** -0.5),
        "final_g": 1.0 + nrm(ks[18], (D_MODEL,), 0.01),
    }

def reference(x, c, ctx, c_ctx, w_mod, b_mod, norm1_g, norm2_g, w_in, w_out, attn_sink,
              diff_lambda, diff_subln_g, ret_decay_logit, w_up, conv_w, conv_b, w_down, final_g):
    bsz, n_lat = x.shape[0], x.shape[1]
    cos_h, sin_h = axial_rope_tables(n_lat, HEAD_DIM)
    cos_r, sin_r = axial_rope_tables(n_lat, C_QK_DIM)
    zero_state = jnp.zeros((bsz, C_HEADS, C_QK_DIM, C_V_DIM), F32)
    xc = ctx
    for l in range(DEPTH):
        is_last = l == DEPTH - 1
        lam_init = 0.8 - 0.6 * math.exp(-0.3 * l)
        mod = jax.nn.silu(c) @ w_mod[l] + b_mod[l]
        mod_c = jax.nn.silu(c_ctx) @ w_mod[l] + b_mod[l]
        sh1, sc1, g1, sh2, sc2, g2 = [m[:, None, :] for m in jnp.split(mod, N_MOD, axis=-1)]
        csh1, csc1, cg1, csh2, csc2, cg2 = jnp.split(mod_c, N_MOD, axis=-1)

        h = modulate(rms_norm(x, norm1_g[l]), sh1, sc1)
        hc = modulate(rms_norm(xc, norm1_g[l]), csh1, csc1)
        qa, ka, va, qb, kb, vb, qr, kr, vr, gr = split_projection(h @ w_in[l])
        qa_c, ka_c, va_c, qb_c, kb_c, vb_c, qr_c, kr_c, vr_c, gr_c = split_projection(hc @ w_in[l])

        qa, ka = apply_rope(qa, cos_h, sin_h), apply_rope(ka, cos_h, sin_h)
        qb, kb = apply_rope(qb, cos_h, sin_h), apply_rope(kb, cos_h, sin_h)
        qr, kr = apply_rope(qr, cos_r, sin_r), apply_rope(kr, cos_r, sin_r)

        lq1, lk1, lq2, lk2 = diff_lambda[l].astype(F32)
        lam = jnp.exp(jnp.sum(lq1 * lk1)) - jnp.exp(jnp.sum(lq2 * lk2)) + lam_init
        log_g = jax.nn.log_sigmoid(ret_decay_logit[l].astype(F32))
        lg_f, lg_b = log_g[0], log_g[1]
        qr_c, kr_c, vr_c = to_bhnd(qr_c), to_bhnd(kr_c), to_bhnd(vr_c)
        s_f, s_b = context_final_states(kr_c, vr_c, lg_f, lg_b)

        a_out = window_gqa_latent(qa, ka, va, ka_c, va_c, attn_sink[l])
        b_out = diff_head_norm(diff_attention_latent(qb, kb, vb, kb_c, vb_c, lam),
                               diff_subln_g[l], lam_init)
        c_out = retention_out(bidir_retention(to_bhnd(qr), to_bhnd(kr), to_bhnd(vr),
                                              lg_f, lg_b, s_f, s_b), gr)
        mix = jnp.concatenate([a_out, b_out.astype(a_out.dtype), c_out.astype(a_out.dtype)], axis=-1)
        x_new = x + g1 * (mix @ w_out[l])
        h2 = modulate(rms_norm(x_new, norm2_g[l]), sh2, sc2)
        x_new = x_new + g2 * gated_conv_ffn(h2, w_up[l], conv_w[l], conv_b[l], w_down[l])

        if not is_last:
            a_c = gqa_context(qa_c, ka_c, va_c, attn_sink[l])
            b_c = diff_head_norm(diff_attend(qb_c, kb_c, vb_c, lam), diff_subln_g[l], lam_init)
            c_c = retention_out(bidir_retention(qr_c, kr_c, vr_c, lg_f, lg_b, zero_state, zero_state),
                                gr_c)
            mix_c = jnp.concatenate([a_c, b_c.astype(a_c.dtype), c_c.astype(a_c.dtype)], axis=-1)
            xc = xc + cg1 * (mix_c @ w_out[l])
            hc2 = modulate(rms_norm(xc, norm2_g[l]), csh2, csc2)
            xc = xc + cg2 * gated_conv_ffn(hc2, w_up[l], conv_w[l], conv_b[l], w_down[l])
        x = x_new
    return rms_norm(x, final_g)


_drawn_inputs = setup_inputs


def setup_inputs(seed=0):
    import zlib

    import numpy as np

    out = dict(_drawn_inputs(seed))
    spreads = {}
    factors = {'norm1_g': 7.457,
     'norm2_g': 5.979,
     'attn_sink': 8.0,
     'diff_subln_g': 22.355,
     'conv_b': 6.992,
     'final_g': 31.833}
    for name, (base, spread) in spreads.items():
        noise = np.random.default_rng([zlib.crc32(name.encode()), seed]).standard_normal(out[name].shape)
        drawn = base * np.exp(spread * noise) if base else spread * noise
        out[name] = __import__('jax').numpy.asarray(drawn.astype(out[name].dtype))
    for name, factor in factors.items():
        out[name] = (out[name] * factor).astype(out[name].dtype)
    return out
```

```python
from contextlib import ExitStack
import math

import numpy as np

import concourse.bass as bass
from concourse import mybir

F32 = mybir.dt.float32
F32R = mybir.dt.float32r
ACT = mybir.ActivationFunctionType
ALU = mybir.AluOpType
AXX = mybir.AxisListType.X

P = 128
D, KD8, LAT, CTX, LAYERS = 1024, 8, 512, 256, 2
TOK = LAT + CTX
EPS = 1e-6
GRID_W, ROPE_BASE = 64, 10000.0
FF, KH = 2816, 11
HD = 64
SCALE = HD ** -0.5
CQ = 32
T_KA, T_KB, T_KR, T_VA, T_GR, T_QA, T_QB, T_QR, N_IN = 0, 1, 5, 6, 13, 15, 17, 21, 22
N_KV = 13
V_A, V_B, V_C, V_G, V_W = 0, 128, 640, 896, 1152
SEGS = [("in_kv", N_KV, 8), ("in_q", N_IN - N_KV, 8), ("out", 8, 8),
        ("up0", 22, 8), ("down0", 8, KH), ("up1", 22, 8), ("down1", 8, KH)]
PER_LAYER = sum(n for _, n, _ in SEGS)
MODS = 48
BM, N1, N2, CW, SG, SK, DZ, VL = 0, 96, 112, 128, 304, 305, 309, 319
K_ID, K_S64, K_S32, K_ONE, K_BAND, K_BD, K_KJ, K_W = 0, 128, 256, 384, 512, 896, 1152, 1154
R_C64, R_S64, R_C32, R_S32, R_C1, R_C2, R_DP, R_DN, R_MG, R_ML, R_W = (
    0, 512, 1024, 1536, 2048, 2176, 2304, 2432, 2560, 2688, 2816)


def constants():
    k = np.zeros((P, K_W), np.float32)
    i = np.arange(P)
    k[:, K_ID:K_ID + P] = np.eye(P)
    k[i, K_S64 + (i ^ 32)] = 1
    k[i, K_S32 + (i ^ 16)] = 1
    k[:, K_ONE:K_ONE + P] = 1
    k[:, K_BAND:K_BAND + P] = np.where(i[None] >= i[:, None], 0, -1e30)
    k[:, K_BAND + 2 * P:K_BAND + 3 * P] = np.where(i[None] <= i[:, None], 0, -1e30)
    k[:, K_BD:K_BD + 256] = (i[:, None] // CQ) == (np.arange(256)[None] // 64)
    k[:, K_KJ], k[:, K_KJ + 1] = P - 1 - i, i
    r = np.zeros((P, R_W), np.float32)
    rows = np.repeat(np.arange(LAT // GRID_W, dtype=np.float32), GRID_W)
    cols = np.tile(np.arange(GRID_W, dtype=np.float32), LAT // GRID_W)
    for dim, c, s in ((HD, R_C64, R_S64), (CQ, R_C32, R_S32)):
        nf = dim // 4
        inv = (np.float32(ROPE_BASE) ** (-np.arange(nf, dtype=np.float32) / np.float32(nf))).astype(np.float32)
        ang = np.concatenate([rows[:, None] * inv, cols[:, None] * inv], -1).T.astype(np.float32)
        f = i % (dim // 2)
        r[:, c:c + LAT] = np.cos(ang)[f]
        r[:, s:s + LAT] = np.where((i % dim < dim // 2)[:, None], -np.sin(ang)[f], np.sin(ang)[f])
    r[:, R_C1:R_C1 + P] = i[None] + 1
    r[:, R_C2:R_C2 + P] = P - i[None]
    d = i[None] - i[:, None]
    r[:, R_DP:R_DP + P] = np.maximum(d, 0)
    r[:, R_DN:R_DN + P] = np.maximum(-d, 0)
    r[:, R_MG:R_MG + P] = (d >= 0) * np.float32(CQ ** -0.5)
    r[:, R_ML:R_ML + P] = (d < 0) * np.float32(CQ ** -0.5)
    return k, r


def attention_steps(l):
    steps = []
    for h in range(4):
        steps += [("B", h, q, [(0, 0, LAT), (LAT, LAT, CTX)], [0, 1, 2, 3, 4, 5]) for q in range(4)]
        if l == 0:
            steps += [("B", h, q, [(0, LAT, CTX)], [4, 5]) for q in (4, 5)]
    for g in range(2):
        for q in range(4):
            b = list(range(max(0, q - 1), min(3, q + 1) + 1))
            steps.append(("A", g, q, [(0, b[0] * P, len(b) * P), (LAT, LAT, CTX)], b + [4, 5]))
        if l == 0:
            steps += [("A", g, q, [(0, LAT, CTX)], [4, 5]) for q in (4, 5)]
    return steps


def turn_groups(steps):
    groups, ends = [], []
    for s, (kind, h, *_) in enumerate(steps):
        if kind == "B":
            groups.append((s, 0, V_B + P * h, P, 256 + P * h))
        else:
            groups += [(s, c, V_A + HD * h, HD, HD * (2 * h + c)) for c in range(2)]
        ends.append(len(groups))
    return groups, ends


def trunk(nc, xin, cin, wk8, wk11, wmod, vin, finalg, lamin, kin, rin, out):
    base, seg_at, n, a8, a11 = {}, {}, 0, 0, 0
    for l in range(LAYERS):
        for name, cnt, k in SEGS:
            seg_at[l, name] = (n, cnt, k, a8 if k == 8 else a11)
            n += cnt
            if k == 8:
                a8 += cnt
            else:
                a11 += cnt
    seg_end = {key: v[0] + v[1] for key, v in seg_at.items()}

    def groups_of(l, name):
        return [(0, LAT), (LAT, TOK)] if l == 0 or name == "in_kv" else [(0, LAT)]

    def tiles_of(l):
        return 6 if l == 0 else 4

    stack = ExitStack()
    with stack:
        def sb(name, cols, dt=F32, rows=P):
            return stack.enter_context(nc.sbuf_tensor(name, [rows, cols], dt))

        xT = sb("xT", KD8 * TOK)[:, :].rearrange("p (k t) -> p k t", k=KD8)
        with ExitStack() as own:
            hT = own.enter_context(nc.sbuf_tensor("hT", [P, 2 * KD8 * TOK], F32R))
        with ExitStack() as own:
            vtok = own.enter_context(nc.sbuf_tensor("vtok", [P, 6 * V_W], F32))
            hm = own.enter_context(nc.sbuf_tensor("attn_scratch", [P, 2 * KD8 * TOK - 6 * V_W], F32))
        hold = sb("hT_bytes", 2 * KD8 * TOK)
        with ExitStack() as own:
            gT = own.enter_context(nc.sbuf_tensor("gT", [P, 2 * KH * TOK], F32R))
        pTt = sb("pT", N_IN * TOK)
        raw = [sb(f"raw{j}", KH * P) for j in range(2)]
        wsp = [sb(f"wsplit{j}", 2 * KH * P, F32R) for j in range(2)]
        tm = sb("tmp", 3072)
        mraw = [sb(f"modraw{j}", KD8 * P) for j in range(2)]
        kc = sb("consts", K_W)
        vec = sb("vec", LAYERS * VL)
        fing = sb("fing", KD8)
        cs = sb("c_in", 16)
        csil = sb("c_silu", 16)
        modv = sb("modv", 96)
        Amul = sb("Amul", 32)
        qdec = sb("qdec", 256)
        mdec = sb("mdec", 512)
        kdec = sb("kdec", 8)
        gch = sb("gch", 2)
        lg = sb("lg", 20)
        sm = sb("small", 5 * 72 + 48)
        nlam = sb("nlam", 2)
        fsc = sb("fsc", 8)
        rsd = sb("rsd", 16)
        ssb = sb("ssb", 24)
        cst = sb("cstat", 96)
        eps = sb("eps", 1)
        G = [stack.enter_context(nc.psum_tensor(f"G{j}", [P, 1024], F32)) for j in range(2)]
        X0 = stack.enter_context(nc.psum_tensor("X0", [P, 1024], F32))
        X1 = stack.enter_context(nc.psum_tensor("X1", [P, 1024], F32))
        M = X1[:, 512:704].rearrange("p (m c) -> p m c", c=2)

        hTv = hT[:, :].rearrange("p (s k t) -> p s k t", s=2, k=KD8)
        gTv = gT[:, :].rearrange("p (s k t) -> p s k t", s=2, k=KH)
        pT = pTt[:, :].rearrange("p (k t) -> p k t", k=N_IN)
        mix = pTt[:, T_VA * TOK:T_VA * TOK + 6 * D].rearrange("p (t f) -> p t f", t=6)
        ysb = pTt[:, TOK:3 * TOK].rearrange("p (n e) -> p n e", n=6)
        ysq = pTt[:, 3 * TOK:5 * TOK].rearrange("p (n e) -> p n e", n=6)
        sgr = pTt[:, T_QB * TOK:(T_QB + 2) * TOK].rearrange("p (n e) -> p n e", n=6)
        vt = vtok[:, :].rearrange("p (t f) -> p t f", t=6)
        Pb = [[hm[:, (2 * p + c) * TOK:(2 * p + c + 1) * TOK] for c in range(2)] for p in range(2)]
        WT = [hm[:, (4 + p) * TOK:(5 + p) * TOK] for p in range(2)]
        ropeA = [hm[:, j * LAT:(j + 1) * LAT] for j in range(2)]
        ropeB = [hm[:, (2 + j) * LAT:(3 + j) * LAT] for j in range(2)]
        dexp = hm[:, 2048:3072].rearrange("p (e c) -> p e c", e=8)
        states = hm[:, 0:3072].rearrange("p (d n e) -> p d n e", d=2, n=6)
        kdk = hm[:, 3072:4608].rearrange("p (d n e) -> p d n e", d=2, n=6)
        Wv = [[wsp[j][:, s * KH * P:(s + 1) * KH * P].rearrange("p (k m) -> p k m", k=KH) for s in range(2)]
              for j in range(2)]
        mrv = [m[:, :].rearrange("p (k m) -> p k m", k=KD8) for m in mraw]
        csv = csil[:, :].rearrange("p (k c) -> p k c", k=KD8)
        mv = modv[:, :].rearrange("p (m c) -> p m c", c=2)
        Av = Amul[:, :].rearrange("p (w k c) -> p w k c", w=2, k=KD8)
        rope = tm[:, 0:R_W]
        ident, ones = kc[:, K_ID:K_ID + P], kc[:, K_ONE:K_ONE + P]
        dg = tm[:, 1536:1536 + TOK]
        MX, NB, LS, ES, PR, RI = (sm[:, j * 72:(j + 1) * 72] for j in range(5)) if False else (
            sm[:, 0:72], sm[:, 72:144], sm[:, 144:216], sm[:, 216:288], sm[:, 288:360], sm[:, 360:408])

        def vecs(l, a, w):
            return vec[:, l * VL + a:l * VL + a + w]

        def sem(name):
            return stack.enter_context(nc.semaphore(name))

        loaded = sem("inputs_loaded")
        ropeld = sem("rope_tables_loaded")
        w_landed = [sem(f"weights_landed{j}") for j in range(2)]
        w_hi, w_lo = sem("weights_hi"), sem("weights_lo")
        used = sem("unit_multiplied")
        ev = sem("unit_evacuated")
        m_landed = [sem(f"mod_landed{j}") for j in range(2)]
        m_used = sem("mod_unit_multiplied")
        c_ready = sem("c_silu_ready")
        modok = sem("modulation_ready")
        sqd, ssd, srt, rsdn, dgd, rbd = (sem(x) for x in (
            "squares_ready", "sums_ready", "roots_ready", "rstd_ready", "diag_ready", "rstd_spread"))
        vsd, hid, hlo = sem("scaled_ready"), sem("operand_hi"), sem("operand_lo")
        accr = sem("conv_centre_ready")
        convl = sem("conv_left_added")
        silud, prodd, ghi, glo = sem("gate_silu"), sem("gated"), sem("gated_hi"), sem("gated_lo")
        dv = sem("vector_chain")
        tabs_a = sem("table_exps")
        start_a = sem("start_act")
        start_v = sem("start_vec")
        stored = sem("stored")
        fin = sem("final_rows")

        class Layer:
            pass
        L = []
        for l in range(LAYERS):
            o = Layer()
            o.rot, o.rsin, o.rcos, o.rdone = (sem(f"{x}{l}") for x in ("rot", "rope_sin", "rope_cos", "roped"))
            o.vt, o.vc = sem(f"values_turned{l}"), sem(f"values_copied{l}")
            o.tab = sem(f"tables{l}")
            o.sc = [sem(f"scores{c}_{l}") for c in range(2)]
            o.nb = [sem(f"negmax{c}_{l}") for c in range(2)]
            o.ex = [sem(f"exp{c}_{l}") for c in range(2)]
            o.cx = [sem(f"ctx_copied{c}_{l}") for c in range(2)]
            o.es = [sem(f"sink_exp{c}_{l}") for c in range(2)]
            o.wr, o.tr, o.te, o.pv, o.oe = (sem(f"{x}{l}") for x in (
                "probs_ready", "probs_turned", "turned_copied", "values_mixed", "mixed_copied"))
            o.kt, o.kd, o.kv, o.st = (sem(f"{x}{l}") for x in ("k_turned", "k_decayed", "kv_ready", "state_ready"))
            o.qd, o.at, o.ad, o.y, o.yc = (sem(f"{x}{l}") for x in (
                "q_decayed", "ret_scores", "ret_decayed", "ret_out", "ret_copied"))
            o.ga = sem(f"group_act{l}")
            o.mixed = sem(f"mixed_rows{l}")
            o.mt, o.mh, o.ml = (sem(f"{x}{l}") for x in ("mixed_turned", "mixed_hi", "mixed_lo"))
            L.append(o)

        def unit_loop(eng, l, name, body, head=0, tail=0):
            cnt = seg_at[l, name][1]
            tail += (cnt - head - tail) % 2
            for r in range(head):
                body(r, 0)
            if cnt - head - tail:
                with eng.Fori(0, (cnt - head - tail) // 2) as i:
                    body(head, i)
                    body(head + 1, i)
            for r in range(cnt - tail, cnt):
                body(r, 0)

        def flat(ap):
            return ap.rearrange("p a t -> p (a t)")

        block = stack.enter_context(nc.Block())

        @block.sync
        def _(sp):
            def weights(l, name, head=0, tail=0):
                n0, cnt, k, a0 = seg_at[l, name]
                src = wk8 if k == 8 else wk11

                def load(r, i):
                    n = n0 + r
                    if n >= 2:
                        sp.wait_ge(w_lo, 2 * i + (n - 1))
                    row = src[a0 + r] if isinstance(i, int) else flat(
                        src[bass.ds(2 * i + (a0 + r), 1)].rearrange("o p c -> p o c"))
                    sp.dma_start(raw[n % 2][:, 0:k * P], row).then_inc(w_landed[n % 2], 16)
                unit_loop(sp, l, name, load, head=2 if n0 == 0 else 0)

            def mod(m, i=0):
                if m >= 2:
                    sp.wait_ge(m_used, 2 * i + (m - 1))
                row = wmod[m] if isinstance(i, int) else flat(
                    wmod[bass.ds(2 * i + m, 1)].rearrange("o p c -> p o c"))
                sp.dma_start(mraw[m % 2][:, :], row).then_inc(m_landed[m % 2], 16)

            sp.dma_start(cs[:, :], cin).then_inc(loaded, 16)
            sp.dma_start(kc[:, :], kin).then_inc(loaded, 16)
            sp.dma_start(vec[:, :], vin).then_inc(loaded, 16)
            sp.dma_start(fing[:, :], finalg).then_inc(loaded, 16)
            sp.dma_start(tm[:, 0:512], lamin).then_inc(loaded, 16)
            mod(0)
            mod(1)
            sp.dma_start(flat(xT), xin).then_inc(loaded, 16)
            for m in range(2, 16):
                mod(m)
            for l in range(LAYERS):
                o = L[l]
                weights(l, "in_kv")
                sp.wait_ge(hlo, 16 * l + 8)
                sp.dma_start(rope, rin).then_inc(ropeld, 16)
                weights(l, "in_q")
                if l == 0:
                    for m in range(16, MODS):
                        mod(m)
                weights(l, "out")
                for hf in range(2):
                    if l == 0:
                        n0, cnt, _, a0 = seg_at[l, f"up{hf}"]
                        with sp.Fori(0, cnt // 2) as i:
                            for j in range(2):
                                sp.wait_ge(w_lo, 2 * i + (n0 + j - 1))
                                sp.dma_start(raw[(n0 + j) % 2][:, 0:KD8 * P], flat(
                                    wk8[bass.ds(2 * i + (a0 + j), 1)].rearrange("o p c -> p o c"))
                                ).then_inc(w_landed[(n0 + j) % 2], 16)
                            for j in range(2):
                                mod(MODS + cnt * hf + j, i)
                    else:
                        weights(l, f"up{hf}")
                    weights(l, f"down{hf}")
                if l == 0:
                    for m in range(MODS + 44, 2 * MODS):
                        mod(m)
            for k in range(KD8):
                sp.wait_ge(fin, k + 1)
                sp.dma_start(out[:, k, :], pT[:, 8 + k, 0:LAT]).then_inc(stored, 16)
            sp.wait_ge(stored, 16 * KD8)

        @block.gpsimd
        def _(pool):
            def residues(l, name):
                n0, cnt, k, _ = seg_at[l, name]

                def lo(r, i):
                    j = (n0 + r) % 2
                    pool.wait_ge(w_hi, 2 * i + (n0 + r + 1))
                    nc.gpsimd.tensor_tensor(wsp[j][:, KH * P:KH * P + k * P], raw[j][:, 0:k * P],
                                            wsp[j][:, 0:k * P].bitcast(F32), ALU.subtract).then_inc(w_lo, 1)
                unit_loop(pool, l, name, lo)

            for l in range(LAYERS):
                o = L[l]
                residues(l, "in_kv")
                residues(l, "in_q")
                pool.wait_ge(ev, seg_end[l, "in_q"])
                pool.wait_ge(ropeld, 16 * (l + 1))
                for i, (t, w) in enumerate(ROPED):
                    if i >= 2:
                        pool.wait_ge(o.rdone, i - 1)
                    c = R_C64 if w == HD else R_C32
                    nc.gpsimd.tensor_tensor(ropeB[i % 2], pT[:, t, 0:LAT], rope[:, c:c + LAT],
                                            ALU.mult).then_inc(o.rcos, 1)
                outs = range(tiles_of(l))
                groups, ends = turn_groups(attention_steps(l))
                pool.wait_ge(o.oe, len(groups))
                pool.wait_ge(o.tab, 1)
                for j, n in enumerate(outs):
                    if j >= 2:
                        pool.wait_ge(o.y, j - 1)
                    for d in range(2):
                        nc.gpsimd.tensor_tensor(tm[:, 512 + 256 * (j % 2) + P * d:][:, 0:P],
                                                pT[:, T_QR, n * P:(n + 1) * P],
                                                qdec[:, d * P:(d + 1) * P], ALU.mult).then_inc(o.qd, 1)
                    nc.gpsimd.tensor_tensor(
                        tm[:, 2048 + 512 * (j % 2):2560 + 512 * (j % 2)].rearrange("p (h c) -> p h c", h=4),
                        pT[:, T_QR, n * P:(n + 1) * P].unsqueeze(1).to_broadcast([P, 4, P]),
                        kc[:, K_BD:K_BD + 256:64].unsqueeze(2).to_broadcast([P, 4, P]),
                        ALU.mult).then_inc(o.qd, 1)
                for name in ("out", "up0", "down0", "up1", "down1"):
                    residues(l, name)

        @block.scalar
        def _(act):
            def split_hi(l, name, r, i=0):
                n0, cnt, k, _ = seg_at[l, name]
                n = n0 + r
                act.wait_ge(w_landed[n % 2], 16 * i + 16 * (n // 2 + 1))
                if n >= 2:
                    act.wait_ge(used, 2 * i + (n - 1))
                nc.scalar.activation(wsp[n % 2][:, 0:k * P], raw[n % 2][:, 0:k * P], ACT.Copy).then_inc(w_hi, 1)

            def norm(ni, l, nt, shift=None, width=TOK):
                for k in range(KD8):
                    nc.scalar.activation(pT[:, k, 0:width], xT[:, k, 0:width], ACT.Square).then_inc(sqd, 1)
                act.wait_ge(ssd, ni + 1)
                nc.scalar.activation(rsd[:, 0:nt], X1[:, 0:nt], ACT.Sqrt, bias=eps[:, 0:1],
                                     scale=1.0 / D).then_inc(srt, 1)

            def operand(ni, w, gr):
                for k in range(KD8):
                    act.wait_ge(vsd, 8 * ni + k + 1)
                    for g, (a, b) in enumerate(gr):
                        ins = nc.scalar.activation(hTv[:, 0, k, a:b], tm[:, (k % 2) * TOK + a:(k % 2) * TOK + b],
                                                   ACT.Identity, bias=mv[:, 24 * w + k, g:g + 1])
                    ins.then_inc(hid, 1)

            act.wait_ge(loaded, 96)
            nc.scalar.activation(csil[:, :], cs[:, :], ACT.Silu).then_inc(c_ready, 1)
            act.wait_ge(start_v, 2)
            nc.scalar.activation(cst[:, 20:40], cst[:, 0:20], ACT.Exp, scale=-1.0).then_inc(start_a, 1)
            nc.scalar.activation(cst[:, 44:48], cst[:, 40:44], ACT.Exp).then_inc(start_a, 1)
            act.wait_ge(start_v, 3)
            nc.scalar.activation(cst[:, 50:70], cst[:, 70:90], ACT.Ln).then_inc(start_a, 1)
            for l in range(LAYERS):
                o = L[l]
                if l:
                    act.wait_ge(ev, seg_end[0, "down1"])
                norm(2 * l, l, 6)
                split_hi(l, "in_kv", 0)
                operand(2 * l, 0, [(0, LAT), (LAT, TOK)])
                for name, nxt in (("in_kv", "in_q"), ("in_q", None)):
                    n0, cnt, k, _ = seg_at[l, name]
                    t0 = 0 if name == "in_kv" else N_KV
                    width = groups_of(l, name)[-1][1]

                    def project(r, i):
                        if r + 1 < cnt:
                            split_hi(l, name, r + 1, i)
                        elif nxt:
                            split_hi(l, nxt, 0)
                        act.wait_ge(used, 2 * i + (n0 + r + 1))
                        nc.scalar.activation(flat(pT[:, bass.ds(2 * i + (t0 + r), 1), 0:width]),
                                             G[(n0 + r) % 2][:, 0:width], ACT.Copy).then_inc(ev, 1)
                    unit_loop(act, l, name, project, head=1 if n0 == 0 else 0, tail=1)
                act.wait_ge(ropeld, 16 * (l + 1))
                act.wait_ge(used, seg_end[l, "in_q"])
                for d, c in ((0, R_C1), (1, R_C2)):
                    nc.scalar.activation(qdec[:, d * P:(d + 1) * P], rope[:, c:c + P], ACT.Exp,
                                         scale=lg[:, 10 * l + 8 + d:10 * l + 9 + d]).then_inc(tabs_a, 1)
                    nc.scalar.activation(kdec[:, 4 * d:4 * d + 4], lg[:, 10 * l + 4 * d:10 * l + 4 * d + 4], ACT.Exp,
                                         scale=kc[:, K_KJ + d:K_KJ + d + 1]).then_inc(tabs_a, 1)
                nc.scalar.activation(gch[:, :], lg[:, 10 * l + 8:10 * l + 10], ACT.Exp,
                                     scale=float(P)).then_inc(tabs_a, 1)
                for h in range(4):
                    for d, c in ((0, R_DP), (1, R_DN)):
                        nc.scalar.activation(dexp[:, 2 * h + d, :], rope[:, c:c + P], ACT.Exp,
                                             scale=lg[:, 10 * l + 4 * d + h:][:, 0:1]).then_inc(tabs_a, 1)
                for v in range(9):
                    nt = 6 if v < 7 else tiles_of(l)
                    act.wait_ge(o.vt, v + 1)
                    nc.scalar.activation(vt[:, 0:nt, v * P:(v + 1) * P],
                                         G[v % 2][:, 0:nt * P].rearrange("p (t c) -> p t c", t=nt),
                                         ACT.Copy).then_inc(o.vc, 1)
                steps = attention_steps(l)
                groups, ends = turn_groups(steps)

                def copy_out(t):
                    s, c, _, w, col = groups[t]
                    kind, h, q = steps[s][:3]
                    act.wait_ge(o.pv, t + 1)
                    first = nc.scalar.activation(mix[:, q, col:col + w], X1[:, 0:w], ACT.Copy, scale=RI[:, t:t + 1])
                    if kind == "B":
                        if t:
                            act.wait_ge(o.oe, t)
                        first = nc.scalar.activation(tm[:, 2944:2944 + P], X1[:, 0:P], ACT.Square,
                                                     scale=RI[:, t:t + 1], accum_out=ssb[:, 4 * q + h:4 * q + h + 1])
                    first.then_inc(o.oe, 1)

                for s in range(len(steps) + 1):
                    if s < len(steps):
                        kind, h, q, spans, keys = steps[s]
                        p, nk = s % 2, P * len(keys)
                        if s == 0:
                            act.wait_ge(o.rdone, len(ROPED))
                            act.wait_ge(o.tab, 1)
                        if s >= 2:
                            act.wait_ge(o.tr, ends[s - 2])
                        if kind == "A":
                            for c in range(2):
                                act.wait_ge(o.sc[c], s + 1)
                                sc0, _, w = spans[-1]
                                nc.scalar.activation(Pb[p][c][:, nk - w:nk], G[c][:, sc0:sc0 + w],
                                                     ACT.Copy).then_inc(o.cx[c], 1)
                        for c in range(2):
                            m = 2 * s + c
                            act.wait_ge(o.nb[c], s + 1)
                            src = G[c] if kind == "B" else Pb[p][c]
                            nc.scalar.activation(Pb[p][c][:, 0:nk], src[:, 0:nk], ACT.Exp, bias=NB[:, m:m + 1],
                                                 scale=SCALE, accum_out=LS[:, m:m + 1]).then_inc(o.ex[c], 1)
                            if kind == "A":
                                hd = 2 * h + c
                                nc.scalar.activation(ES[:, m:m + 1], vecs(l, SK + hd, 1), ACT.Exp,
                                                     bias=NB[:, m:m + 1]).then_inc(o.es[c], 1)
                    if s >= 1:
                        for t in range(ends[s - 2] if s >= 2 else 0, ends[s - 1]):
                            nk = P * len(steps[groups[t][0]][4])
                            act.wait_ge(o.tr, t + 1)
                            if t >= 2:
                                act.wait_ge(o.pv, t - 1)
                            nc.scalar.activation(WT[t % 2][:, 0:nk], X0[:, 0:nk], ACT.Copy).then_inc(o.te, 1)
                            if t >= 1:
                                copy_out(t - 1)
                copy_out(len(groups) - 1)
                nt = tiles_of(l)
                for j in range(nt):
                    act.wait_ge(o.y, j + 1)
                    nc.scalar.activation(ysb[:, j, :], G[1][:, 512 * (j % 2):512 * (j % 2) + 256],
                                         ACT.Copy).then_inc(o.yc, 1)
                act.wait_ge(o.mixed, 1)
                nc.scalar.activation(ysq[:, 0:nt, :], ysb[:, 0:nt, :], ACT.Square).then_inc(o.ga, 1)
                nc.scalar.activation(sgr[:, 0:nt, :], vt[:, 0:nt, V_G:V_G + 256], ACT.Silu).then_inc(o.ga, 1)
                nc.scalar.activation(cst[:, 0:4 * nt], ssb[:, 0:4 * nt], ACT.Sqrt, bias=eps[:, 0:1],
                                     scale=1.0 / P).then_inc(o.ga, 1)
                act.wait_ge(o.mixed, 2)
                nc.scalar.activation(cst[:, 24:24 + 4 * nt], cst[:, 72:72 + 4 * nt], ACT.Sqrt, bias=eps[:, 0:1],
                                     scale=1.0 / 64).then_inc(o.ga, 1)
                split_hi(l, "out", 0)
                for f in range(KD8):
                    act.wait_ge(o.mt, f + 1)
                    nc.scalar.activation(hTv[:, 0, f, 0:nt * P], G[f % 2][:, 0:nt * P], ACT.Copy,
                                         scale=fsc[:, f:f + 1]).then_inc(o.mh, 1)
                for r in range(1, 8):
                    split_hi(l, "out", r)
                act.wait_ge(ev, seg_end[l, "out"])
                width = TOK if l == 0 else LAT
                norm(2 * l + 1, l, nt, width=width)
                split_hi(l, "up0", 0)
                operand(2 * l + 1, 1, groups_of(l, "up0"))
                accs = (tm[:, 0:TOK], tm[:, TOK:2 * TOK])
                for hf in range(2):
                    name, down = f"up{hf}", f"down{hf}"
                    n0, cnt, _, _ = seg_at[l, name]
                    g0 = (2 * l + hf) * KH

                    def pair(r, i, last=False):
                        for j in range(2):
                            if j == 0:
                                split_hi(l, name, r + 1, i)
                            elif not last:
                                split_hi(l, name, r + 2, i)
                            else:
                                split_hi(l, down, 0)
                            act.wait_ge(used, 2 * i + (n0 + r + j + 1))
                            pr = g0 + r // 2
                            if pr:
                                act.wait_ge(glo if j == 0 else prodd, i + pr)
                            cw = vecs(l, CW, 176).rearrange("p (u w) -> p u w", w=4)[
                                :, bass.ds(2 * i + (hf * 22 + r + j), 1), :].rearrange("p a w -> p (a w)")
                            nc.scalar.activation(accs[j][:, 0:width], G[(n0 + r + j) % 2][:, 0:width], ACT.Identity,
                                                 bias=cw[:, 3:4], scale=cw[:, 1:2]).then_inc(accr, 1)
                        act.wait_ge(ev, 2 * i + (n0 + r + 2))
                        nc.scalar.activation(accs[1][:, 0:width], accs[1][:, 0:width], ACT.Silu).then_inc(silud, 1)
                        act.wait_ge(prodd, i + (g0 + r // 2 + 1))
                        nc.scalar.activation(flat(gTv[:, 0, bass.ds(i + r // 2, 1), 0:width]), accs[0][:, 0:width],
                                             ACT.Copy).then_inc(ghi, 1)
                    pair(0, 0)
                    with act.Fori(0, KH - 2) as i:
                        pair(2, i)
                    pair(cnt - 2, 0, last=True)
                    for r in range(1, 8):
                        split_hi(l, down, r)
                    if hf == 0:
                        split_hi(l, "up1", 0)
            act.wait_ge(ev, seg_end[1, "down1"])
            norm(4, 1, 4, width=LAT)

        @block.vector
        def _(dve):
            chain = [0]

            def link(ins):
                chain[0] += 1
                ins.then_inc(dv, 1)
                dve.wait_ge(dv, chain[0])

            def norm(ni, nt):
                dve.wait_ge(srt, ni + 1)
                link(nc.vector.reciprocal(rsd[:, 8:8 + nt], rsd[:, 0:nt]))
                for t in range(nt):
                    ins = nc.vector.tensor_scalar(dg[:, t * P:(t + 1) * P], ident, rsd[:, 8 + t:9 + t], None, ALU.mult)
                ins.then_inc(dgd, 1)

            def operand(ni, w, gr):
                dve.wait_ge(rbd, ni + 1)
                for k in range(KD8):
                    if k >= 2:
                        dve.wait_ge(hlo, 8 * ni + k - 1)
                    tk = tm[:, (k % 2) * TOK:(k % 2 + 1) * TOK]
                    for g, (a, b) in enumerate(gr):
                        ins = nc.vector.scalar_tensor_tensor(tk[:, a:b], xT[:, k, a:b], Av[:, w, k, g:g + 1],
                                                             X0[:, a:b], ALU.mult, ALU.mult)
                    ins.then_inc(vsd, 1)
                    dve.wait_ge(hid, 8 * ni + k + 1)
                    for g, (a, b) in enumerate(gr):
                        ins = nc.vector.scalar_tensor_tensor(hTv[:, 1, k, a:b], tk[:, a:b],
                                                             mv[:, 24 * w + k, g:g + 1],
                                                             hTv[:, 0, k, a:b].bitcast(F32), ALU.add, ALU.subtract)
                    ins.then_inc(hlo, 1)

            def scales(l, w):
                gv = vecs(l, N1 if w == 0 else N2, 16).rearrange("p (k c) -> p k c", c=2)
                link(nc.vector.scalar_tensor_tensor(Av[:, w, :, :], mv[:, 24 * w + 8:24 * w + 16, :], 1.0, gv,
                                                    ALU.add, ALU.mult))

            def modulation(l, a, b):
                bm = vecs(l, BM, 96).rearrange("p (m c) -> p m c", c=2)
                dve.wait_ge(m_used, MODS * l + b)
                link(nc.vector.tensor_tensor(mv[:, a:b, :], M[:, MODS * l + a:MODS * l + b, :], bm[:, a:b, :], ALU.add))

            def residual(l, name, gate):
                n0, cnt, _, _ = seg_at[l, name]

                def add(r, i):
                    dve.wait_ge(used, 2 * i + (n0 + r + 1))
                    m = 2 * i + r
                    for g, (a, b) in enumerate(groups_of(l, name)):
                        xk = flat(xT[:, bass.ds(m, 1), a:b])
                        ga = mv[:, bass.ds(m + gate * 8, 1), g:g + 1].rearrange("p a c -> p (a c)")
                        ins = nc.vector.scalar_tensor_tensor(xk, G[(n0 + r) % 2][:, a:b], ga, xk, ALU.mult, ALU.add)
                    ins.then_inc(ev, 1)
                unit_loop(dve, l, name, add)

            nc.vector.memset(eps[:, :], EPS).then_inc(start_v, 1)
            dve.wait_ge(loaded, 96)
            lv = tm[:, 0:512].rearrange("p (a b c) -> p a b c", a=4, b=2)
            lp = tm[:, 512:768].rearrange("p (a c) -> p a c", a=4)
            link(nc.vector.tensor_tensor(lp, lv[:, :, 0, :], lv[:, :, 1, :], ALU.mult))
            link(nc.vector.reduce_sum(cst[:, 40:44], lp, AXX))
            for l in range(LAYERS):
                link(nc.vector.tensor_copy(cst[:, 70 + 10 * l:80 + 10 * l], vecs(l, DZ, 10)))
            z = cst[:, 70:90]
            link(nc.vector.tensor_scalar(cst[:, 50:70], z, -1.0, None, ALU.mult))
            link(nc.vector.tensor_scalar(lg[:, :], z, 0.0, None, ALU.min))
            nc.vector.tensor_tensor(cst[:, 0:20], z, cst[:, 50:70], ALU.max).then_inc(start_v, 1)
            dve.wait_ge(start_a, 2)
            dve.wait_ge(start_v, 2)
            nc.vector.tensor_scalar(cst[:, 70:90], cst[:, 20:40], 1.0, None, ALU.add).then_inc(start_v, 1)
            lam_init = [0.8 - 0.6 * math.exp(-0.3 * l) for l in range(LAYERS)]
            for l in range(LAYERS):
                link(nc.vector.tensor_tensor(nlam[:, l:l + 1], cst[:, 45 + 2 * l:46 + 2 * l],
                                             cst[:, 44 + 2 * l:45 + 2 * l], ALU.subtract))
                link(nc.vector.tensor_scalar(nlam[:, l:l + 1], nlam[:, l:l + 1], -lam_init[l], None, ALU.add))
            dve.wait_ge(start_a, 3)
            link(nc.vector.tensor_tensor(lg[:, :], lg[:, :], cst[:, 50:70], ALU.subtract))
            for l in range(LAYERS):
                o = L[l]
                nt = tiles_of(l)
                if l == 0:
                    modulation(0, 0, 16)
                else:
                    dve.wait_ge(ev, seg_end[0, "down1"])
                    modulation(1, 0, MODS)
                    scales(1, 1)
                scales(l, 0)
                norm(2 * l, 6)
                operand(2 * l, 0, [(0, LAT), (LAT, TOK)])
                for i, (t, w) in enumerate(ROPED):
                    if i == 0:
                        dve.wait_ge(ropeld, 16 * (l + 1))
                    dve.wait_ge(o.rot, i + 1)
                    if i >= 2:
                        dve.wait_ge(o.rdone, i - 1)
                    c = R_S64 if w == HD else R_S32
                    nc.vector.tensor_tensor(ropeA[i % 2], X0[:, 512 * (i % 2):512 * (i % 2) + LAT], rope[:, c:c + LAT],
                                            ALU.mult).then_inc(o.rsin, 1)
                    dve.wait_ge(o.rsin, i + 1)
                    dve.wait_ge(o.rcos, i + 1)
                    nc.vector.tensor_tensor(pT[:, t, 0:LAT], ropeA[i % 2], ropeB[i % 2], ALU.add).then_inc(o.rdone, 1)
                dve.wait_ge(tabs_a, 13 * (l + 1))
                link(nc.vector.tensor_scalar(kdec[:, :], kdec[:, :], CQ ** -0.5, None, ALU.mult))
                for h in range(4):
                    md = mdec[:, h * P:(h + 1) * P]
                    link(nc.vector.tensor_tensor(md, dexp[:, 2 * h, :], rope[:, R_MG:R_MG + P], ALU.mult))
                    link(nc.vector.tensor_tensor(dexp[:, 2 * h + 1, :], dexp[:, 2 * h + 1, :],
                                                 rope[:, R_ML:R_ML + P], ALU.mult))
                    link(nc.vector.tensor_tensor(md, md, dexp[:, 2 * h + 1, :], ALU.add))
                link(nc.vector.memset(fsc[:, :], 1.0))
                link(nc.vector.tensor_scalar(fsc[:, 2:6], vecs(l, SG, 1).to_broadcast([P, 4]),
                                             1.0 - lam_init[l], None, ALU.mult))
                nc.vector.tensor_copy(cst[:, 95:96], eps[:, :]).then_inc(o.tab, 1)
                steps = attention_steps(l)
                groups, ends = turn_groups(steps)
                for s in range(len(steps) + 1):
                    if s < len(steps):
                        kind, h, q, spans, keys = steps[s]
                        p, nk = s % 2, P * len(keys)
                        if kind == "A" and s >= 2:
                            dve.wait_ge(o.tr, ends[s - 2])
                        if kind == "A" and len(spans) == 2:
                            off = K_BAND + (P if q == 0 else 0)
                            for c in range(2):
                                dve.wait_ge(o.sc[c], s + 1)
                                w = spans[0][2]
                                link(nc.vector.tensor_tensor(Pb[p][c][:, 0:w], G[c][:, 0:w], kc[:, off:off + w],
                                                             ALU.add))
                        for c in range(2):
                            m = 2 * s + c
                            if kind == "B":
                                dve.wait_ge(o.sc[c], s + 1)
                                link(nc.vector.reduce_max(MX[:, m:m + 1], G[c][:, 0:nk], AXX))
                                nc.vector.tensor_scalar(NB[:, m:m + 1], MX[:, m:m + 1], -SCALE, None,
                                                        ALU.mult).then_inc(o.nb[c], 1)
                            else:
                                dve.wait_ge(o.cx[c], s + 1 - NB_STEPS[l])
                                link(nc.vector.reduce_max(MX[:, m:m + 1], Pb[p][c][:, 0:nk], AXX))
                                link(nc.vector.tensor_scalar(PR[:, m:m + 1], MX[:, m:m + 1], SCALE,
                                                             vecs(l, SK + 2 * h + c, 1), ALU.mult, ALU.max))
                                nc.vector.tensor_scalar(NB[:, m:m + 1], PR[:, m:m + 1], -1.0, None,
                                                        ALU.mult).then_inc(o.nb[c], 1)
                    if s >= 1:
                        kind, h, q, spans, keys = steps[s - 1]
                        p, nk, m, t = (s - 1) % 2, P * len(keys), 2 * (s - 1), ends[s - 1] - 1
                        if kind == "B":
                            dve.wait_ge(o.ex[0], s)
                            dve.wait_ge(o.ex[1], s)
                            link(nc.vector.reciprocal(ES[:, m:m + 1], LS[:, m + 1:m + 2]))
                            link(nc.vector.reciprocal(RI[:, t:t + 1], LS[:, m:m + 1]))
                            link(nc.vector.scalar_tensor_tensor(PR[:, m:m + 1], ES[:, m:m + 1], LS[:, m:m + 1],
                                                                nlam[:, l:l + 1], ALU.mult, ALU.mult))
                            nc.vector.scalar_tensor_tensor(Pb[p][0][:, 0:nk], Pb[p][1][:, 0:nk], PR[:, m:m + 1],
                                                           Pb[p][0][:, 0:nk], ALU.mult, ALU.add).then_inc(o.wr, 1)
                        else:
                            for c in range(2):
                                dve.wait_ge(o.es[c], s - NB_STEPS[l])
                                link(nc.vector.tensor_tensor(MX[:, m + c:m + c + 1], LS[:, m + c:m + c + 1],
                                                             ES[:, m + c:m + c + 1], ALU.add))
                                nc.vector.reciprocal(RI[:, t - 1 + c:t + c],
                                                     MX[:, m + c:m + c + 1]).then_inc(o.wr, 1)
                dve.wait_ge(o.kt, 1)
                dve.wait_ge(o.oe, len(groups))
                for d in range(2):
                    kb = kdec[:, 4 * d:4 * d + 4].unsqueeze(1).unsqueeze(3).to_broadcast([P, 6, 4, CQ])
                    nc.vector.tensor_tensor(kdk[:, d].rearrange("p n (h e) -> p n h e", h=4),
                                            G[0][:, 0:TOK].rearrange("p (n h e) -> p n h e", n=6, h=4),
                                            kb, ALU.mult).then_inc(o.kd, 1)
                for i, (d, n, to, prev) in enumerate(STATE_CHAIN):
                    dve.wait_ge(o.kv, i + 1)
                    dst = states[:, d, to, :] if prev is None else tm[:, 256 * (i % 2):256 * (i % 2) + 256]
                    src = (G[1] if i % 4 < 2 else X0)[:, 512 * (i % 2):512 * (i % 2) + 256]
                    if prev is not None:
                        link(nc.vector.tensor_tensor(dst, src, kc[:, K_BD:K_BD + 256], ALU.mult))
                        nc.vector.scalar_tensor_tensor(states[:, d, to, :], states[:, d, prev, :], gch[:, d:d + 1],
                                                       dst, ALU.mult, ALU.add).then_inc(o.st, 1)
                    else:
                        nc.vector.tensor_tensor(dst, src, kc[:, K_BD:K_BD + 256], ALU.mult).then_inc(o.st, 1)
                    dve.wait_ge(o.st, i + 1)
                for j in range(nt):
                    dve.wait_ge(o.at, j + 1)
                    if j >= 2:
                        dve.wait_ge(o.y, j - 1)
                    nc.vector.tensor_tensor(tm[:, 1024 + 512 * (j % 2):1536 + 512 * (j % 2)],
                                            X0[:, 512 * (j % 2):512 * (j % 2) + 512], mdec[:, :],
                                            ALU.mult).then_inc(o.ad, 1)
                dve.wait_ge(o.yc, nt)
                yg = ysb[:, 0:nt, :].rearrange("p n (h e) -> p (n h) e", h=4)
                yq = ysq[:, 0:nt, :].rearrange("p n (h e) -> p (n h) e", h=4)
                link(nc.vector.reduce_sum(cst[:, 48:48 + 4 * nt], yg, AXX))
                link(nc.vector.tensor_scalar(cst[:, 48:48 + 4 * nt], cst[:, 48:48 + 4 * nt], 1.0 / 64, None, ALU.mult))
                nc.vector.tensor_tensor(yg, yg, cst[:, 48:48 + 4 * nt].unsqueeze(2).to_broadcast([P, 4 * nt, 64]),
                                        ALU.subtract).then_inc(o.mixed, 1)
                dve.wait_ge(o.mixed, 1)
                dve.wait_ge(o.ga, 1)
                nc.vector.reduce_sum(cst[:, 72:72 + 4 * nt], yq, AXX).then_inc(o.mixed, 1)
                dve.wait_ge(o.ga, 3)
                link(nc.vector.reciprocal(ssb[:, 0:4 * nt], cst[:, 0:4 * nt]))
                mb = mix[:, 0:nt, 256:768].rearrange("p n (h e) -> p n h e", h=4)
                rb = ssb[:, 0:4 * nt].rearrange("p (n h) -> p n h", h=4).unsqueeze(3).to_broadcast([P, nt, 4, P])
                nc.vector.tensor_tensor(mb, mb, rb, ALU.mult).then_inc(o.mixed, 1)
                dve.wait_ge(o.ga, 4)
                dve.wait_ge(o.mixed, 3)
                link(nc.vector.reciprocal(cst[:, 48:48 + 4 * nt], cst[:, 24:24 + 4 * nt]))
                link(nc.vector.tensor_tensor(yg, yg, cst[:, 48:48 + 4 * nt].unsqueeze(2).to_broadcast([P, 4 * nt, 64]),
                                             ALU.mult))
                nc.vector.tensor_tensor(mix[:, 0:nt, 768:1024], ysb[:, 0:nt, :], sgr[:, 0:nt, :],
                                        ALU.mult).then_inc(o.mixed, 1)
                for f in range(KD8):
                    dve.wait_ge(o.mh, f + 1)
                    nc.vector.scalar_tensor_tensor(hTv[:, 1, f, 0:nt * P], G[f % 2][:, 0:nt * P], fsc[:, f:f + 1],
                                                   hTv[:, 0, f, 0:nt * P].bitcast(F32), ALU.mult,
                                                   ALU.subtract).then_inc(o.ml, 1)
                if l == 0:
                    modulation(0, 16, MODS)
                    scales(0, 1)
                residual(l, "out", 2)
                dve.wait_ge(ev, seg_end[l, "out"])
                norm(2 * l + 1, nt)
                gr = groups_of(l, "up0")
                operand(2 * l + 1, 1, gr)
                width = gr[-1][1]
                accs = (tm[:, 0:TOK], tm[:, TOK:2 * TOK])
                for hf in range(2):
                    n0 = seg_at[l, f"up{hf}"][0]
                    g0 = (2 * l + hf) * KH
                    with dve.Fori(0, KH) as i:
                        for j in range(2):
                            u0 = 2 * g0 + j
                            dve.wait_ge(accr, 2 * i + (u0 + 1))
                            cw = vecs(l, CW, 176).rearrange("p (u w) -> p u w", w=4)[
                                :, bass.ds(2 * i + (hf * 22 + j), 1), :].rearrange("p a w -> p (a w)")
                            src = G[(n0 + j) % 2]
                            for a, b in gr:
                                ins = nc.vector.scalar_tensor_tensor(accs[j][:, a + 1:b], src[:, a:b - 1], cw[:, 0:1],
                                                                     accs[j][:, a + 1:b], ALU.mult, ALU.add)
                            ins.then_inc(convl, 1)
                            dve.wait_ge(convl, 2 * i + (u0 + 1))
                            for a, b in gr:
                                ins = nc.vector.scalar_tensor_tensor(accs[j][:, a:b - 1], src[:, a + 1:b], cw[:, 2:3],
                                                                     accs[j][:, a:b - 1], ALU.mult, ALU.add)
                            ins.then_inc(ev, 1)
                        dve.wait_ge(silud, i + (g0 + 1))
                        nc.vector.tensor_tensor(accs[0][:, 0:width], accs[0][:, 0:width], accs[1][:, 0:width],
                                                ALU.mult).then_inc(prodd, 1)
                        dve.wait_ge(ghi, i + (g0 + 1))
                        nc.vector.tensor_tensor(flat(gTv[:, 1, bass.ds(i, 1), 0:width]), accs[0][:, 0:width],
                                                flat(gTv[:, 0, bass.ds(i, 1), 0:width]).bitcast(F32),
                                                ALU.subtract).then_inc(glo, 1)
                    residual(l, f"down{hf}", 5)
            dve.wait_ge(ev, seg_end[1, "down1"])
            norm(4, 4)
            dve.wait_ge(rbd, 5)
            for k in range(KD8):
                nc.vector.scalar_tensor_tensor(pT[:, 8 + k, 0:LAT], xT[:, k, 0:LAT], fing[:, k:k + 1], X0[:, 0:LAT],
                                               ALU.mult, ALU.mult).then_inc(fin, 1)

        @block.tensor
        def _(pe):
            def mod(m, i=0):
                pe.wait_ge(m_landed[m % 2], 16 * i + 16 * (m // 2 + 1))
                o = M[:, m, :] if isinstance(i, int) else M[:, bass.ds(2 * i + m, 1), :].rearrange("p a c -> p (a c)")
                for k in range(KD8):
                    ins = nc.tensor.matmul(o, mrv[m % 2][:, k, :], csv[:, k, :], start=(k == 0), stop=(k == KD8 - 1))
                ins.then_inc(m_used, 1)

            def norm(ni, nt):
                pe.wait_ge(sqd, 8 * ni + 8)
                for t in range(nt):
                    for k in range(KD8):
                        ins = nc.tensor.matmul(X1[:, t:t + 1], pT[:, k, t * P:(t + 1) * P], ones[:, 0:1],
                                               start=(k == 0), stop=(k == KD8 - 1))
                ins.then_inc(ssd, 1)
                pe.wait_ge(dgd, ni + 1)
                for t in range(nt):
                    ins = nc.tensor.matmul(X0[:, t * P:(t + 1) * P], ones, dg[:, t * P:(t + 1) * P],
                                           start=True, stop=True)
                ins.then_inc(rbd, 1)

            def multiply(l, name, r, i, rhs):
                n0, cnt, k, _ = seg_at[l, name]
                n = n0 + r
                pe.wait_ge(w_lo, 2 * i + (n + 1))
                if n >= 2:
                    pe.wait_ge(ev, 2 * i + (n - 1))
                gr = groups_of(l, name)
                for kk in range(k):
                    for pi, (ws, xs) in enumerate(((0, 0), (0, 1), (1, 0))):
                        for a, b in gr:
                            ins = nc.tensor.matmul(G[n % 2][:, a:b], Wv[n % 2][ws][:, kk, :], rhs[:, xs, kk, a:b],
                                                   start=(kk == 0 and pi == 0), stop=(kk == k - 1 and pi == 2))
                ins.then_inc(used, 1)

            def segment(l, name, rhs):
                unit_loop(pe, l, name, lambda r, i: multiply(l, name, r, i, rhs),
                          head=2 if seg_at[l, name][0] == 0 else 0)

            pe.wait_ge(loaded, 96)
            pe.wait_ge(c_ready, 1)
            for m in range(16):
                mod(m)
            for l in range(LAYERS):
                o = L[l]
                nt = tiles_of(l)
                norm(2 * l, 6)
                pe.wait_ge(hlo, 16 * l + 8)
                segment(l, "in_kv", hTv)
                segment(l, "in_q", hTv)
                pe.wait_ge(ev, seg_end[l, "in_q"])
                for i in range(len(ROPED)):
                    t, w = ROPED[i]
                    if i >= 2:
                        pe.wait_ge(o.rsin, i - 1)
                    sw = K_S64 if w == HD else K_S32
                    nc.tensor.matmul(X0[:, 512 * (i % 2):512 * (i % 2) + LAT], kc[:, sw:sw + P], pT[:, t, 0:LAT],
                                     start=True, stop=True).then_inc(o.rot, 1)
                    if i < 9:
                        if i >= 2:
                            pe.wait_ge(o.vc, i - 1)
                        for t in range(6 if i < 7 else nt):
                            ins = nc.tensor.transpose(G[i % 2][:, t * P:(t + 1) * P], pT[:, T_VA + i, t * P:(t + 1) * P],
                                                      ident)
                        ins.then_inc(o.vt, 1)
                steps = attention_steps(l)
                groups, ends = turn_groups(steps)

                def mix_values(t):
                    s, c, vcol, w, _ = groups[t]
                    keys = steps[s][4]
                    pe.wait_ge(o.te, t + 1)
                    if t >= 1:
                        pe.wait_ge(o.oe, t)
                    for i, kt in enumerate(keys):
                        ins = nc.tensor.matmul(X1[:, 0:w], WT[t % 2][:, i * P:(i + 1) * P], vt[:, kt, vcol:vcol + w],
                                               start=(i == 0), stop=(i == len(keys) - 1))
                    ins.then_inc(o.pv, 1)

                pe.wait_ge(o.rdone, len(ROPED))
                pe.wait_ge(o.vc, 9)
                for s in range(len(steps) + 1):
                    if s < len(steps):
                        kind, h, q, spans, keys = steps[s]
                        for c in range(2):
                            if s >= 1:
                                pe.wait_ge(o.ex[c], s)
                            b0 = HD * (c if kind == "B" else h)
                            tq, tk = (T_QB + h, T_KB + h) if kind == "B" else (T_QA + c, T_KA)
                            for sc0, k0, w in spans:
                                ins = nc.tensor.matmul(G[c][:, sc0:sc0 + w], pT[b0:b0 + HD, tq, q * P:(q + 1) * P],
                                                       pT[b0:b0 + HD, tk, k0:k0 + w], start=True, stop=True)
                            ins.then_inc(o.sc[c], 1)
                        if l == 0 and s < MODS - 16:
                            mod(16 + s)
                    if s >= 1:
                        for t in range(ends[s - 2] if s >= 2 else 0, ends[s - 1]):
                            _, c, _, _, _ = groups[t]
                            pe.wait_ge(o.wr, t + 1)
                            if t >= 1:
                                pe.wait_ge(o.te, t)
                            for i in range(len(steps[s - 1][4])):
                                ins = nc.tensor.transpose(X0[:, i * P:(i + 1) * P],
                                                          Pb[(s - 1) % 2][c][:, i * P:(i + 1) * P], ident)
                            ins.then_inc(o.tr, 1)
                            if t >= 1:
                                mix_values(t - 1)
                mix_values(len(groups) - 1)
                for n in range(6):
                    ins = nc.tensor.transpose(G[0][:, n * P:(n + 1) * P], pT[:, T_KR, n * P:(n + 1) * P], ident)
                ins.then_inc(o.kt, 1)
                pe.wait_ge(o.kd, 2)
                for i, (d, n, to, prev) in enumerate(STATE_CHAIN):
                    if i >= 4:
                        pe.wait_ge(o.st, i - 3)
                    nc.tensor.matmul((G[1] if i % 4 < 2 else X0)[:, 512 * (i % 2):512 * (i % 2) + 256],
                                     kdk[:, d, n, :], vt[:, n, V_C:V_C + 256], start=True, stop=True).then_inc(o.kv, 1)
                pe.wait_ge(o.st, len(STATE_CHAIN))

                def ret_scores(j):
                    if j >= 2:
                        pe.wait_ge(o.ad, j - 1)
                    pe.wait_ge(o.qd, 3 * j + 3)
                    nc.tensor.matmul(X0[:, 512 * (j % 2):512 * (j % 2) + 512], pT[:, T_KR, j * P:(j + 1) * P],
                                     tm[:, 2048 + 512 * (j % 2):2560 + 512 * (j % 2)],
                                     start=True, stop=True).then_inc(o.at, 1)

                ret_scores(0)
                for j in range(nt):
                    if j + 1 < nt:
                        ret_scores(j + 1)
                    if j >= 2:
                        pe.wait_ge(o.yc, j - 1)
                    y = G[1][:, 512 * (j % 2):512 * (j % 2) + 256]
                    dirs = [d for d in range(2) if j != 4 + d]
                    for d in dirs:
                        nc.tensor.matmul(y, tm[:, 512 + 256 * (j % 2) + P * d:][:, 0:P], states[:, d, j, :],
                                         start=(d == dirs[0]), stop=False)
                    pe.wait_ge(o.ad, j + 1)
                    for h in range(4):
                        ins = nc.tensor.matmul(y[:, 64 * h:64 * h + 64], tm[:, 1024 + 512 * (j % 2) + h * P:][:, 0:P],
                                               vt[:, j, V_C + 64 * h:V_C + 64 * h + 64], start=False, stop=(h == 3))
                    ins.then_inc(o.y, 1)
                pe.wait_ge(o.mixed, 4)
                for f in range(KD8):
                    if f >= 2:
                        pe.wait_ge(o.ml, f - 1)
                    for t in range(nt):
                        ins = nc.tensor.transpose(G[f % 2][:, t * P:(t + 1) * P], mix[:, t, f * P:(f + 1) * P], ident)
                    ins.then_inc(o.mt, 1)
                pe.wait_ge(o.ml, KD8)
                segment(l, "out", hTv)
                norm(2 * l + 1, nt)
                pe.wait_ge(hlo, 16 * l + 16)
                for hf in range(2):
                    if l == 0:
                        with pe.Fori(0, KH) as i:
                            multiply(l, f"up{hf}", 0, i, hTv)
                            multiply(l, f"up{hf}", 1, i, hTv)
                            mod(MODS + 22 * hf, i)
                            mod(MODS + 22 * hf + 1, i)
                    else:
                        segment(l, f"up{hf}", hTv)
                    pe.wait_ge(glo, (2 * l + hf + 1) * KH)
                    segment(l, f"down{hf}", gTv)
                if l == 0:
                    for m in range(MODS + 44, 2 * MODS):
                        mod(m)
            norm(4, 4)


ROPED = ([(T_KA, HD)] + [(T_KB + h, HD) for h in range(4)] + [(T_KR, CQ)]
         + [(T_QA, HD), (T_QA + 1, HD)] + [(T_QB + h, HD) for h in range(4)] + [(T_QR, CQ)])
NB_STEPS = [24, 16]
_F, _B = [4, 5, 0, 1, 2, 3], [5, 4, 3, 2, 1, 0]
STATE_CHAIN = []
for _i in range(5):
    STATE_CHAIN.append((0, _F[_i], _F[_i + 1], _F[_i] if _i else None))
    STATE_CHAIN.append((1, _B[_i], _B[_i + 1], _B[_i] if _i else None))


def kernel(**inputs):
    import numpy as _np
    import concourse.bacc as _bacc
    from concourse import mybir as _mybir
    from concourse.bass_utils import run_bass_kernel_spmd as _run

    a = {k: _np.asarray(v) for k, v in inputs.items()}
    cc = _np.concatenate
    xc = cc([a["x"][0], a["ctx"][0]], 0)
    xin = xc.T.reshape(8, 128, 768).transpose(1, 0, 2).reshape(128, -1)
    cin = _np.stack([a["c"][0], a["c_ctx"]], -1).reshape(8, 128, 2).transpose(1, 0, 2).reshape(128, -1)

    def unit(w, rows, cols):
        return w[rows][:, cols].reshape(-1, 128, 128).transpose(1, 0, 2).reshape(128, -1)

    A, dk = _np.arange, 64
    qa = cc([A(0, 64), A(128, 192), A(64, 128), A(192, 256)])
    cols = cc([A(256, 384), A(1024, 1536), A(2176, 2304), A(384, 512), A(1536, 2048), A(2304, 2560),
               A(2560, 2816), qa, A(512, 1024), A(2048, 2176)])
    k8, k11, wm, vin = [], [], [], []
    for l in range(LAYERS):
        full = slice(None)
        k8 += [unit(a["w_in"][l], full, cols[128 * t:128 * t + 128]) for t in range(N_IN)]
        k8 += [unit(a["w_out"][l], full, slice(128 * m, 128 * m + 128)) for m in range(8)]
        order = [s * 22 + j for j in range(22) for s in range(2)]
        k8 += [unit(a["w_up"][l], full, slice(128 * u, 128 * u + 128)) for u in order]
        for hf in range(2):
            rows = slice(KH * 128 * hf, KH * 128 * (hf + 1))
            k11 += [unit(a["w_down"][l], rows, slice(128 * m, 128 * m + 128)) for m in range(8)]
        wm += [unit(a["w_mod"][l], full, slice(128 * m, 128 * m + 128)) for m in range(MODS)]

        def fm(v):
            return v.reshape(-1, 128).T

        conv = _np.stack([fm(a["conv_w"][l, 0]), fm(a["conv_w"][l, 1]), fm(a["conv_w"][l, 2]),
                          fm(a["conv_b"][l])], -1)[:, order].reshape(128, -1)
        z = a["ret_decay_logit"][l]
        vin += [_np.repeat(fm(a["b_mod"][l]), 2, 1), _np.repeat(fm(a["norm1_g"][l]), 2, 1),
                _np.repeat(fm(a["norm2_g"][l]), 2, 1), conv, a["diff_subln_g"][l][:, None],
                _np.broadcast_to(a["attn_sink"][l][None], (128, 4)),
                _np.broadcast_to(z.reshape(1, 8), (128, 8)), _np.repeat(z.T, 32, 0)]
    kin, rin = constants()
    arrays = {
        "x": xin, "c": cin, "wk8": _np.stack(k8), "wk11": _np.stack(k11), "wmod": _np.stack(wm),
        "vec": cc(vin, 1), "final_g": a["final_g"].reshape(8, 128).T,
        "lam": _np.broadcast_to(a["diff_lambda"].reshape(1, -1), (128, 512)), "consts": kin, "rope": rin,
    }
    arrays = {k: _np.ascontiguousarray(v) for k, v in arrays.items()}
    nc = _bacc.Bacc("TRN2", target_bir_lowering=False, num_devices=1)
    args = [nc.dram_tensor(f"in_{k}", v.shape, _mybir.dt.from_np(v.dtype), kind="ExternalInput").ap()
            for k, v in arrays.items()]
    args.append(nc.dram_tensor("out", (128, 8, 512), _mybir.dt.float32, kind="ExternalOutput").ap())
    trunk(nc, *args)
    r = _run(nc, [{f"in_{k}": v for k, v in arrays.items()}], core_ids=[0])
    return r.results[0]["out"].transpose(2, 1, 0).reshape(1, 512, 1024)
```

```python
from contextlib import ExitStack
import math

import numpy as np

import concourse.bass as bass
from concourse import mybir

F32 = mybir.dt.float32
F32R = mybir.dt.float32r
ACT = mybir.ActivationFunctionType
ALU = mybir.AluOpType
AXX = mybir.AxisListType.X

P = 128
D, KD8, LAT, CTX, LAYERS = 1024, 8, 512, 256, 2
TOK = LAT + CTX
EPS = 1e-6
GRID_W, ROPE_BASE = 64, 10000.0
FF, KH = 2816, 11
HD = 64
SCALE = HD ** -0.5
CQ = 32
T_KA, T_KB, T_KR, T_VA, T_GR, T_QA, T_QB, T_QR, N_IN = 0, 1, 5, 6, 13, 15, 17, 21, 22
N_KV = 13
V_A, V_B, V_C, V_G, V_W = 0, 128, 640, 896, 1152
SEGS = [("in_kv", N_KV, 8), ("in_q", N_IN - N_KV, 8), ("out", 8, 8),
        ("up0", 22, 8), ("down0", 8, KH), ("up1", 22, 8), ("down1", 8, KH)]
PER_LAYER = sum(n for _, n, _ in SEGS)
MODS = 48
BM, N1, N2, CW, SG, SK, DZ, VL = 0, 96, 112, 128, 304, 305, 309, 319
K_ID, K_S64, K_S32, K_ONE, K_BAND, K_BD, K_KJ, K_SC, K_W = 0, 128, 256, 384, 512, 896, 1152, 1154, 1163
R_C64, R_S64, R_C32, R_S32, R_C1, R_C2, R_DP, R_DN, R_MG, R_ML, R_W = (
    0, 512, 1024, 1536, 2048, 2176, 2304, 2432, 2560, 2688, 2816)


def constants():
    k = np.zeros((P, K_W), np.float32)
    i = np.arange(P)
    k[:, K_ID:K_ID + P] = np.eye(P)
    k[i, K_S64 + (i ^ 32)] = 1
    k[i, K_S32 + (i ^ 16)] = 1
    k[:, K_ONE:K_ONE + P] = 1
    k[:, K_BAND:K_BAND + P] = np.where(i[None] >= i[:, None], 0, -1e30)
    k[:, K_BAND + 2 * P:K_BAND + 3 * P] = np.where(i[None] <= i[:, None], 0, -1e30)
    k[:, K_BD:K_BD + 256] = (i[:, None] // CQ) == (np.arange(256)[None] // 64)
    k[:, K_KJ], k[:, K_KJ + 1] = P - 1 - i, i
    for t in range(N_KV, N_IN):
        k[:, K_SC + t - N_KV] = SCALE if t in ATTN_SCALED else 1
    r = np.zeros((P, R_W), np.float32)
    rows = np.repeat(np.arange(LAT // GRID_W, dtype=np.float32), GRID_W)
    cols = np.tile(np.arange(GRID_W, dtype=np.float32), LAT // GRID_W)
    for dim, c, s in ((HD, R_C64, R_S64), (CQ, R_C32, R_S32)):
        nf = dim // 4
        inv = (np.float32(ROPE_BASE) ** (-np.arange(nf, dtype=np.float32) / np.float32(nf))).astype(np.float32)
        ang = np.concatenate([rows[:, None] * inv, cols[:, None] * inv], -1).T.astype(np.float32)
        f = i % (dim // 2)
        r[:, c:c + LAT] = np.cos(ang)[f]
        r[:, s:s + LAT] = np.where((i % dim < dim // 2)[:, None], -np.sin(ang)[f], np.sin(ang)[f])
    r[:, R_C1:R_C1 + P] = i[None] + 1
    r[:, R_C2:R_C2 + P] = P - i[None]
    d = i[None] - i[:, None]
    r[:, R_DP:R_DP + P] = np.maximum(d, 0)
    r[:, R_DN:R_DN + P] = np.maximum(-d, 0)
    r[:, R_MG:R_MG + P] = (d >= 0) * np.float32(CQ ** -0.5)
    r[:, R_ML:R_ML + P] = (d < 0) * np.float32(CQ ** -0.5)
    return k, r


def attention_steps(l):
    long, short = [], []
    for h in range(4):
        long += [("B", h, q, [(0, 0, LAT, None), (LAT, LAT, CTX, None)], [0, 1, 2, 3, 4, 5]) for q in range(4)]
        if l == 0:
            short += [("B", h, q, [(0, LAT, CTX, None)], [4, 5]) for q in (4, 5)]
    for g in range(2):
        for q in range(4):
            near = list(range(max(0, q - 1), min(3, q + 1) + 1))
            spans = [(0, LAT, CTX, None)]
            for i, kt in enumerate(near):
                spans.append((CTX + i * P, kt * P, P, None if kt == q else K_BAND + (kt - q + 1) * P))
            short.append(("A", g, q, spans, [4, 5] + near))
    if l == 0:
        short += [("A", g, q, [(0, LAT, CTX, None)], [4, 5]) for g in range(2) for q in (4, 5)]
    steps, late = [], 4 if l == 0 else 3
    mixed = short[:-late]
    for i, step in enumerate(long):
        steps.append(step)
        while mixed and (len(short) - late - len(mixed) + 1) * len(long) <= (i + 1) * (len(short) - late):
            steps.append(mixed.pop(0))
    return steps + short[-late:]


def turn_groups(steps):
    groups, ends = [], []
    for s, (kind, h, *_) in enumerate(steps):
        if kind == "B":
            groups.append((s, 0, V_B + P * h, P, 256 + P * h))
        else:
            groups += [(s, c, V_A + HD * h, HD, HD * (2 * h + c)) for c in range(2)]
        ends.append(len(groups))
    return groups, ends


def trunk(nc, xin, cin, cbin, wk8, wk11, wmod, vin, finalg, lamin, kin, rin, out):
    base, seg_at, n, a8, a11 = {}, {}, 0, 0, 0
    for l in range(LAYERS):
        for name, cnt, k in SEGS:
            seg_at[l, name] = (n, cnt, k, a8 if k == 8 else a11)
            n += cnt
            if k == 8:
                a8 += cnt
            else:
                a11 += cnt
    seg_end = {key: v[0] + v[1] for key, v in seg_at.items()}

    def groups_of(l, name):
        return [(0, LAT), (LAT, TOK)] if l == 0 or name == "in_kv" else [(0, LAT)]

    def tiles_of(l):
        return 6 if l == 0 else 4

    stack = ExitStack()
    with stack:
        def sb(name, cols, dt=F32, rows=P):
            return stack.enter_context(nc.sbuf_tensor(name, [rows, cols], dt))

        xT = sb("xT", KD8 * TOK)[:, :].rearrange("p (k t) -> p k t", k=KD8)
        with ExitStack() as own:
            hT = own.enter_context(nc.sbuf_tensor("hT", [P, 2 * KD8 * TOK], F32R))
        with ExitStack() as own:
            vtok = own.enter_context(nc.sbuf_tensor("vtok", [P, 6 * V_W], F32))
            hm = own.enter_context(nc.sbuf_tensor("attn_scratch", [P, 2 * KD8 * TOK - 6 * V_W], F32))
        hold = sb("hT_bytes", 2 * KD8 * TOK)
        with ExitStack() as own:
            gT = own.enter_context(nc.sbuf_tensor("gT", [P, 2 * KH * TOK], F32R))
        pTt = sb("pT", N_IN * TOK)
        raw = [sb(f"raw{j}", KH * P) for j in range(2)]
        wsp = [sb(f"wsplit{j}", 2 * KH * P, F32R) for j in range(2)]
        tm = sb("tmp", 2 * TOK + 2 * D)
        mraw = [sb(f"modraw{j}", KD8 * P) for j in range(2)]
        kc = sb("consts", K_W)
        vec = sb("vec", LAYERS * VL)
        fing = sb("fing", KD8)
        cs = sb("c_in", 16)
        csil = sb("c_silu", 16)
        modv = sb("modv", 2 * 96)
        msum = sb("mod_sums", 2 * 96)
        Amul = sb("Amul", 64)
        qdec = sb("qdec", 256)
        mdec = sb("mdec", 512)
        kdec = sb("kdec", 8)
        gch = sb("gch", 2)
        lg = sb("lg", 20)
        sm = sb("small", 4 * 72)
        nsink = sb("minus_sink", 8)
        nlam = sb("nlam", 2)
        fsc = sb("fsc", 8)
        rsd = sb("rsd", 16)
        ssb = sb("ssb", 24)
        cst = sb("cstat", 96)
        half = sb("minus_half", 24)
        dummy = sb("warm", 5)
        eps = sb("eps", 1)
        G = [stack.enter_context(nc.psum_tensor(f"G{j}", [P, 1024], F32)) for j in range(2)]
        X0 = stack.enter_context(nc.psum_tensor("X0", [P, 1024], F32))
        X1 = stack.enter_context(nc.psum_tensor("X1", [P, 1024], F32))
        hTv = hT[:, :].rearrange("p (s k t) -> p s k t", s=2, k=KD8)
        gTv = gT[:, :].rearrange("p (s k t) -> p s k t", s=2, k=KH)
        pT = pTt[:, :].rearrange("p (k t) -> p k t", k=N_IN)
        mix = pTt[:, T_VA * TOK:T_VA * TOK + 6 * D].rearrange("p (t f) -> p t f", t=6)
        ysb = mix[:, :, 768:1024].rearrange("p n (h e) -> p n h e", h=4)
        ysq = tm[:, 0:1536].rearrange("p (n h e) -> p n h e", n=6, h=4)
        vt = vtok[:, :].rearrange("p (t f) -> p t f", t=6)
        Pb = [[hm[:, (2 * p + c) * TOK:(2 * p + c + 1) * TOK] for c in range(2)] for p in range(2)]
        WT = [hm[:, (4 + p) * TOK:(5 + p) * TOK] for p in range(2)]
        ropeA = [hm[:, j * LAT:(j + 1) * LAT] for j in range(2)]
        ropeB = [hm[:, (2 + j) * LAT:(3 + j) * LAT] for j in range(2)]
        dexp = hm[:, 2048:3072].rearrange("p (e c) -> p e c", e=8)
        states = hm[:, 0:3072].rearrange("p (d n e) -> p d n e", d=2, n=6)
        kdk = hm[:, 3072:4608].rearrange("p (d n e) -> p d n e", d=2, n=6)
        Wv = [[wsp[j][:, s * KH * P:(s + 1) * KH * P].rearrange("p (k m) -> p k m", k=KH) for s in range(2)]
              for j in range(2)]
        first_mod = pTt[:, 0:16 * D].rearrange("p (m c) -> p m c", m=16)
        cb = tm[:, 2 * TOK:2 * TOK + 2 * D].rearrange("p (c k) -> p c k", c=2)
        sq, sacc = tm[:, 0:TOK], tm[:, TOK:2 * TOK]
        msv = msum[:, :].rearrange("p (m c) -> p m c", c=2)
        csv = csil[:, :].rearrange("p (k c) -> p k c", k=KD8)
        mvl = [modv[:, 96 * l:96 * l + 96].rearrange("p (m c) -> p m c", c=2) for l in range(LAYERS)]
        Avl = [Amul[:, 32 * l:32 * l + 32].rearrange("p (w k c) -> p w k c", w=2, k=KD8) for l in range(LAYERS)]
        rope = tm[:, 0:R_W]
        ident, ones = kc[:, K_ID:K_ID + P], kc[:, K_ONE:K_ONE + P]
        dg = pTt[:, (N_IN - 1) * TOK:N_IN * TOK]
        NB, LS, RC, ES = (sm[:, 72 * j:72 * j + 72] for j in range(4))

        order = [(l, name) for l in range(LAYERS) for name, _, _ in SEGS]
        FMT = [2, 3, 4, 5, 6, 7, 0, 1]

        def vecs(l, a, w):
            return vec[:, l * VL + a:l * VL + a + w]

        def sem(name):
            return stack.enter_context(nc.semaphore(name))

        c_landed, v_landed, x_landed = sem("c_landed"), sem("vectors_landed"), sem("x_landed")
        ropeld = sem("rope_tables_loaded")
        w_landed = [sem(f"weights_landed{j}") for j in range(2)]
        w_hi, w_lo = sem("weights_hi"), sem("weights_lo")
        used = sem("unit_multiplied")
        ev = sem("unit_evacuated")
        m_landed = [sem(f"mod_landed{j}") for j in range(2)]
        m_first = [sem(f"first_mod_landed{j}") for j in range(8)]
        m_used = sem("mod_unit_multiplied")
        m_pe, m_dv = sem("first_shift_multiplied"), sem("first_scale_multiplied")
        c_ready = sem("c_silu_ready")
        cb_ready = sem("c_silu_spread")
        cb_landed = sem("c_spread_landed")
        modok = sem("modulation_ready")
        sqd, sqa, ssd, srt, dgd, rbd = (sem(x) for x in (
            "squares_ready", "squares_added", "sums_ready", "roots_ready", "diag_ready", "rstd_spread"))
        vsd, hid, hlo = sem("scaled_ready"), sem("operand_hi"), sem("operand_lo")
        accr = sem("conv_centre_ready")
        convl = sem("conv_left_added")
        silud, prodd, ghi, glo = sem("gate_silu"), sem("gated"), sem("gated_hi"), sem("gated_lo")
        dv = sem("vector_chain")
        tabs_a = sem("table_exps")
        start_a = sem("start_act")
        start_v = sem("start_vec")
        stored = sem("stored")
        fin = sem("final_rows")

        class Layer:
            pass
        L = []
        for l in range(LAYERS):
            o = Layer()
            o.rot, o.rsin, o.rcos, o.rdone = (sem(f"{x}{l}") for x in ("rot", "rope_sin", "rope_cos", "roped"))
            o.vt, o.vc = sem(f"values_turned{l}"), sem(f"values_copied{l}")
            o.tab = sem(f"tables{l}")
            o.sc = [sem(f"scores{c}_{l}") for c in range(2)]
            o.nb = [sem(f"negmax{c}_{l}") for c in range(2)]
            o.ex = [sem(f"exp{c}_{l}") for c in range(2)]
            o.es = [sem(f"sink_exp{c}_{l}") for c in range(2)]
            o.wr, o.tr, o.te, o.pv, o.oe = (sem(f"{x}{l}") for x in (
                "probs_ready", "probs_turned", "turned_copied", "values_mixed", "mixed_copied"))
            o.kt, o.kd, o.kv, o.st = (sem(f"{x}{l}") for x in ("k_turned", "k_decayed", "kv_ready", "state_ready"))
            o.qd, o.at, o.ad, o.y, o.yc = (sem(f"{x}{l}") for x in (
                "q_decayed", "ret_scores", "ret_decayed", "ret_out", "ret_copied"))
            o.gp, o.gd = sem(f"group_pool{l}"), sem(f"group_vec{l}")
            o.mt, o.mh, o.ml = (sem(f"{x}{l}") for x in ("mixed_turned", "mixed_hi", "mixed_lo"))
            L.append(o)

        def unit_loop(eng, l, name, body, head=0, tail=0):
            cnt = seg_at[l, name][1]
            tail += (cnt - head - tail) % 2
            for r in range(head):
                body(r, 0)
            if cnt - head - tail:
                with eng.Fori(0, (cnt - head - tail) // 2) as i:
                    body(head, i)
                    body(head + 1, i)
            for r in range(cnt - tail, cnt):
                body(r, 0)

        def flat(ap):
            return ap.rearrange("p a t -> p (a t)")

        block = stack.enter_context(nc.Block())

        @block.sync
        def _(sp):
            def weights(l, name, head=0, tail=0):
                n0, cnt, k, a0 = seg_at[l, name]
                src = wk8 if k == 8 else wk11

                def load(r, i):
                    n = n0 + r
                    if n >= 2:
                        sp.wait_ge(w_lo, 2 * i + (n - 1))
                    row = src[a0 + r] if isinstance(i, int) else flat(
                        src[bass.ds(2 * i + (a0 + r), 1)].rearrange("o p c -> p o c"))
                    sp.dma_start(raw[n % 2][:, 0:k * P], row).then_inc(w_landed[n % 2], 16)
                unit_loop(sp, l, name, load, head=2 if n0 == 0 else 0)

            def mod(m, i=0):
                if m >= 2:
                    sp.wait_ge(m_used, 2 * i + (m - 1))
                row = wmod[m + 16] if isinstance(i, int) else flat(
                    wmod[bass.ds(2 * i + (m + 16), 1)].rearrange("o p c -> p o c"))
                sp.dma_start(mraw[m % 2][:, :], row).then_inc(m_landed[m % 2], 16)

            sp.dma_start(cs[:, :], cin).then_inc(c_landed, 16)
            sp.dma_start(kc[:, :], kin).then_inc(c_landed, 16)
            sp.dma_start(cb[:, :, :].rearrange("p c k -> p (c k)"), cbin).then_inc(cb_landed, 16)
            for j in range(8):
                sp.dma_start(first_mod[:, 2 * j:2 * j + 2, :],
                             wmod[2 * j:2 * j + 2].rearrange("m p c -> p m c")).then_inc(m_first[j], 16)
                if j == 0:
                    sp.dma_start(vec[:, :], vin).then_inc(v_landed, 16)
                    sp.dma_start(fing[:, :], finalg).then_inc(v_landed, 16)
                    sp.dma_start(mraw[0][:, 0:512], lamin).then_inc(v_landed, 16)
                if j == 4:
                    sp.dma_start(flat(xT), xin).then_inc(x_landed, 16)
            for l in range(LAYERS):
                if l == 0:
                    for name, per in (("in_kv", 4), ("in_q", 4)):
                        n0, cnt, _, a0 = seg_at[l, name]
                        m0 = 0 if name == "in_kv" else 20
                        head = 2 if n0 == 0 else 0
                        pairs = (cnt - head) // 2
                        for r in range(head):
                            sp.dma_start(raw[r][:, 0:KD8 * P], wk8[a0 + r]).then_inc(w_landed[r], 16)
                        if name == "in_kv":
                            sp.wait_ge(start_v, 3)
                            for m in range(4):
                                mod(m)
                            m0, pairs = 4, pairs - 1
                            for r in (2, 3):
                                sp.wait_ge(w_lo, r - 1)
                                sp.dma_start(raw[r % 2][:, 0:KD8 * P], wk8[a0 + r]).then_inc(w_landed[r % 2], 16)
                            head = 4
                        with sp.Fori(0, pairs) as i:
                            for j in range(2):
                                n = n0 + head + j
                                sp.wait_ge(w_lo, 2 * i + (n - 1))
                                sp.dma_start(raw[n % 2][:, 0:KD8 * P], flat(
                                    wk8[bass.ds(2 * i + (a0 + head + j), 1)].rearrange("o p c -> p o c"))
                                ).then_inc(w_landed[n % 2], 16)
                            for j in range(per):
                                sp.wait_ge(m_used, per * i + (m0 + j - 1))
                                sp.dma_start(mraw[j % 2][:, :], flat(
                                    wmod[bass.ds(per * i + (m0 + j + 16), 1)].rearrange("o p c -> p o c"))
                                ).then_inc(m_landed[j % 2], 16)
                        n = n0 + cnt - 1
                        sp.wait_ge(w_lo, n - 1)
                        sp.dma_start(raw[n % 2][:, 0:KD8 * P], wk8[a0 + cnt - 1]).then_inc(w_landed[n % 2], 16)
                        if name == "in_kv":
                            assert m0 + per * pairs == 20
                    sp.wait_ge(m_used, 36)
                else:
                    weights(l, "in_kv")
                    weights(l, "in_q")
                sp.wait_ge(hlo, 16 * l + 8)
                sp.dma_start(rope, rin).then_inc(ropeld, 16)
                weights(l, "out")
                for hf in range(2):
                    if l == 0:
                        if hf == 0:
                            sp.wait_ge(L[0].ml, 8)
                            sp.dma_start(cb[:, :, :].rearrange("p c k -> p (c k)"), cbin).then_inc(cb_landed, 16)
                        n0, cnt, _, a0 = seg_at[l, f"up{hf}"]
                        with sp.Fori(0, cnt // 2) as i:
                            for j in range(2):
                                sp.wait_ge(w_lo, 2 * i + (n0 + j - 1))
                                sp.dma_start(raw[(n0 + j) % 2][:, 0:KD8 * P], flat(
                                    wk8[bass.ds(2 * i + (a0 + j), 1)].rearrange("o p c -> p o c"))
                                ).then_inc(w_landed[(n0 + j) % 2], 16)
                            for j in range(2):
                                mod(36 + cnt * hf + j, i)
                    else:
                        weights(l, f"up{hf}")
                    weights(l, f"down{hf}")
            for k in range(KD8):
                sp.wait_ge(fin, k + 1)
                sp.dma_start(out[:, k, :], pT[:, 8 + k, 0:LAT]).then_inc(stored, 16)
            sp.wait_ge(stored, 16 * KD8)

        @block.gpsimd
        def _(pool):
            def residues(l, name):
                n0, cnt, k, _ = seg_at[l, name]

                def lo(r, i):
                    j = (n0 + r) % 2
                    pool.wait_ge(w_hi, 2 * i + (n0 + r + 1))
                    nc.gpsimd.tensor_tensor(wsp[j][:, KH * P:KH * P + k * P], raw[j][:, 0:k * P],
                                            wsp[j][:, 0:k * P].bitcast(F32), ALU.subtract).then_inc(w_lo, 1)
                unit_loop(pool, l, name, lo)

            for l in range(LAYERS):
                o = L[l]
                residues(l, "in_kv")
                residues(l, "in_q")
                pool.wait_ge(ev, seg_end[l, "in_q"])
                pool.wait_ge(ropeld, 16 * (l + 1))
                for i, (t, w) in enumerate(ROPED):
                    if i >= 2:
                        pool.wait_ge(o.rdone, i - 1)
                    c = R_C64 if w == HD else R_C32
                    nc.gpsimd.tensor_tensor(ropeB[i % 2], pT[:, t, 0:LAT], rope[:, c:c + LAT],
                                            ALU.mult).then_inc(o.rcos, 1)
                nt = tiles_of(l)
                pool.wait_ge(o.rdone, len(ROPED))
                pool.wait_ge(o.tab, 1)
                for j in range(nt):
                    if j >= 2:
                        pool.wait_ge(o.at, j - 1)
                    qj = pT[:, T_QR, j * P:(j + 1) * P]
                    nc.gpsimd.tensor_tensor(
                        tm[:, 2048 + 512 * (j % 2):2560 + 512 * (j % 2)].rearrange("p (h c) -> p h c", h=4),
                        qj.unsqueeze(1).to_broadcast([P, 4, P]),
                        kc[:, K_BD:K_BD + 256:64].unsqueeze(2).to_broadcast([P, 4, P]),
                        ALU.mult).then_inc(o.qd, 1)
                    if j >= 2:
                        pool.wait_ge(o.y, j - 1)
                    for d in range(2):
                        nc.gpsimd.tensor_tensor(tm[:, 512 + 256 * (j % 2) + P * d:][:, 0:P], qj,
                                                qdec[:, d * P:(d + 1) * P], ALU.mult).then_inc(o.qd, 1)
                yg = ysb[:, 0:nt]

                def spread(c0, w):
                    return cst[:, c0:c0 + 4 * nt].rearrange("p (n h) -> p n h", h=4).unsqueeze(3).to_broadcast(
                        [P, nt, 4, w])

                pool.wait_ge(o.gd, 1)
                nc.gpsimd.tensor_tensor(yg, yg, spread(48, 64), ALU.subtract).then_inc(o.gp, 1)
                pool.wait_ge(o.gp, 1)
                nc.gpsimd.tensor_tensor(ysq[:, 0:nt], yg, yg, ALU.mult).then_inc(o.gp, 1)
                pool.wait_ge(o.gd, 2)
                nc.gpsimd.tensor_tensor(cst[:, 24:24 + 4 * nt], cst[:, 72:72 + 4 * nt], half[:, 0:4 * nt],
                                        ALU.pow).then_inc(o.gp, 1)
                pool.wait_ge(o.gp, 3)
                nc.gpsimd.tensor_tensor(yg, yg, spread(24, 64), ALU.mult).then_inc(o.gp, 1)
                pool.wait_ge(o.gp, 4)
                nc.gpsimd.tensor_tensor(mix[:, 0:nt, 768:1024], mix[:, 0:nt, 768:1024], vt[:, 0:nt, V_G:V_G + 256],
                                        ALU.mult).then_inc(o.gp, 1)
                pool.wait_ge(o.gd, 3)
                nc.gpsimd.tensor_tensor(cst[:, 0:4 * nt], ssb[:, 0:4 * nt], half[:, 0:4 * nt],
                                        ALU.pow).then_inc(o.gp, 1)
                pool.wait_ge(o.gp, 6)
                mb = mix[:, 0:nt, 256:768].rearrange("p n (h e) -> p n h e", h=4)
                nc.gpsimd.tensor_tensor(mb, mb, spread(0, P), ALU.mult).then_inc(o.gp, 1)
                for name in ("out", "up0", "down0", "up1", "down1"):
                    residues(l, name)

        @block.scalar
        def _(act):
            def split_hi(l, name, r, i=0):
                n0, cnt, k, _ = seg_at[l, name]
                if isinstance(i, int) and r >= cnt:
                    nxt = order[order.index((l, name)) + 1:][:1]
                    if nxt:
                        split_hi(*nxt[0], r - cnt)
                    return
                n = n0 + r
                act.wait_ge(w_landed[n % 2], 16 * i + 16 * (n // 2 + 1))
                if n >= 2:
                    act.wait_ge(used, 2 * i + (n - 1))
                nc.scalar.activation(wsp[n % 2][:, 0:k * P], raw[n % 2][:, 0:k * P], ACT.Copy).then_inc(w_hi, 1)

            def splits_only(l, name):
                unit_loop(act, l, name, lambda r, i: split_hi(l, name, r + 2, i), tail=2)

            def square(ni, k, width, kk=None):
                if isinstance(k, int) and k == 0:
                    nc.scalar.activation(sacc[:, 0:width], xT[:, 0, 0:width], ACT.Square).then_inc(sqd, 1)
                    return
                if not (isinstance(k, int) and k == 1):
                    act.wait_ge(sqa, 7 * ni + k - 1)
                nc.scalar.activation(sq[:, 0:width], flat(xT[:, bass.ds(k, 1), 0:width]), ACT.Square).then_inc(sqd, 1)

            def squares(l, name, ni, width):
                n0 = seg_at[l, name][0]

                def body(r, i):
                    act.wait_ge(used, 2 * i + (n0 + r + 1))
                    split_hi(l, name, r + 2, i)
                    act.wait_ge(ev, 2 * i + (n0 + r + 1))
                    square(ni, r if isinstance(i, int) else 2 * i + r, width)
                unit_loop(act, l, name, body, head=2, tail=2)

            def root(ni, nt):
                nc.scalar.activation(dummy[:, ni:ni + 1], eps[:, :], ACT.Sqrt)
                act.wait_ge(ssd, ni + 1)
                nc.scalar.activation(rsd[:, 0:nt], X1[:, 0:nt], ACT.Sqrt, bias=eps[:, 0:1],
                                     scale=1.0 / D).then_inc(srt, 1)

            def operand(ni, w, gr):
                for k in range(KD8):
                    act.wait_ge(vsd, 8 * ni + k + 1)
                    for g, (a, b) in enumerate(gr):
                        ins = nc.scalar.activation(hTv[:, 0, k, a:b], tm[:, (k % 2) * TOK + a:(k % 2) * TOK + b],
                                                   ACT.Identity, bias=mvl[ni // 2][:, 24 * w + k, g:g + 1])
                    ins.then_inc(hid, 1)

            act.wait_ge(c_landed, 32)
            nc.scalar.activation(csil[:, :], cs[:, :], ACT.Silu).then_inc(c_ready, 1)
            act.wait_ge(cb_landed, 16)
            nc.scalar.activation(cb[:, :, :], cb[:, :, :], ACT.Silu).then_inc(cb_ready, 1)
            act.wait_ge(x_landed, 16)
            for k in range(KD8):
                square(0, k, TOK)
            act.wait_ge(start_v, 3)
            nc.scalar.activation(cst[:, 20:40], cst[:, 0:20], ACT.Exp, scale=-1.0).then_inc(start_a, 1)
            nc.scalar.activation(cst[:, 44:48], cst[:, 40:44], ACT.Exp).then_inc(start_a, 1)
            act.wait_ge(start_v, 4)
            nc.scalar.activation(cst[:, 50:70], cst[:, 70:90], ACT.Ln).then_inc(start_a, 1)
            for l in range(LAYERS):
                o = L[l]
                root(2 * l, 6)
                if l == 0:
                    split_hi(0, "in_kv", 0)
                    split_hi(0, "in_kv", 1)
                operand(2 * l, 0, [(0, LAT), (LAT, TOK)])
                for name in ("in_kv", "in_q"):
                    n0, cnt, k, _ = seg_at[l, name]
                    t0 = 0 if name == "in_kv" else N_KV
                    width = groups_of(l, name)[-1][1]

                    def project(r, i):
                        act.wait_ge(used, 2 * i + (n0 + r + 1))
                        nc.scalar.activation(flat(pT[:, bass.ds(2 * i + (t0 + r), 1), 0:width]),
                                             G[(n0 + r) % 2][:, 0:width], ACT.Copy,
                                             scale=kc[:, bass.ds(2 * i + (K_SC + r), 1)] if t0 else 1.0
                                             ).then_inc(ev, 1)
                        split_hi(l, name, r + 2, i)
                    unit_loop(act, l, name, project, tail=2)
                act.wait_ge(ropeld, 16 * (l + 1))
                act.wait_ge(used, seg_end[l, "in_q"])
                for d, c in ((0, R_C1), (1, R_C2)):
                    nc.scalar.activation(qdec[:, d * P:(d + 1) * P], rope[:, c:c + P], ACT.Exp,
                                         scale=lg[:, 10 * l + 8 + d:10 * l + 9 + d]).then_inc(tabs_a, 1)
                    nc.scalar.activation(kdec[:, 4 * d:4 * d + 4], lg[:, 10 * l + 4 * d:10 * l + 4 * d + 4], ACT.Exp,
                                         scale=kc[:, K_KJ + d:K_KJ + d + 1]).then_inc(tabs_a, 1)
                nc.scalar.activation(gch[:, :], lg[:, 10 * l + 8:10 * l + 10], ACT.Exp,
                                     scale=float(P)).then_inc(tabs_a, 1)
                for h in range(4):
                    for d, c in ((0, R_DP), (1, R_DN)):
                        nc.scalar.activation(dexp[:, 2 * h + d, :], rope[:, c:c + P], ACT.Exp,
                                             scale=lg[:, 10 * l + 4 * d + h:][:, 0:1]).then_inc(tabs_a, 1)
                for v in range(9):
                    nt = 6 if v < 7 else tiles_of(l)
                    act.wait_ge(o.vt, v + 1)
                    nc.scalar.activation(vt[:, 0:nt, v * P:(v + 1) * P],
                                         G[v % 2][:, 0:nt * P].rearrange("p (t c) -> p t c", t=nt),
                                         ACT.Copy if v < 7 else ACT.Silu).then_inc(o.vc, 1)
                nt = tiles_of(l)
                for j in range(nt):
                    act.wait_ge(o.y, j + 1)
                    nc.scalar.activation(mix[:, j, 768:1024], G[1][:, 512 * (j % 2):512 * (j % 2) + 256],
                                         ACT.Copy).then_inc(o.yc, 1)
                steps = attention_steps(l)
                groups, ends = turn_groups(steps)

                def copy_out(t):
                    s, c, _, w, col = groups[t]
                    kind, h, q = steps[s][:3]
                    act.wait_ge(o.pv, t + 1)
                    act.wait_ge(o.wr, ends[s])
                    inv = RC[:, 2 * s + c:2 * s + c + 1]
                    first = nc.scalar.activation(mix[:, q, col:col + w], X1[:, 0:w], ACT.Copy, scale=inv)
                    if kind == "B":
                        if t:
                            act.wait_ge(o.oe, t)
                        first = nc.scalar.activation(tm[:, 2944:2944 + P], X1[:, 0:P], ACT.Square,
                                                     scale=inv, accum_out=ssb[:, 4 * q + h:4 * q + h + 1])
                    first.then_inc(o.oe, 1)

                for s in range(len(steps) + 1):
                    if s < len(steps):
                        kind, h, q, spans, keys = steps[s]
                        p, nk = s % 2, P * len(keys)
                        if s >= 2:
                            act.wait_ge(o.tr, ends[s - 2])
                        for c in range(2):
                            m = 2 * s + c
                            act.wait_ge(o.nb[c], s + 1)
                            nc.scalar.activation(Pb[p][c][:, 0:nk], G[c][:, 0:nk], ACT.Exp, bias=NB[:, m:m + 1],
                                                 accum_out=LS[:, m:m + 1]).then_inc(o.ex[c], 1)
                            if kind == "A":
                                nc.scalar.activation(ES[:, m:m + 1], vecs(l, SK + 2 * h + c, 1), ACT.Exp,
                                                     bias=NB[:, m:m + 1]).then_inc(o.es[c], 1)
                    if s >= 1:
                        for t in range(ends[s - 2] if s >= 2 else 0, ends[s - 1]):
                            nk = P * len(steps[groups[t][0]][4])
                            act.wait_ge(o.tr, t + 1)
                            if t >= 2:
                                act.wait_ge(o.pv, t - 1)
                            nc.scalar.activation(WT[t % 2][:, 0:nk], X0[:, 0:nk], ACT.Copy).then_inc(o.te, 1)
                            if t >= 1:
                                copy_out(t - 1)
                copy_out(len(groups) - 1)
                for i, f in enumerate(FMT):
                    act.wait_ge(o.mt, i + 1)
                    nc.scalar.activation(hTv[:, 0, f, 0:nt * P], (X0, X1)[i % 2][:, 0:nt * P], ACT.Copy,
                                         scale=fsc[:, f:f + 1]).then_inc(o.mh, 1)
                width = TOK if l == 0 else LAT
                squares(l, "out", 2 * l + 1, width)
                root(2 * l + 1, nt)
                if l == 0:
                    act.wait_ge(cb_landed, 32)
                    nc.scalar.activation(cb[:, :, :], cb[:, :, :], ACT.Silu).then_inc(cb_ready, 1)
                operand(2 * l + 1, 1, groups_of(l, "up0"))
                accs = (tm[:, 0:TOK], tm[:, TOK:2 * TOK])
                for hf in range(2):
                    name, down = f"up{hf}", f"down{hf}"
                    n0, cnt, _, _ = seg_at[l, name]
                    g0 = (2 * l + hf) * KH

                    def pair(r, i):
                        for j in range(2):
                            act.wait_ge(used, 2 * i + (n0 + r + j + 1))
                            pr = g0 + r // 2
                            if pr:
                                act.wait_ge(glo if j == 0 else prodd, i + pr)
                            cw = vecs(l, CW, 176).rearrange("p (u w) -> p u w", w=4)[
                                :, bass.ds(2 * i + (hf * 22 + r + j), 1), :].rearrange("p a w -> p (a w)")
                            nc.scalar.activation(accs[j][:, 0:width], G[(n0 + r + j) % 2][:, 0:width], ACT.Identity,
                                                 bias=cw[:, 3:4], scale=cw[:, 1:2]).then_inc(accr, 1)
                            split_hi(l, name, r + j + 2, i)
                        act.wait_ge(ev, 2 * i + (n0 + r + 2))
                        nc.scalar.activation(accs[1][:, 0:width], accs[1][:, 0:width], ACT.Silu).then_inc(silud, 1)
                        act.wait_ge(prodd, i + (g0 + r // 2 + 1))
                        nc.scalar.activation(flat(gTv[:, 0, bass.ds(i + r // 2, 1), 0:width]), accs[0][:, 0:width],
                                             ACT.Copy).then_inc(ghi, 1)
                    pair(0, 0)
                    with act.Fori(0, KH - 2) as i:
                        pair(2, i)
                    pair(cnt - 2, 0)
                    if hf == 0:
                        splits_only(l, down)
                    else:
                        act.wait_ge(glo, (2 * l + 2) * KH)
                        squares(l, down, 2 * l + 2, TOK if l == 0 else LAT)
            root(4, 4)

        @block.vector
        def _(dve):
            chain = [0]

            def link(ins):
                chain[0] += 1
                ins.then_inc(dv, 1)
                dve.wait_ge(dv, chain[0])

            def add_square(ni, k, width):
                dve.wait_ge(sqd, 8 * ni + k + 1)
                if isinstance(k, int) and k > 1 or not isinstance(k, int):
                    dve.wait_ge(sqa, 7 * ni + k - 1)
                nc.vector.tensor_tensor(sacc[:, 0:width], sacc[:, 0:width], sq[:, 0:width], ALU.add).then_inc(sqa, 1)

            def norm(ni, nt):
                dve.wait_ge(srt, ni + 1)
                link(nc.vector.reciprocal(rsd[:, 8:8 + nt], rsd[:, 0:nt]))
                nc.vector.tensor_tensor(dg[:, 0:nt * P].rearrange("p (t c) -> p t c", t=nt),
                                        ident.unsqueeze(1).to_broadcast([P, nt, P]),
                                        rsd[:, 8:8 + nt].unsqueeze(2).to_broadcast([P, nt, P]),
                                        ALU.mult).then_inc(dgd, 1)

            def operand(ni, w, gr):
                Av, mv = Avl[ni // 2], mvl[ni // 2]

                def slot(k):
                    return tm[:, (k % 2) * TOK:(k % 2 + 1) * TOK]

                def scaled(k):
                    if k >= 2:
                        dve.wait_ge(hlo, 8 * ni + k - 1)
                    for g, (a, b) in enumerate(gr):
                        ins = nc.vector.scalar_tensor_tensor(slot(k)[:, a:b], xT[:, k, a:b], Av[:, w, k, g:g + 1],
                                                             X0[:, a:b], ALU.mult, ALU.mult)
                    ins.then_inc(vsd, 1)

                dve.wait_ge(rbd, ni + 1)
                scaled(0)
                scaled(1)
                for k in range(KD8):
                    dve.wait_ge(hid, 8 * ni + k + 1)
                    for g, (a, b) in enumerate(gr):
                        ins = nc.vector.scalar_tensor_tensor(hTv[:, 1, k, a:b], slot(k)[:, a:b],
                                                             mv[:, 24 * w + k, g:g + 1],
                                                             hTv[:, 0, k, a:b].bitcast(F32), ALU.add, ALU.subtract)
                    ins.then_inc(hlo, 1)
                    if k + 2 < KD8:
                        scaled(k + 2)

            def scales(l, w, n):
                gv = vecs(l, N1 if w == 0 else N2, 16).rearrange("p (k c) -> p k c", c=2)
                link(nc.vector.scalar_tensor_tensor(Avl[l][:, w, :, 0:n], mvl[l][:, 24 * w + 8:24 * w + 16, 0:n], 1.0,
                                                    gv[:, :, 0:n], ALU.add, ALU.mult))

            def modulation(l, src, a, b, n=2):
                bm = vecs(l, BM, 96).rearrange("p (m c) -> p m c", c=2)
                link(nc.vector.tensor_tensor(mvl[l][:, a:b, 0:n], src, bm[:, a:b, 0:n], ALU.add))

            def mod(row, tile, n, done, before):
                for c in range(n):
                    if before is not None and c == 0:
                        dve.wait_ge(*before)
                    ins = nc.vector.scalar_tensor_tensor(
                        (X0, X1)[c][:, :], row, 1.0, cb[:, c, :], ALU.mult, ALU.mult,
                        accum_out=msv[:, bass.ds(tile, 1), c:c + 1].rearrange("p a c -> p (a c)"))
                ins.then_inc(done, 1)

            def ring_mod(m, i, n):
                dve.wait_ge(m_landed[m % 2], 16 * i + 16 * (m // 2 + 1))
                mod(mraw[m % 2][:, :], 2 * i + (m + 16), n, m_used, (m_used, 2 * i + m) if m else (m_dv, 8))

            def residual(l, name, gate, ni=None):
                n0, cnt, _, _ = seg_at[l, name]
                width = groups_of(l, name)[-1][1]

                def add(r, i):
                    dve.wait_ge(used, 2 * i + (n0 + r + 1))
                    m = 2 * i + r
                    for g, (a, b) in enumerate(groups_of(l, name)):
                        xk = flat(xT[:, bass.ds(m, 1), a:b])
                        ga = mvl[l][:, bass.ds(m + gate * 8, 1), g:g + 1].rearrange("p a c -> p (a c)")
                        ins = nc.vector.scalar_tensor_tensor(xk, G[(n0 + r) % 2][:, a:b], ga, xk, ALU.mult, ALU.add)
                    ins.then_inc(ev, 1)
                    if ni is not None and r >= 2:
                        add_square(ni, m - 1, width)
                unit_loop(dve, l, name, add, head=2)
                if ni is not None:
                    add_square(ni, 7, width)

            nc.vector.memset(eps[:, :], EPS).then_inc(start_v, 1)
            nc.vector.memset(half[:, :], -0.5).then_inc(start_v, 1)
            dve.wait_ge(v_landed, 48)
            for l in range(LAYERS):
                link(nc.vector.tensor_scalar(nsink[:, 4 * l:4 * l + 4], vecs(l, SK, 4), -1.0, None, ALU.mult))
            lv = mraw[0][:, 0:512].rearrange("p (a b c) -> p a b c", a=4, b=2)
            lp = mraw[1][:, 0:256].rearrange("p (a c) -> p a c", a=4)
            link(nc.vector.tensor_tensor(lp, lv[:, :, 0, :], lv[:, :, 1, :], ALU.mult))
            link(nc.vector.reduce_sum(cst[:, 40:44], lp, AXX))
            for l in range(LAYERS):
                link(nc.vector.tensor_copy(cst[:, 70 + 10 * l:80 + 10 * l], vecs(l, DZ, 10)))
            z = cst[:, 70:90]
            link(nc.vector.tensor_scalar(cst[:, 50:70], z, -1.0, None, ALU.mult))
            link(nc.vector.tensor_scalar(lg[:, :], z, 0.0, None, ALU.min))
            nc.vector.tensor_tensor(cst[:, 0:20], z, cst[:, 50:70], ALU.max).then_inc(start_v, 1)
            dve.wait_ge(cb_ready, 1)
            for j in range(8):
                dve.wait_ge(m_first[j], 16)
                mod(first_mod[:, 2 * j + 1, :], 8 + j, 2, m_dv, (m_dv, j) if j else None)
                if j == 0:
                    dve.wait_ge(start_v, 3)
                if j >= 5:
                    for k in range(2 * j - 9, 2 * j - 7):
                        add_square(0, k, TOK)
            add_square(0, 7, TOK)
            dve.wait_ge(start_a, 2)
            nc.vector.tensor_scalar(cst[:, 70:90], cst[:, 20:40], 1.0, None, ALU.add).then_inc(start_v, 1)
            lam_init = [0.8 - 0.6 * math.exp(-0.3 * l) for l in range(LAYERS)]
            for l in range(LAYERS):
                link(nc.vector.tensor_tensor(nlam[:, l:l + 1], cst[:, 45 + 2 * l:46 + 2 * l],
                                             cst[:, 44 + 2 * l:45 + 2 * l], ALU.subtract))
                link(nc.vector.tensor_scalar(nlam[:, l:l + 1], nlam[:, l:l + 1], -lam_init[l], None, ALU.add))
            dve.wait_ge(start_a, 3)
            link(nc.vector.tensor_tensor(lg[:, :], lg[:, :], cst[:, 50:70], ALU.subtract))
            for l in range(LAYERS):
                o = L[l]
                if l == 0:
                    dve.wait_ge(m_pe, 1)
                    modulation(0, G[0][:, 0:16].rearrange("p (m c) -> p m c", c=2), 0, 8)
                    dve.wait_ge(m_dv, 8)
                    modulation(0, msv[:, 8:16], 8, 16)
                    scales(0, 0, 2)
                norm(2 * l, 6)
                operand(2 * l, 0, [(0, LAT), (LAT, TOK)])
                if l == 0:
                    ring_mod(0, 0, 2)
                    ring_mod(1, 0, 2)
                    with dve.Fori(0, 17) as i:
                        ring_mod(2, i, 2)
                        ring_mod(3, i, 2)
                    dve.wait_ge(m_used, 36)
                    modulation(0, msv[:, 16:MODS], 16, MODS)
                    scales(0, 1, 2)
                for i, (t, w) in enumerate(ROPED):
                    if i == 0:
                        dve.wait_ge(ropeld, 16 * (l + 1))
                    dve.wait_ge(o.rot, i + 1)
                    if i >= 2:
                        dve.wait_ge(o.rdone, i - 1)
                    c = R_S64 if w == HD else R_S32
                    nc.vector.tensor_tensor(ropeA[i % 2], X0[:, 512 * (i % 2):512 * (i % 2) + LAT], rope[:, c:c + LAT],
                                            ALU.mult).then_inc(o.rsin, 1)
                    dve.wait_ge(o.rsin, i + 1)
                    dve.wait_ge(o.rcos, i + 1)
                    nc.vector.tensor_tensor(pT[:, t, 0:LAT], ropeA[i % 2], ropeB[i % 2], ALU.add).then_inc(o.rdone, 1)
                dve.wait_ge(tabs_a, 13 * (l + 1))
                link(nc.vector.tensor_scalar(kdec[:, :], kdec[:, :], CQ ** -0.5, None, ALU.mult))
                for h in range(4):
                    md = mdec[:, h * P:(h + 1) * P]
                    link(nc.vector.tensor_tensor(md, dexp[:, 2 * h, :], rope[:, R_MG:R_MG + P], ALU.mult))
                    link(nc.vector.tensor_tensor(dexp[:, 2 * h + 1, :], dexp[:, 2 * h + 1, :],
                                                 rope[:, R_ML:R_ML + P], ALU.mult))
                    link(nc.vector.tensor_tensor(md, md, dexp[:, 2 * h + 1, :], ALU.add))
                link(nc.vector.memset(fsc[:, :], 1.0))
                nc.vector.tensor_scalar(fsc[:, 2:6], vecs(l, SG, 1).to_broadcast([P, 4]),
                                        1.0 - lam_init[l], None, ALU.mult).then_inc(o.tab, 1)
                dve.wait_ge(o.kt, 1)
                for d in range(2):
                    kb = kdec[:, 4 * d:4 * d + 4].unsqueeze(1).unsqueeze(3).to_broadcast([P, 6, 4, CQ])
                    nc.vector.tensor_tensor(kdk[:, d].rearrange("p n (h e) -> p n h e", h=4),
                                            G[0][:, 0:TOK].rearrange("p (n h e) -> p n h e", n=6, h=4),
                                            kb, ALU.mult).then_inc(o.kd, 1)
                for i, (d, n, to, prev) in enumerate(STATE_CHAIN):
                    dve.wait_ge(o.kv, i + 1)
                    dst = states[:, d, to, :] if prev is None else tm[:, 256 * (i % 2):256 * (i % 2) + 256]
                    src = (G[1] if i % 4 < 2 else X0)[:, 512 * (i % 2):512 * (i % 2) + 256]
                    if prev is not None:
                        link(nc.vector.tensor_tensor(dst, src, kc[:, K_BD:K_BD + 256], ALU.mult))
                        nc.vector.scalar_tensor_tensor(states[:, d, to, :], states[:, d, prev, :], gch[:, d:d + 1],
                                                       dst, ALU.mult, ALU.add).then_inc(o.st, 1)
                    else:
                        nc.vector.tensor_tensor(dst, src, kc[:, K_BD:K_BD + 256], ALU.mult).then_inc(o.st, 1)
                    dve.wait_ge(o.st, i + 1)
                nt = tiles_of(l)
                for j in range(nt):
                    dve.wait_ge(o.at, j + 1)
                    if j >= 2:
                        dve.wait_ge(o.y, j - 1)
                    nc.vector.tensor_tensor(tm[:, 1024 + 512 * (j % 2):1536 + 512 * (j % 2)],
                                            X0[:, 512 * (j % 2):512 * (j % 2) + 512], mdec[:, :],
                                            ALU.mult).then_inc(o.ad, 1)
                steps = attention_steps(l)
                groups, ends = turn_groups(steps)
                windowed = [sum(st[0] == "A" for st in steps[:s + 1]) for s in range(len(steps))]
                last_b = max(s for s, st in enumerate(steps) if st[0] == "B")
                for s in range(len(steps) + 1):
                    if s >= 1:
                        kind, h, q, spans, keys = steps[s - 1]
                        p, nk, m = (s - 1) % 2, P * len(keys), 2 * (s - 1)
                        if kind == "B":
                            dve.wait_ge(o.ex[0], s)
                            dve.wait_ge(o.ex[1], s)
                            link(nc.vector.reciprocal(RC[:, m:m + 2], LS[:, m:m + 2]))
                            link(nc.vector.scalar_tensor_tensor(ES[:, m:m + 1], RC[:, m + 1:m + 2], LS[:, m:m + 1],
                                                                nlam[:, l:l + 1], ALU.mult, ALU.mult))
                            nc.vector.scalar_tensor_tensor(Pb[p][0][:, 0:nk], Pb[p][1][:, 0:nk], ES[:, m:m + 1],
                                                           Pb[p][0][:, 0:nk], ALU.mult, ALU.add).then_inc(o.wr, 1)
                        else:
                            for c in range(2):
                                dve.wait_ge(o.es[c], windowed[s - 1])
                            link(nc.vector.tensor_tensor(LS[:, m:m + 2], LS[:, m:m + 2], ES[:, m:m + 2], ALU.add))
                            nc.vector.reciprocal(RC[:, m:m + 2], LS[:, m:m + 2]).then_inc(o.wr, 2)
                    if s < len(steps):
                        kind, h, q, spans, keys = steps[s]
                        p, nk = s % 2, P * len(keys)
                        for c in range(2):
                            m = 2 * s + c
                            dve.wait_ge(o.sc[c], s + 1)
                            mx = nc.vector.reduce_max(NB[:, m:m + 1], G[c][:, 0:nk], AXX, negate=True)
                            if kind == "A":
                                link(mx)
                                mx = nc.vector.tensor_tensor(NB[:, m:m + 1], NB[:, m:m + 1],
                                                             nsink[:, 4 * l + 2 * h + c:][:, 0:1], ALU.min)
                            mx.then_inc(o.nb[c], 1)
                    if s == 1:
                        dve.wait_ge(o.yc, nt)
                        link(nc.vector.reduce_sum(cst[:, 48:48 + 4 * nt].rearrange("p (n h) -> p n h", h=4),
                                                  ysb[:, 0:nt], AXX))
                        nc.vector.tensor_scalar(cst[:, 48:48 + 4 * nt], cst[:, 48:48 + 4 * nt], 1.0 / 64, None,
                                                ALU.mult).then_inc(o.gd, 1)
                    if s == 5:
                        dve.wait_ge(o.gp, 2)
                        link(nc.vector.reduce_sum(cst[:, 72:72 + 4 * nt].rearrange("p (n h) -> p n h", h=4),
                                                  ysq[:, 0:nt], AXX))
                        nc.vector.tensor_scalar(cst[:, 72:72 + 4 * nt], cst[:, 72:72 + 4 * nt], 1.0 / 64, EPS,
                                                ALU.mult, ALU.add).then_inc(o.gd, 1)
                    if s == last_b + 3:
                        dve.wait_ge(o.oe, ends[last_b])
                        nc.vector.tensor_scalar(ssb[:, 0:4 * nt], ssb[:, 0:4 * nt], 1.0 / P, EPS,
                                                ALU.mult, ALU.add).then_inc(o.gd, 1)
                for i, f in enumerate(FMT):
                    dve.wait_ge(o.mh, i + 1)
                    nc.vector.scalar_tensor_tensor(hTv[:, 1, f, 0:nt * P], (X0, X1)[i % 2][:, 0:nt * P], fsc[:, f:f + 1],
                                                   hTv[:, 0, f, 0:nt * P].bitcast(F32), ALU.mult,
                                                   ALU.subtract).then_inc(o.ml, 1)
                residual(l, "out", 2, ni=2 * l + 1)
                norm(2 * l + 1, nt)
                gr = groups_of(l, "up0")
                operand(2 * l + 1, 1, gr)
                width = gr[-1][1]
                accs = (tm[:, 0:TOK], tm[:, TOK:2 * TOK])
                for hf in range(2):
                    n0 = seg_at[l, f"up{hf}"][0]
                    g0 = (2 * l + hf) * KH
                    if l == 0 and hf == 0:
                        dve.wait_ge(cb_ready, 2)
                    with dve.Fori(0, KH) as i:
                        for j in range(2):
                            u0 = 2 * g0 + j
                            dve.wait_ge(accr, 2 * i + (u0 + 1))
                            cw = vecs(l, CW, 176).rearrange("p (u w) -> p u w", w=4)[
                                :, bass.ds(2 * i + (hf * 22 + j), 1), :].rearrange("p a w -> p (a w)")
                            src = G[(n0 + j) % 2]
                            for a, b in gr:
                                ins = nc.vector.scalar_tensor_tensor(accs[j][:, a + 1:b], src[:, a:b - 1], cw[:, 0:1],
                                                                     accs[j][:, a + 1:b], ALU.mult, ALU.add)
                            ins.then_inc(convl, 1)
                            dve.wait_ge(convl, 2 * i + (u0 + 1))
                            for a, b in gr:
                                ins = nc.vector.scalar_tensor_tensor(accs[j][:, a:b - 1], src[:, a + 1:b], cw[:, 2:3],
                                                                     accs[j][:, a:b - 1], ALU.mult, ALU.add)
                            ins.then_inc(ev, 1)
                        dve.wait_ge(silud, i + (g0 + 1))
                        nc.vector.tensor_tensor(accs[0][:, 0:width], accs[0][:, 0:width], accs[1][:, 0:width],
                                                ALU.mult).then_inc(prodd, 1)
                        dve.wait_ge(ghi, i + (g0 + 1))
                        nc.vector.tensor_tensor(flat(gTv[:, 1, bass.ds(i, 1), 0:width]), accs[0][:, 0:width],
                                                flat(gTv[:, 0, bass.ds(i, 1), 0:width]).bitcast(F32),
                                                ALU.subtract).then_inc(glo, 1)
                        if l == 0:
                            ring_mod(36 + 22 * hf, i, 2 - hf)
                            ring_mod(37 + 22 * hf, i, 2 - hf)
                    if hf == 1 and l == 0:
                        dve.wait_ge(m_used, 80)
                        modulation(1, msv[:, MODS:MODS + 26], 0, 26)
                        modulation(1, msv[:, MODS + 26:2 * MODS, 0:1], 26, MODS, 1)
                        scales(1, 0, 2)
                        scales(1, 1, 1)
                    residual(l, f"down{hf}", 5, ni=2 * l + 2 if hf else None)
            norm(4, 4)
            dve.wait_ge(rbd, 5)
            for k in range(KD8):
                nc.vector.scalar_tensor_tensor(pT[:, 8 + k, 0:LAT], xT[:, k, 0:LAT], fing[:, k:k + 1], X0[:, 0:LAT],
                                               ALU.mult, ALU.mult).then_inc(fin, 1)

        @block.tensor
        def _(pe):
            def norm(ni, nt):
                pe.wait_ge(sqa, 7 * ni + 7)
                for t in range(nt):
                    ins = nc.tensor.matmul(X1[:, t:t + 1], sacc[:, t * P:(t + 1) * P], ones[:, 0:1],
                                           start=True, stop=True)
                ins.then_inc(ssd, 1)
                pe.wait_ge(dgd, ni + 1)
                for a, b in ((0, LAT), (LAT, TOK))[:1 if nt == 4 else 2]:
                    ins = nc.tensor.matmul(X0[:, a:b], ones, dg[:, a:b], start=True, stop=True)
                ins.then_inc(rbd, 1)

            def multiply(l, name, r, i, rhs, gate=None, ks=None):
                n0, cnt, k, _ = seg_at[l, name]
                n = n0 + r
                pe.wait_ge(w_lo, 2 * i + (n + 1))
                if n >= 2:
                    pe.wait_ge(ev, 2 * i + (n - 1))
                gr = groups_of(l, name)
                ks = ks or list(range(k))
                for kn, kk in enumerate(ks):
                    if gate:
                        pe.wait_ge(gate[0], gate[1] + kn + 1)
                    for pi, (ws, xs) in enumerate(((0, 0), (0, 1), (1, 0))):
                        for a, b in gr:
                            ins = nc.tensor.matmul(G[n % 2][:, a:b], Wv[n % 2][ws][:, kk, :], rhs[:, xs, kk, a:b],
                                                   start=(kn == 0 and pi == 0), stop=(kn == k - 1 and pi == 2))
                ins.then_inc(used, 1)

            def segment(l, name, rhs, gate=None, ks=None):
                unit_loop(pe, l, name, lambda r, i: multiply(
                    l, name, r, i, rhs, gate if r == 0 and isinstance(i, int) else None, ks),
                    head=2 if gate else 0)

            pe.wait_ge(c_ready, 1)
            for j in range(8):
                pe.wait_ge(m_first[j], 16)
                wj = first_mod[:, 2 * j, :].rearrange("p (k m) -> p k m", k=KD8)
                for k in range(KD8):
                    ins = nc.tensor.matmul(G[0][:, 2 * j:2 * j + 2], wj[:, k, :], csv[:, k, :],
                                           start=(k == 0), stop=(k == KD8 - 1))
            ins.then_inc(m_pe, 1)
            for l in range(LAYERS):
                o = L[l]
                nt = tiles_of(l)
                norm(2 * l, 6)
                segment(l, "in_kv", hTv, (hlo, 16 * l))
                segment(l, "in_q", hTv)
                pe.wait_ge(ev, seg_end[l, "in_q"])
                for i in range(len(ROPED)):
                    t, w = ROPED[i]
                    if i >= 2:
                        pe.wait_ge(o.rsin, i - 1)
                    sw = K_S64 if w == HD else K_S32
                    nc.tensor.matmul(X0[:, 512 * (i % 2):512 * (i % 2) + LAT], kc[:, sw:sw + P], pT[:, t, 0:LAT],
                                     start=True, stop=True).then_inc(o.rot, 1)
                    if i < 9:
                        if i >= 2:
                            pe.wait_ge(o.vc, i - 1)
                        for t in range(6 if i < 7 else nt):
                            ins = nc.tensor.transpose(G[i % 2][:, t * P:(t + 1) * P], pT[:, T_VA + i, t * P:(t + 1) * P],
                                                      ident)
                        ins.then_inc(o.vt, 1)
                pe.wait_ge(o.rdone, len(ROPED))
                pe.wait_ge(o.vc, 9)
                for n in range(6):
                    ins = nc.tensor.transpose(G[0][:, n * P:(n + 1) * P], pT[:, T_KR, n * P:(n + 1) * P], ident)
                ins.then_inc(o.kt, 1)
                pe.wait_ge(o.kd, 2)
                for i, (d, n, to, prev) in enumerate(STATE_CHAIN):
                    if i >= 4:
                        pe.wait_ge(o.st, i - 3)
                    nc.tensor.matmul((G[1] if i % 4 < 2 else X0)[:, 512 * (i % 2):512 * (i % 2) + 256],
                                     kdk[:, d, n, :], vt[:, n, V_C:V_C + 256], start=True, stop=True).then_inc(o.kv, 1)
                pe.wait_ge(o.st, len(STATE_CHAIN))

                def ret_scores(j):
                    if j >= 2:
                        pe.wait_ge(o.ad, j - 1)
                    pe.wait_ge(o.qd, 3 * j + 1)
                    nc.tensor.matmul(X0[:, 512 * (j % 2):512 * (j % 2) + 512], pT[:, T_KR, j * P:(j + 1) * P],
                                     tm[:, 2048 + 512 * (j % 2):2560 + 512 * (j % 2)],
                                     start=True, stop=True).then_inc(o.at, 1)

                ret_scores(0)
                for j in range(nt):
                    if j + 1 < nt:
                        ret_scores(j + 1)
                    if j >= 2:
                        pe.wait_ge(o.yc, j - 1)
                    y = G[1][:, 512 * (j % 2):512 * (j % 2) + 256]
                    dirs = [d for d in range(2) if j != 4 + d]
                    pe.wait_ge(o.qd, 3 * j + 3)
                    for d in dirs:
                        nc.tensor.matmul(y, tm[:, 512 + 256 * (j % 2) + P * d:][:, 0:P], states[:, d, j, :],
                                         start=(d == dirs[0]), stop=False)
                    pe.wait_ge(o.ad, j + 1)
                    for h in range(4):
                        ins = nc.tensor.matmul(y[:, 64 * h:64 * h + 64], tm[:, 1024 + 512 * (j % 2) + h * P:][:, 0:P],
                                               vt[:, j, V_C + 64 * h:V_C + 64 * h + 64], start=False, stop=(h == 3))
                    ins.then_inc(o.y, 1)
                steps = attention_steps(l)
                groups, ends = turn_groups(steps)

                def mix_values(t):
                    s, c, vcol, w, _ = groups[t]
                    keys = steps[s][4]
                    pe.wait_ge(o.te, t + 1)
                    if t >= 1:
                        pe.wait_ge(o.oe, t)
                    for i, kt in enumerate(keys):
                        ins = nc.tensor.matmul(X1[:, 0:w], WT[t % 2][:, i * P:(i + 1) * P], vt[:, kt, vcol:vcol + w],
                                               start=(i == 0), stop=(i == len(keys) - 1))
                    ins.then_inc(o.pv, 1)

                pe.wait_ge(o.yc, nt)
                for s in range(len(steps) + 1):
                    if s < len(steps):
                        kind, h, q, spans, keys = steps[s]
                        for c in range(2):
                            if s >= 1:
                                pe.wait_ge(o.ex[c], s)
                            b0 = HD * (c if kind == "B" else h)
                            tq, tk = (T_QB + h, T_KB + h) if kind == "B" else (T_QA + c, T_KA)
                            for sc0, k0, w, band in spans:
                                ins = nc.tensor.matmul(G[c][:, sc0:sc0 + w], pT[b0:b0 + HD, tq, q * P:(q + 1) * P],
                                                       pT[b0:b0 + HD, tk, k0:k0 + w], start=True, stop=band is None)
                                if band is not None:
                                    ins = nc.tensor.matmul(G[c][:, sc0:sc0 + w], ident, kc[:, band:band + w],
                                                           start=False, stop=True)
                            ins.then_inc(o.sc[c], 1)
                    if s >= 1:
                        for t in range(ends[s - 2] if s >= 2 else 0, ends[s - 1]):
                            _, c, _, _, _ = groups[t]
                            if steps[s - 1][0] == "B":
                                pe.wait_ge(o.wr, t + 1)
                            else:
                                pe.wait_ge(o.ex[c], s)
                            if t >= 1:
                                pe.wait_ge(o.te, t)
                            for i in range(len(steps[s - 1][4])):
                                ins = nc.tensor.transpose(X0[:, i * P:(i + 1) * P],
                                                          Pb[(s - 1) % 2][c][:, i * P:(i + 1) * P], ident)
                            ins.then_inc(o.tr, 1)
                            if t >= 1:
                                mix_values(t - 1)
                mix_values(len(groups) - 1)
                pe.wait_ge(o.gp, 7)
                for i, f in enumerate(FMT):
                    if i >= 2:
                        pe.wait_ge(o.ml, i - 1)
                    if i == 1:
                        pe.wait_ge(o.oe, len(groups))
                    for t in range(nt):
                        ins = nc.tensor.transpose((X0, X1)[i % 2][:, t * P:(t + 1) * P], mix[:, t, f * P:(f + 1) * P], ident)
                    ins.then_inc(o.mt, 1)
                segment(l, "out", hTv, (o.ml, 0), FMT)
                norm(2 * l + 1, nt)
                for hf in range(2):
                    segment(l, f"up{hf}", hTv, (hlo, 16 * l + 8) if hf == 0 else None)
                    segment(l, f"down{hf}", gTv, (glo, (2 * l + hf) * KH))
            norm(4, 4)


ROPED = ([(T_KA, HD)] + [(T_KB + h, HD) for h in range(4)] + [(T_KR, CQ)]
         + [(T_QA, HD), (T_QA + 1, HD)] + [(T_QB + h, HD) for h in range(4)] + [(T_QR, CQ)])
ATTN_SCALED = (T_QA, T_QA + 1, T_QB, T_QB + 1, T_QB + 2, T_QB + 3)
_F, _B = [4, 5, 0, 1, 2, 3], [5, 4, 3, 2, 1, 0]
STATE_CHAIN = []
for _i in range(5):
    STATE_CHAIN.append((0, _F[_i], _F[_i + 1], _F[_i] if _i else None))
    STATE_CHAIN.append((1, _B[_i], _B[_i + 1], _B[_i] if _i else None))


def kernel(**inputs):
    import numpy as _np
    import concourse.bacc as _bacc
    from concourse import mybir as _mybir
    from concourse.bass_utils import run_bass_kernel_spmd as _run

    a = {k: _np.asarray(v) for k, v in inputs.items()}
    cc = _np.concatenate
    xc = cc([a["x"][0], a["ctx"][0]], 0)
    xin = xc.T.reshape(8, 128, 768).transpose(1, 0, 2).reshape(128, -1)
    cin = _np.stack([a["c"][0], a["c_ctx"]], -1).reshape(8, 128, 2).transpose(1, 0, 2).reshape(128, -1)

    def unit(w, rows, cols):
        return w[rows][:, cols].reshape(-1, 128, 128).transpose(1, 0, 2).reshape(128, -1)

    A, dk = _np.arange, 64
    qa = cc([A(0, 64), A(128, 192), A(64, 128), A(192, 256)])
    cols = cc([A(256, 384), A(1024, 1536), A(2176, 2304), A(384, 512), A(1536, 2048), A(2304, 2560),
               A(2560, 2816), qa, A(512, 1024), A(2048, 2176)])
    k8, k11, wm, vin = [], [], [], []

    def row_unit(m):
        return a["w_mod"][m // MODS][:, 128 * (m % MODS):128 * (m % MODS) + 128].T

    for j in range(8):
        wm += [unit(a["w_mod"][0], slice(None), slice(128 * j, 128 * j + 128)), row_unit(8 + j)]
    wm += [row_unit(m) for m in range(16, 2 * MODS)]
    for l in range(LAYERS):
        full = slice(None)
        k8 += [unit(a["w_in"][l], full, cols[128 * t:128 * t + 128]) for t in range(N_IN)]
        k8 += [unit(a["w_out"][l], full, slice(128 * m, 128 * m + 128)) for m in range(8)]
        order = [s * 22 + j for j in range(22) for s in range(2)]
        k8 += [unit(a["w_up"][l], full, slice(128 * u, 128 * u + 128)) for u in order]
        for hf in range(2):
            rows = slice(KH * 128 * hf, KH * 128 * (hf + 1))
            k11 += [unit(a["w_down"][l], rows, slice(128 * m, 128 * m + 128)) for m in range(8)]

        def fm(v):
            return v.reshape(-1, 128).T

        conv = _np.stack([fm(a["conv_w"][l, 0]), fm(a["conv_w"][l, 1]), fm(a["conv_w"][l, 2]),
                          fm(a["conv_b"][l])], -1)[:, order].reshape(128, -1)
        z = a["ret_decay_logit"][l]
        vin += [_np.repeat(fm(a["b_mod"][l]), 2, 1), _np.repeat(fm(a["norm1_g"][l]), 2, 1),
                _np.repeat(fm(a["norm2_g"][l]), 2, 1), conv, a["diff_subln_g"][l][:, None],
                _np.broadcast_to(a["attn_sink"][l][None], (128, 4)),
                _np.broadcast_to(z.reshape(1, 8), (128, 8)), _np.repeat(z.T, 32, 0)]
    kin, rin = constants()
    cbin = _np.broadcast_to(cc([a["c"][0], a["c_ctx"]])[None], (128, 2048))
    arrays = {
        "x": xin, "c": cin, "cb": cbin, "wk8": _np.stack(k8), "wk11": _np.stack(k11), "wmod": _np.stack(wm),
        "vec": cc(vin, 1), "final_g": a["final_g"].reshape(8, 128).T,
        "lam": _np.broadcast_to(a["diff_lambda"].reshape(1, -1), (128, 512)), "consts": kin, "rope": rin,
    }
    arrays = {k: _np.ascontiguousarray(v) for k, v in arrays.items()}
    nc = _bacc.Bacc("TRN2", target_bir_lowering=False, num_devices=1)
    args = [nc.dram_tensor(f"in_{k}", v.shape, _mybir.dt.from_np(v.dtype), kind="ExternalInput").ap()
            for k, v in arrays.items()]
    args.append(nc.dram_tensor("out", (128, 8, 512), _mybir.dt.float32, kind="ExternalOutput").ap())
    trunk(nc, *args)
    r = _run(nc, [{f"in_{k}": v for k, v in arrays.items()}], core_ids=[0])
    return r.results[0]["out"].transpose(2, 1, 0).reshape(1, 512, 1024)
```

```python
from contextlib import ExitStack
import math

import numpy as np

import concourse.bass as bass
from concourse import mybir

F32 = mybir.dt.float32
F32R = mybir.dt.float32r
ACT = mybir.ActivationFunctionType
ALU = mybir.AluOpType
AXX = mybir.AxisListType.X

P = 128
D, KD8, LAT, CTX, LAYERS = 1024, 8, 512, 256, 2
TOK = LAT + CTX
EPS = 1e-6
GRID_W, ROPE_BASE = 64, 10000.0
FF, KH = 2816, 11
HD = 64
SCALE = HD ** -0.5
CQ = 32
T_KA, T_KB, T_KR, T_VA, T_GR, T_QA, T_QB, T_QR, N_IN = 0, 1, 5, 6, 13, 15, 17, 21, 22
N_KV = 13
V_A, V_B, V_C, V_G, V_W = 0, 128, 640, 896, 1152
SEGS = [("in_kv", N_KV, 8), ("in_q", N_IN - N_KV, 8), ("out", 8, 8),
        ("up0", 22, 8), ("down0", 8, KH), ("up1", 22, 8), ("down1", 8, KH)]
PER_LAYER = sum(n for _, n, _ in SEGS)
MODS = 48
BM, N1, N2, CW, SG, SK, DZ, VL = 0, 96, 112, 128, 304, 305, 309, 319
K_ID, K_S64, K_S32, K_ONE, K_BAND, K_BD, K_KJ, K_SC, K_W = 0, 128, 256, 384, 512, 896, 1152, 1154, 1163
R_C64, R_S64, R_C32, R_S32, R_C1, R_C2, R_DP, R_DN, R_MG, R_ML, R_W = (
    0, 512, 1024, 1536, 2048, 2176, 2304, 2432, 2560, 2688, 2816)


def constants():
    k = np.zeros((P, K_W), np.float32)
    i = np.arange(P)
    k[:, K_ID:K_ID + P] = np.eye(P)
    k[i, K_S64 + (i ^ 32)] = 1
    k[i, K_S32 + (i ^ 16)] = 1
    k[:, K_ONE:K_ONE + P] = 1
    k[:, K_BAND:K_BAND + P] = np.where(i[None] >= i[:, None], 0, -1e30)
    k[:, K_BAND + 2 * P:K_BAND + 3 * P] = np.where(i[None] <= i[:, None], 0, -1e30)
    k[:, K_BD:K_BD + 256] = (i[:, None] // CQ) == (np.arange(256)[None] // 64)
    k[:, K_KJ], k[:, K_KJ + 1] = P - 1 - i, i
    for t in range(N_KV, N_IN):
        k[:, K_SC + t - N_KV] = SCALE if t in ATTN_SCALED else 1
    r = np.zeros((P, R_W), np.float32)
    rows = np.repeat(np.arange(LAT // GRID_W, dtype=np.float32), GRID_W)
    cols = np.tile(np.arange(GRID_W, dtype=np.float32), LAT // GRID_W)
    for dim, c, s in ((HD, R_C64, R_S64), (CQ, R_C32, R_S32)):
        nf = dim // 4
        inv = (np.float32(ROPE_BASE) ** (-np.arange(nf, dtype=np.float32) / np.float32(nf))).astype(np.float32)
        ang = np.concatenate([rows[:, None] * inv, cols[:, None] * inv], -1).T.astype(np.float32)
        f = i % (dim // 2)
        r[:, c:c + LAT] = np.cos(ang)[f]
        r[:, s:s + LAT] = np.where((i % dim < dim // 2)[:, None], -np.sin(ang)[f], np.sin(ang)[f])
    r[:, R_C1:R_C1 + P] = i[None] + 1
    r[:, R_C2:R_C2 + P] = P - i[None]
    d = i[None] - i[:, None]
    r[:, R_DP:R_DP + P] = np.maximum(d, 0)
    r[:, R_DN:R_DN + P] = np.maximum(-d, 0)
    r[:, R_MG:R_MG + P] = (d >= 0) * np.float32(CQ ** -0.5)
    r[:, R_ML:R_ML + P] = (d < 0) * np.float32(CQ ** -0.5)
    return k, r


def attention_steps(l):
    long, short = [], []
    for h in range(4):
        long += [("B", h, q, [(0, 0, LAT, None), (LAT, LAT, CTX, None)], [0, 1, 2, 3, 4, 5]) for q in range(4)]
        if l == 0:
            short += [("B", h, q, [(0, LAT, CTX, None)], [4, 5]) for q in (4, 5)]
    for g in range(2):
        for q in range(4):
            near = list(range(max(0, q - 1), min(3, q + 1) + 1))
            spans = [(0, LAT, CTX, None)]
            for i, kt in enumerate(near):
                spans.append((CTX + i * P, kt * P, P, None if kt == q else K_BAND + (kt - q + 1) * P))
            short.append(("A", g, q, spans, [4, 5] + near))
    if l == 0:
        short += [("A", g, q, [(0, LAT, CTX, None)], [4, 5]) for g in range(2) for q in (4, 5)]
    steps, late = [], 4 if l == 0 else 3
    mixed = short[:-late]
    for i, step in enumerate(long):
        steps.append(step)
        while mixed and (len(short) - late - len(mixed) + 1) * len(long) <= (i + 1) * (len(short) - late):
            steps.append(mixed.pop(0))
    return steps + short[-late:]


def turn_groups(steps):
    groups, ends = [], []
    for s, (kind, h, *_) in enumerate(steps):
        if kind == "B":
            groups.append((s, 0, V_B + P * h, P, 256 + P * h))
        else:
            groups += [(s, c, V_A + HD * h, HD, HD * (2 * h + c)) for c in range(2)]
        ends.append(len(groups))
    return groups, ends


def trunk(nc, xin, cin, cbin, wk8, wk11, wmod, vin, finalg, lamin, kin, rin, out):
    base, seg_at, n, a8, a11 = {}, {}, 0, 0, 0
    for l in range(LAYERS):
        for name, cnt, k in SEGS:
            seg_at[l, name] = (n, cnt, k, a8 if k == 8 else a11)
            n += cnt
            if k == 8:
                a8 += cnt
            else:
                a11 += cnt
    seg_end = {key: v[0] + v[1] for key, v in seg_at.items()}

    def groups_of(l, name):
        return [(0, LAT), (LAT, TOK)] if l == 0 or name == "in_kv" else [(0, LAT)]

    def in_sbuf(l, t):
        return seg_at[l, "in_kv"][0] + t + 1

    def tiles_of(l):
        return 6 if l == 0 else 4

    stack = ExitStack()
    with stack:
        def sb(name, cols, dt=F32, rows=P):
            return stack.enter_context(nc.sbuf_tensor(name, [rows, cols], dt))

        xT = sb("xT", KD8 * TOK)[:, :].rearrange("p (k t) -> p k t", k=KD8)
        with ExitStack() as own:
            hT = own.enter_context(nc.sbuf_tensor("hT", [P, 2 * KD8 * TOK], F32R))
        with ExitStack() as own:
            vtok = own.enter_context(nc.sbuf_tensor("vtok", [P, 6 * V_W], F32))
            hm = own.enter_context(nc.sbuf_tensor("attn_scratch", [P, 2 * KD8 * TOK - 6 * V_W], F32))
        hold = sb("hT_bytes", 2 * KD8 * TOK)
        with ExitStack() as own:
            gT = own.enter_context(nc.sbuf_tensor("gT", [P, 2 * KH * TOK], F32R))
        pTt = sb("pT", N_IN * TOK)
        raw = [sb(f"raw{j}", KH * P) for j in range(2)]
        wsp = [sb(f"wsplit{j}", 2 * KH * P, F32R) for j in range(2)]
        tm = sb("tmp", 2 * TOK + 2 * D)
        mraw = [sb(f"modraw{j}", KD8 * P) for j in range(2)]
        kc = sb("consts", K_W)
        vec = sb("vec", LAYERS * VL)
        fing = sb("fing", KD8)
        cs = sb("c_in", 16)
        csil = sb("c_silu", 16)
        modv = sb("modv", 2 * 96)
        msum = sb("mod_sums", 2 * 96)
        Amul = sb("Amul", 64)
        qdec = sb("qdec", 256)
        mdec = sb("mdec", 512)
        kdec = sb("kdec", 8)
        gch = sb("gch", 2)
        lg = sb("lg", 20)
        sm = sb("small", 4 * 72)
        nsink = sb("minus_sink", 8)
        nlam = sb("nlam", 2)
        fsc = sb("fsc", 8)
        rsd = sb("rsd", 16)
        ssb = sb("ssb", 24)
        cst = sb("cstat", 96)
        half = sb("minus_half", 24)
        dummy = sb("warm", 5)
        eps = sb("eps", 1)
        G = [stack.enter_context(nc.psum_tensor(f"G{j}", [P, 1024], F32)) for j in range(2)]
        X0 = stack.enter_context(nc.psum_tensor("X0", [P, 1024], F32))
        X1 = stack.enter_context(nc.psum_tensor("X1", [P, 1024], F32))
        hTv = hT[:, :].rearrange("p (s k t) -> p s k t", s=2, k=KD8)
        gTv = gT[:, :].rearrange("p (s k t) -> p s k t", s=2, k=KH)
        pT = pTt[:, :].rearrange("p (k t) -> p k t", k=N_IN)
        mix = pTt[:, T_VA * TOK:T_VA * TOK + 6 * D].rearrange("p (t f) -> p t f", t=6)
        ysb = mix[:, :, 768:1024].rearrange("p n (h e) -> p n h e", h=4)
        ysq = tm[:, 0:1536].rearrange("p (n h e) -> p n h e", n=6, h=4)
        vt = vtok[:, :].rearrange("p (t f) -> p t f", t=6)
        Pb = [[hm[:, (2 * p + c) * TOK:(2 * p + c + 1) * TOK] for c in range(2)] for p in range(2)]
        WT = [hm[:, (4 + p) * TOK:(5 + p) * TOK] for p in range(2)]
        ropeA = [mraw[0][:, j * LAT:(j + 1) * LAT] for j in range(2)]
        ropeB = [mraw[1][:, j * LAT:(j + 1) * LAT] for j in range(2)]
        dback = tm[:, R_W:R_W + 512]
        states = hm[:, 0:3072].rearrange("p (d n e) -> p d n e", d=2, n=6)
        kdk = hm[:, 3072:4608].rearrange("p (d n e) -> p d n e", d=2, n=6)
        Wv = [[wsp[j][:, s * KH * P:(s + 1) * KH * P].rearrange("p (k m) -> p k m", k=KH) for s in range(2)]
              for j in range(2)]
        first_mod = pTt[:, 0:16 * D].rearrange("p (m c) -> p m c", m=16)
        cb = tm[:, 2 * TOK:2 * TOK + 2 * D].rearrange("p (c k) -> p c k", c=2)
        sq, sacc = tm[:, 0:TOK], tm[:, TOK:2 * TOK]
        msv = msum[:, :].rearrange("p (m c) -> p m c", c=2)
        csv = csil[:, :].rearrange("p (k c) -> p k c", k=KD8)
        mvl = [modv[:, 96 * l:96 * l + 96].rearrange("p (m c) -> p m c", c=2) for l in range(LAYERS)]
        Avl = [Amul[:, 32 * l:32 * l + 32].rearrange("p (w k c) -> p w k c", w=2, k=KD8) for l in range(LAYERS)]
        rope = tm[:, 0:R_W]
        ident, ones = kc[:, K_ID:K_ID + P], kc[:, K_ONE:K_ONE + P]
        dg = pTt[:, (N_IN - 1) * TOK:N_IN * TOK]
        dg3 = pTt[:, (N_IN - 2) * TOK:(N_IN - 1) * TOK]
        NB, LS, RC, ES = (sm[:, 72 * j:72 * j + 72] for j in range(4))

        def slot(k):
            return (tm[:, 0:TOK], tm[:, TOK:2 * TOK], dg3)[k % 3]

        def lo_done(ni, k):
            if k in POOL_LO:
                return plo, len(POOL_LO) * ni + POOL_LO.index(k) + 1
            mine = [j for j in range(KD8) if j not in POOL_LO]
            return hlo, len(mine) * ni + mine.index(k) + 1

        diags = [0, 2, 4, 6, 7]

        def value_bank(i):
            return G[i] if i < 2 else (X1, G[0])[i % 2]

        order = [(l, name) for l in range(LAYERS) for name, _, _ in SEGS]
        FMT = [6, 7, 2, 3, 4, 5, 0, 1]

        def vecs(l, a, w):
            return vec[:, l * VL + a:l * VL + a + w]

        def sem(name):
            return stack.enter_context(nc.semaphore(name))

        c_landed, v_landed, x_landed = sem("c_landed"), sem("vectors_landed"), sem("x_landed")
        ropeld = sem("rope_tables_loaded")
        w_landed = [sem(f"weights_landed{j}") for j in range(2)]
        w_hi, w_lo = sem("weights_hi"), sem("weights_lo")
        used = sem("unit_multiplied")
        ev = sem("unit_evacuated")
        m_landed = [sem(f"mod_landed{j}") for j in range(2)]
        m_first = [sem(f"first_mod_landed{j}") for j in range(8)]
        m_used = sem("mod_unit_multiplied")
        m_pe, m_dv = sem("first_shift_multiplied"), sem("first_scale_multiplied")
        c_ready = sem("c_silu_ready")
        cb_ready = sem("c_silu_spread")
        cb_landed = sem("c_spread_landed")
        c_spread = sem("c_silu_on_partitions")
        k_landed = sem("constants_landed")
        modok = sem("modulation_ready")
        sqd, sqa, ssd, srt, dgd, rbd = (sem(x) for x in (
            "squares_ready", "squares_added", "sums_ready", "roots_ready", "diag_ready", "rstd_spread"))
        vsd, hid, hlo = sem("scaled_ready"), sem("operand_hi"), sem("operand_lo")
        plo, full = sem("operand_lo_pool"), sem("operand_full")
        accr = sem("conv_centre_ready")
        convl = sem("conv_left_added")
        silud, prodd, ghi, glo = sem("gate_silu"), sem("gated"), sem("gated_hi"), sem("gated_lo")
        dv = sem("vector_chain")
        tabs_a = sem("table_exps")
        start_a = sem("start_act")
        start_v = sem("start_vec")
        stored = sem("stored")
        fin = sem("final_rows")

        class Layer:
            pass
        L = []
        for l in range(LAYERS):
            o = Layer()
            o.rot, o.rsin, o.rcos, o.rdone = (sem(f"{x}{l}") for x in ("rot", "rope_sin", "rope_cos", "roped"))
            o.vt, o.vc = sem(f"values_turned{l}"), sem(f"values_copied{l}")
            o.tab = sem(f"tables{l}")
            o.sc = [sem(f"scores{c}_{l}") for c in range(2)]
            o.nb = [sem(f"negmax{c}_{l}") for c in range(2)]
            o.ex = [sem(f"exp{c}_{l}") for c in range(2)]
            o.es = [sem(f"sink_exp{c}_{l}") for c in range(2)]
            o.wr, o.tr, o.te, o.pv, o.oe = (sem(f"{x}{l}") for x in (
                "probs_ready", "probs_turned", "turned_copied", "values_mixed", "mixed_copied"))
            o.kt, o.kd, o.kv, o.st = (sem(f"{x}{l}") for x in ("k_turned", "k_decayed", "kv_ready", "state_ready"))
            o.qd, o.at, o.ad, o.y, o.yc = (sem(f"{x}{l}") for x in (
                "q_decayed", "ret_scores", "ret_decayed", "ret_out", "ret_copied"))
            o.gp, o.gd = sem(f"group_pool{l}"), sem(f"group_vec{l}")
            o.mt, o.mh, o.ml = (sem(f"{x}{l}") for x in ("mixed_turned", "mixed_hi", "mixed_lo"))
            L.append(o)

        def unit_loop(eng, l, name, body, head=0, tail=0):
            cnt = seg_at[l, name][1]
            tail += (cnt - head - tail) % 2
            for r in range(head):
                body(r, 0)
            if cnt - head - tail:
                with eng.Fori(0, (cnt - head - tail) // 2) as i:
                    body(head, i)
                    body(head + 1, i)
            for r in range(cnt - tail, cnt):
                body(r, 0)

        def flat(ap):
            return ap.rearrange("p a t -> p (a t)")

        block = stack.enter_context(nc.Block())

        @block.sync
        def _(sp):
            def weights(l, name, between=None):
                n0, cnt, k, a0 = seg_at[l, name]
                src = wk8 if k == 8 else wk11

                def load(r, i):
                    n = n0 + r
                    if n >= 2:
                        sp.wait_ge(w_lo, 2 * i + (n - 1))
                    row = src[a0 + r] if isinstance(i, int) else flat(
                        src[bass.ds(2 * i + (a0 + r), 1)].rearrange("o p c -> p o c"))
                    sp.dma_start(raw[n % 2][:, 0:k * P], row).then_inc(w_landed[n % 2], 16)
                    if between and r == 1 and isinstance(i, int):
                        between()
                unit_loop(sp, l, name, load, head=2 if between else 0)

            def mod(m, i=0):
                if m >= 2:
                    sp.wait_ge(m_used, 2 * i + (m - 1))
                row = wmod[m + 16] if isinstance(i, int) else flat(
                    wmod[bass.ds(2 * i + (m + 16), 1)].rearrange("o p c -> p o c"))
                sp.dma_start(mraw[m % 2][:, :], row).then_inc(m_landed[m % 2], 16)

            sp.dma_start(cs[:, :], cin).then_inc(c_landed, 16)
            sp.dma_start(ident, kin[:, K_ID:K_ID + P]).then_inc(c_landed, 16)
            for j in range(8):
                sp.dma_start(first_mod[:, 2 * j:2 * j + 2, :],
                             wmod[2 * j:2 * j + 2].rearrange("m p c -> p m c")).then_inc(m_first[j], 16)
                if j == 0:
                    sp.dma_start(flat(xT), xin).then_inc(x_landed, 16)
                    sp.dma_start(vec[:, :], vin).then_inc(v_landed, 16)
                    sp.dma_start(fing[:, :], finalg).then_inc(v_landed, 16)
                    sp.dma_start(mraw[0][:, 0:512], lamin).then_inc(v_landed, 16)
            sp.dma_start(kc[:, P:K_W], kin[:, P:K_W]).then_inc(k_landed, 16)
            for l in range(LAYERS):
                n0, cnt, _, a0 = seg_at[l, "in_kv"]
                if l == 0:
                    for r in range(4):
                        if r == 2:
                            sp.wait_ge(start_v, 3)
                            mod(0)
                            mod(1)
                        if r >= 2:
                            sp.wait_ge(w_lo, r - 1)
                        sp.dma_start(raw[r % 2][:, 0:KD8 * P], wk8[a0 + r]).then_inc(w_landed[r % 2], 16)
                    mod(2)
                    mod(3)
                    with sp.Fori(0, (cnt - 5) // 2) as i:
                        for j in range(2):
                            sp.wait_ge(w_lo, 2 * i + (j + 3))
                            sp.dma_start(raw[j][:, 0:KD8 * P], flat(
                                wk8[bass.ds(2 * i + (a0 + 4 + j), 1)].rearrange("o p c -> p o c"))
                            ).then_inc(w_landed[j], 16)
                            for m in range(3 * j, 3 * j + 3):
                                sp.wait_ge(m_used, 6 * i + (m + 3))
                                sp.dma_start(mraw[m % 2][:, :], flat(
                                    wmod[bass.ds(6 * i + (m + 20), 1)].rearrange("o p c -> p o c"))
                                ).then_inc(m_landed[m % 2], 16)
                    sp.wait_ge(w_lo, cnt - 2)
                    sp.dma_start(raw[(cnt - 1) % 2][:, 0:KD8 * P], wk8[a0 + cnt - 1]).then_inc(
                        w_landed[(cnt - 1) % 2], 16)
                else:
                    weights(l, "in_kv")
                n0, cnt, _, a0 = seg_at[l, "in_q"]
                for r in range(cnt):
                    n = n0 + r
                    if r == (6 if l == 0 else 0):
                        if l == 0:
                            sp.wait_ge(m_used, 36)
                        for k in (POOL_LO[-1], KD8 - 1):
                            sp.wait_ge(*lo_done(2 * l, k))
                        sp.dma_start(rope, rin).then_inc(ropeld, 16)
                    sp.wait_ge(w_lo, n - 1)
                    sp.dma_start(raw[n % 2][:, 0:KD8 * P], wk8[a0 + r]).then_inc(w_landed[n % 2], 16)
                    if l == 0 and r < 4:
                        mod(28 + 2 * r)
                        mod(29 + 2 * r)
                weights(l, "out")
                for hf in range(2):
                    if l == 0:
                        if hf == 0:
                            sp.wait_ge(L[0].ml, 8)
                            sp.dma_start(cb[:, :, :].rearrange("p c k -> p (c k)"), cbin).then_inc(cb_landed, 16)
                        n0, cnt, _, a0 = seg_at[l, f"up{hf}"]

                        def pair_loads(i):
                            for j in range(2):
                                sp.wait_ge(w_lo, 2 * i + (n0 + j - 1))
                                sp.dma_start(raw[(n0 + j) % 2][:, 0:KD8 * P], flat(
                                    wk8[bass.ds(2 * i + (a0 + j), 1)].rearrange("o p c -> p o c"))
                                ).then_inc(w_landed[(n0 + j) % 2], 16)

                        pair_loads(0)
                        with sp.Fori(0, cnt // 2 - 1) as i:
                            pair_loads(i + 1)
                            for j in range(2):
                                mod(36 + cnt * hf + j, i)

                        def last_mods():
                            for m in range(cnt - 2, cnt):
                                mod(36 + cnt * hf + m)
                    else:
                        weights(l, f"up{hf}")
                    weights(l, f"down{hf}", last_mods if l == 0 else None)
            for k in range(KD8):
                sp.wait_ge(fin, k + 1)
                sp.dma_start(out[:, k, :], pT[:, 8 + k, 0:LAT]).then_inc(stored, 16)
            sp.wait_ge(stored, 16 * KD8)

        @block.gpsimd
        def _(pool):
            def residue(l, name, r, i):
                n0, cnt, k, _ = seg_at[l, name]
                j = (n0 + r) % 2
                pool.wait_ge(w_hi, 2 * i + (n0 + r + 1))
                nc.gpsimd.tensor_tensor(wsp[j][:, KH * P:KH * P + k * P], raw[j][:, 0:k * P],
                                        wsp[j][:, 0:k * P].bitcast(F32), ALU.subtract).then_inc(w_lo, 1)

            def residues(l, name, ni=None):
                def body(r, i):
                    residue(l, name, r, i)
                    if ni is not None and r == 1 and isinstance(i, int):
                        width = groups_of(l, name)[-1][1]
                        for k in POOL_LO:
                            pool.wait_ge(hid, 8 * ni + k + 1)
                            nc.gpsimd.tensor_tensor(hTv[:, 1, k, 0:width], slot(k)[:, 0:width],
                                                    hTv[:, 0, k, 0:width].bitcast(F32), ALU.subtract).then_inc(plo, 1)
                unit_loop(pool, l, name, body, head=2 if ni is not None else 0)

            for k in range(1, 7):
                pool.wait_ge(sqd, k + 1)
                if k > 1:
                    pool.wait_ge(sqa, k - 1)
                nc.gpsimd.tensor_tensor(sacc, sacc, sq, ALU.add).then_inc(sqa, 1)
            for l in range(LAYERS):
                o = L[l]
                residues(l, "in_kv", 2 * l)
                def rotate(i):
                    t, w = ROPED[i]
                    pool.wait_ge(ev, in_sbuf(l, t))
                    pool.wait_ge(ropeld, 16 * (l + 1))
                    if i >= 2:
                        pool.wait_ge(o.rdone, i - 1)
                    c = R_C64 if w == HD else R_C32
                    nc.gpsimd.tensor_tensor(ropeB[i % 2], pT[:, t, 0:LAT], rope[:, c:c + LAT],
                                            ALU.mult).then_inc(o.rcos, 1)
                for r in range(N_IN - N_KV):
                    residue(l, "in_q", r, 0)
                    for i in ROTARY_AT[l].get(r - 1, []):
                        rotate(i)
                for i in ROTARY_AT[l][8]:
                    rotate(i)
                nt = tiles_of(l)
                pool.wait_ge(o.rdone, len(ROPED))
                pool.wait_ge(o.tab, 1)
                for j in range(nt):
                    if j >= 2:
                        pool.wait_ge(o.at, j - 1)
                    qj = pT[:, T_QR, j * P:(j + 1) * P]
                    nc.gpsimd.tensor_tensor(
                        tm[:, 2048 + 512 * (j % 2):2560 + 512 * (j % 2)].rearrange("p (h c) -> p h c", h=4),
                        qj.unsqueeze(1).to_broadcast([P, 4, P]),
                        kc[:, K_BD:K_BD + 256:64].unsqueeze(2).to_broadcast([P, 4, P]),
                        ALU.mult).then_inc(o.qd, 1)
                    if j >= 2:
                        pool.wait_ge(o.y, j - 1)
                    for d in range(2):
                        nc.gpsimd.tensor_tensor(tm[:, 512 + 256 * (j % 2) + P * d:][:, 0:P], qj,
                                                qdec[:, d * P:(d + 1) * P], ALU.mult).then_inc(o.qd, 1)
                yg = ysb[:, 0:nt]

                def spread(c0, w):
                    return cst[:, c0:c0 + 4 * nt].rearrange("p (n h) -> p n h", h=4).unsqueeze(3).to_broadcast(
                        [P, nt, 4, w])

                pool.wait_ge(o.gd, 1)
                nc.gpsimd.tensor_tensor(yg, yg, spread(48, 64), ALU.subtract).then_inc(o.gp, 1)
                pool.wait_ge(o.gp, 1)
                nc.gpsimd.tensor_tensor(ysq[:, 0:nt], yg, yg, ALU.mult).then_inc(o.gp, 1)
                pool.wait_ge(o.gd, 2)
                nc.gpsimd.tensor_tensor(cst[:, 24:24 + 4 * nt], cst[:, 72:72 + 4 * nt], half[:, 0:4 * nt],
                                        ALU.pow).then_inc(o.gp, 1)
                pool.wait_ge(o.gp, 3)
                nc.gpsimd.tensor_tensor(yg, yg, spread(24, 64), ALU.mult).then_inc(o.gp, 1)
                pool.wait_ge(o.gp, 4)
                nc.gpsimd.tensor_tensor(mix[:, 0:nt, 768:1024], mix[:, 0:nt, 768:1024], vt[:, 0:nt, V_G:V_G + 256],
                                        ALU.mult).then_inc(o.gp, 1)
                pool.wait_ge(o.gd, 3)
                nc.gpsimd.tensor_tensor(cst[:, 0:4 * nt], ssb[:, 0:4 * nt], half[:, 0:4 * nt],
                                        ALU.pow).then_inc(o.gp, 1)
                pool.wait_ge(o.gp, 6)
                mb = mix[:, 0:nt, 256:768].rearrange("p n (h e) -> p n h e", h=4)
                nc.gpsimd.tensor_tensor(mb, mb, spread(0, P), ALU.mult).then_inc(o.gp, 1)
                for name in ("out", "up0", "down0", "up1", "down1"):
                    residues(l, name, 2 * l + 1 if name == "up0" else None)

        @block.scalar
        def _(act):
            def split_hi(l, name, r, i=0):
                n0, cnt, k, _ = seg_at[l, name]
                if isinstance(i, int) and r >= cnt:
                    nxt = order[order.index((l, name)) + 1:][:1]
                    if nxt:
                        split_hi(*nxt[0], r - cnt)
                    return
                n = n0 + r
                act.wait_ge(w_landed[n % 2], 16 * i + 16 * (n // 2 + 1))
                if n >= 2:
                    act.wait_ge(used, 2 * i + (n - 1))
                nc.scalar.activation(wsp[n % 2][:, 0:k * P], raw[n % 2][:, 0:k * P], ACT.Copy).then_inc(w_hi, 1)

            def splits_only(l, name):
                unit_loop(act, l, name, lambda r, i: split_hi(l, name, r + 2, i), tail=2)

            def square(ni, k, width, kk=None):
                if isinstance(k, int) and k == 0:
                    nc.scalar.activation(sacc[:, 0:width], xT[:, 0, 0:width], ACT.Square).then_inc(sqd, 1)
                    return
                if not (isinstance(k, int) and k == 1):
                    act.wait_ge(sqa, 6 * ni + k - 1)
                nc.scalar.activation(sq[:, 0:width], flat(xT[:, bass.ds(k, 1), 0:width]), ACT.Square).then_inc(sqd, 1)

            def squares(l, name, ni, width):
                n0 = seg_at[l, name][0]

                def body(r, i):
                    act.wait_ge(used, 2 * i + (n0 + r + 1))
                    split_hi(l, name, r + 2, i)
                    act.wait_ge(ev, 2 * i + (n0 + r + 1))
                    square(ni, r if isinstance(i, int) else 2 * i + r, width)
                unit_loop(act, l, name, body, head=2, tail=2)

            def root(ni, nt):
                nc.scalar.activation(dummy[:, ni:ni + 1], eps[:, :], ACT.Sqrt)
                act.wait_ge(ssd, ni + 1)
                nc.scalar.activation(rsd[:, 0:nt], X1[:, 0:nt], ACT.Sqrt, bias=eps[:, 0:1],
                                     scale=1.0 / D).then_inc(srt, 1)

            def operand(ni, w, gr):
                width = gr[-1][1]
                for k in range(KD8):
                    act.wait_ge(vsd, 8 * ni + k + 1)
                    mine = k in POOL_LO
                    for g, (a, b) in enumerate(gr):
                        ins = nc.scalar.activation(slot(k)[:, a:b] if mine else hTv[:, 0, k, a:b], slot(k)[:, a:b],
                                                   ACT.Identity, bias=mvl[ni // 2][:, 24 * w + k, g:g + 1])
                    if mine:
                        ins.then_inc(full, 1)
                        act.wait_ge(full, len(POOL_LO) * ni + POOL_LO.index(k) + 1)
                        ins = nc.scalar.activation(hTv[:, 0, k, 0:width], slot(k)[:, 0:width], ACT.Copy)
                    ins.then_inc(hid, 1)

            act.wait_ge(c_landed, 32)
            nc.scalar.activation(csil[:, :], cs[:, :], ACT.Silu).then_inc(c_ready, 1)
            for c in range(2):
                act.wait_ge(c_spread, c + 1)
                nc.scalar.activation(cb[:, c, :], (X0, X1)[c][:, :], ACT.Copy).then_inc(cb_ready, 1)
            act.wait_ge(x_landed, 16)
            for k in range(KD8):
                square(0, k, TOK)
            act.wait_ge(start_v, 3)
            nc.scalar.activation(cst[:, 20:40], cst[:, 0:20], ACT.Exp, scale=-1.0).then_inc(start_a, 1)
            nc.scalar.activation(cst[:, 44:48], cst[:, 40:44], ACT.Exp).then_inc(start_a, 1)
            act.wait_ge(start_v, 4)
            nc.scalar.activation(cst[:, 50:70], cst[:, 70:90], ACT.Ln).then_inc(start_a, 1)
            for l in range(LAYERS):
                o = L[l]
                root(2 * l, 6)
                if l == 0:
                    split_hi(0, "in_kv", 0)
                    split_hi(0, "in_kv", 1)
                operand(2 * l, 0, [(0, LAT), (LAT, TOK)])
                def project(name, r, i):
                    n0 = seg_at[l, name][0]
                    width = groups_of(l, name)[-1][1]
                    t0 = 0 if name == "in_kv" else N_KV
                    act.wait_ge(used, 2 * i + (n0 + r + 1))
                    nc.scalar.activation(flat(pT[:, bass.ds(2 * i + (t0 + r), 1), 0:width]),
                                         G[(n0 + r) % 2][:, 0:width], ACT.Copy,
                                         scale=kc[:, K_SC + r:K_SC + r + 1] if t0 else 1.0).then_inc(ev, 1)
                    split_hi(l, name, r + 2, i)

                unit_loop(act, l, "in_kv", lambda r, i: project("in_kv", r, i), tail=2)
                for r in range(N_IN - N_KV):
                    project("in_q", r, 0)
                    if r == (6 if l == 0 else 3):
                        act.wait_ge(ropeld, 16 * (l + 1))
                        for d, c in ((0, R_C1), (1, R_C2)):
                            nc.scalar.activation(qdec[:, d * P:(d + 1) * P], rope[:, c:c + P], ACT.Exp,
                                                 scale=lg[:, 10 * l + 8 + d:10 * l + 9 + d]).then_inc(tabs_a, 1)
                            nc.scalar.activation(kdec[:, 4 * d:4 * d + 4], lg[:, 10 * l + 4 * d:10 * l + 4 * d + 4],
                                                 ACT.Exp, scale=kc[:, K_KJ + d:K_KJ + d + 1]).then_inc(tabs_a, 1)
                        nc.scalar.activation(gch[:, :], lg[:, 10 * l + 8:10 * l + 10], ACT.Exp,
                                             scale=float(P)).then_inc(tabs_a, 1)
                        for h in range(4):
                            for dst, d, c in ((mdec, 0, R_DP), (dback, 1, R_DN)):
                                nc.scalar.activation(dst[:, h * P:(h + 1) * P], rope[:, c:c + P], ACT.Exp,
                                                     scale=lg[:, 10 * l + 4 * d + h:][:, 0:1]).then_inc(tabs_a, 1)
                act.wait_ge(used, seg_end[l, "in_q"])
                for i, v in enumerate(VALUE_ORDER):
                    nt = 6 if v < 7 else tiles_of(l)
                    act.wait_ge(o.vt, i + 1)
                    nc.scalar.activation(vt[:, 0:nt, v * P:(v + 1) * P],
                                         value_bank(i)[:, 0:nt * P].rearrange("p (t c) -> p t c", t=nt),
                                         ACT.Copy if v < 7 else ACT.Silu).then_inc(o.vc, 1)
                nt = tiles_of(l)
                for j in range(nt):
                    act.wait_ge(o.y, j + 1)
                    nc.scalar.activation(mix[:, j, 768:1024], G[1][:, 512 * (j % 2):512 * (j % 2) + 256],
                                         ACT.Copy).then_inc(o.yc, 1)
                steps = attention_steps(l)
                groups, ends = turn_groups(steps)

                def copy_turned(t):
                    nk = P * len(steps[groups[t][0]][4])
                    act.wait_ge(o.tr, t + 1)
                    if t >= 2:
                        act.wait_ge(o.pv, t - 1)
                    nc.scalar.activation(WT[t % 2][:, 0:nk], X0[:, 0:nk], ACT.Copy).then_inc(o.te, 1)

                def copy_out(t):
                    s, c, _, w, col = groups[t]
                    kind, h, q = steps[s][:3]
                    act.wait_ge(o.pv, t + 1)
                    act.wait_ge(o.wr, ends[s])
                    inv = RC[:, 2 * s + c:2 * s + c + 1]
                    b = 512 * (t % 2)
                    first = nc.scalar.activation(mix[:, q, col:col + w], X1[:, b:b + w], ACT.Copy, scale=inv)
                    if kind == "B":
                        if t:
                            act.wait_ge(o.oe, t)
                        first = nc.scalar.activation(tm[:, 2944:2944 + P], X1[:, b:b + P], ACT.Square,
                                                     scale=inv, accum_out=ssb[:, 4 * q + h:4 * q + h + 1])
                    first.then_inc(o.oe, 1)

                for s in range(len(steps) + 1):
                    if s < len(steps):
                        kind, h, q, spans, keys = steps[s]
                        p, nk = s % 2, P * len(keys)
                        if s >= 2:
                            act.wait_ge(o.tr, ends[s - 2])
                        for c in range(2):
                            m = 2 * s + c
                            if c == 1 and s >= 1 and steps[s - 1][0] == "A":
                                copy_turned(ends[s - 1] - 2)
                            act.wait_ge(o.nb[c], s + 1)
                            nc.scalar.activation(Pb[p][c][:, 0:nk], G[c][:, 0:nk], ACT.Exp, bias=NB[:, m:m + 1],
                                                 accum_out=LS[:, m:m + 1]).then_inc(o.ex[c], 1)
                            if kind == "A":
                                nc.scalar.activation(ES[:, m:m + 1], vecs(l, SK + 2 * h + c, 1), ACT.Exp,
                                                     bias=NB[:, m:m + 1]).then_inc(o.es[c], 1)
                    if s >= 1:
                        for t in range(ends[s - 2] if s >= 2 else 0, ends[s - 1]):
                            if s == len(steps) or steps[s - 1][0] == "B" or t == ends[s - 1] - 1:
                                copy_turned(t)
                            if t >= 1:
                                copy_out(t - 1)
                copy_out(len(groups) - 1)
                for i, f in enumerate(FMT):
                    act.wait_ge(o.mt, i + 1)
                    nc.scalar.activation(hTv[:, 0, f, 0:nt * P], (X0, X1)[i % 2][:, 0:nt * P], ACT.Copy,
                                         scale=fsc[:, f:f + 1]).then_inc(o.mh, 1)
                width = TOK if l == 0 else LAT
                squares(l, "out", 2 * l + 1, width)
                root(2 * l + 1, nt)
                if l == 0:
                    act.wait_ge(cb_landed, 16)
                    nc.scalar.activation(cb[:, :, :], cb[:, :, :], ACT.Silu).then_inc(cb_ready, 1)
                operand(2 * l + 1, 1, groups_of(l, "up0"))
                accs = (tm[:, 0:TOK], tm[:, TOK:2 * TOK])
                for hf in range(2):
                    name, down = f"up{hf}", f"down{hf}"
                    n0, cnt, _, _ = seg_at[l, name]
                    g0 = (2 * l + hf) * KH

                    def pair(r, i):
                        for j in range(2):
                            act.wait_ge(used, 2 * i + (n0 + r + j + 1))
                            pr = g0 + r // 2
                            if pr:
                                act.wait_ge(glo if j == 0 else prodd, i + pr)
                            cw = vecs(l, CW, 176).rearrange("p (u w) -> p u w", w=4)[
                                :, bass.ds(2 * i + (hf * 22 + r + j), 1), :].rearrange("p a w -> p (a w)")
                            nc.scalar.activation(accs[j][:, 0:width], G[(n0 + r + j) % 2][:, 0:width], ACT.Identity,
                                                 bias=cw[:, 3:4], scale=cw[:, 1:2]).then_inc(accr, 1)
                            split_hi(l, name, r + j + 2, i)
                        act.wait_ge(ev, 2 * i + (n0 + r + 2))
                        nc.scalar.activation(accs[1][:, 0:width], accs[1][:, 0:width], ACT.Silu).then_inc(silud, 1)
                        act.wait_ge(prodd, i + (g0 + r // 2 + 1))
                        nc.scalar.activation(flat(gTv[:, 0, bass.ds(i + r // 2, 1), 0:width]), accs[0][:, 0:width],
                                             ACT.Copy).then_inc(ghi, 1)
                    pair(0, 0)
                    with act.Fori(0, KH - 2) as i:
                        pair(2, i)
                    pair(cnt - 2, 0)
                    if hf == 0:
                        splits_only(l, down)
                    else:
                        act.wait_ge(glo, (2 * l + 2) * KH)
                        squares(l, down, 2 * l + 2, TOK if l == 0 else LAT)
            root(4, 4)

        @block.vector
        def _(dve):
            chain = [0]

            def link(ins):
                chain[0] += 1
                ins.then_inc(dv, 1)
                dve.wait_ge(dv, chain[0])

            def add_square(ni, k, width):
                dve.wait_ge(sqd, 8 * ni + k + 1)
                if isinstance(k, int) and k > 1 or not isinstance(k, int):
                    dve.wait_ge(sqa, 6 * ni + k - 1)
                nc.vector.tensor_tensor(sacc[:, 0:width], sacc[:, 0:width], sq[:, 0:width], ALU.add).then_inc(sqa, 1)

            def norm(ni, nt):
                dve.wait_ge(srt, ni + 1)
                link(nc.vector.reciprocal(rsd[:, 8:8 + nt], rsd[:, 0:nt]))
                for t0, t1 in ((0, 4), (4, 6))[:1 if nt == 4 else 2]:
                    nc.vector.tensor_tensor(dg[:, t0 * P:t1 * P].rearrange("p (t c) -> p t c", t=t1 - t0),
                                            ident.unsqueeze(1).to_broadcast([P, t1 - t0, P]),
                                            rsd[:, 8 + t0:8 + t1].unsqueeze(2).to_broadcast([P, t1 - t0, P]),
                                            ALU.mult).then_inc(dgd, 1)

            def operand(ni, w, gr):
                Av, mv = Avl[ni // 2], mvl[ni // 2]

                def scaled(k):
                    if k >= 3:
                        dve.wait_ge(*lo_done(ni, k - 3))
                    for g, (a, b) in enumerate(gr):
                        if k == 0:
                            dve.wait_ge(rbd, diags[ni] + g + 1)
                        ins = nc.vector.scalar_tensor_tensor(slot(k)[:, a:b], xT[:, k, a:b], Av[:, w, k, g:g + 1],
                                                             X0[:, a:b], ALU.mult, ALU.mult)
                    ins.then_inc(vsd, 1)

                scaled(0)
                scaled(1)
                for k in range(KD8):
                    if k not in POOL_LO:
                        dve.wait_ge(hid, 8 * ni + k + 1)
                        for g, (a, b) in enumerate(gr):
                            ins = nc.vector.scalar_tensor_tensor(hTv[:, 1, k, a:b], slot(k)[:, a:b],
                                                                 mv[:, 24 * w + k, g:g + 1],
                                                                 hTv[:, 0, k, a:b].bitcast(F32), ALU.add, ALU.subtract)
                        ins.then_inc(hlo, 1)
                    if k + 2 < KD8:
                        scaled(k + 2)

            def scales(l, w, n):
                gv = vecs(l, N1 if w == 0 else N2, 16).rearrange("p (k c) -> p k c", c=2)
                link(nc.vector.scalar_tensor_tensor(Avl[l][:, w, :, 0:n], mvl[l][:, 24 * w + 8:24 * w + 16, 0:n], 1.0,
                                                    gv[:, :, 0:n], ALU.add, ALU.mult))

            def modulation(l, src, a, b, n=2):
                bm = vecs(l, BM, 96).rearrange("p (m c) -> p m c", c=2)
                link(nc.vector.tensor_tensor(mvl[l][:, a:b, 0:n], src, bm[:, a:b, 0:n], ALU.add))

            def mod(row, tile, n, done, before):
                for c in range(n):
                    if before is not None and c == 0:
                        dve.wait_ge(*before)
                    ins = nc.vector.scalar_tensor_tensor(
                        (X0, X1)[c][:, :], row, 1.0, cb[:, c, :], ALU.mult, ALU.mult,
                        accum_out=msv[:, bass.ds(tile, 1), c:c + 1].rearrange("p a c -> p (a c)"))
                ins.then_inc(done, 1)

            def ring_mod(m, i, n):
                dve.wait_ge(m_landed[m % 2], 16 * i + 16 * (m // 2 + 1))
                mod(mraw[m % 2][:, :], 2 * i + (m + 16), n, m_used, (m_used, 2 * i + m) if m else (m_dv, 8))

            def residual(l, name, gate, ni=None):
                n0, cnt, _, _ = seg_at[l, name]
                width = groups_of(l, name)[-1][1]

                def add(r, i):
                    m = 2 * i + r
                    if ni is not None and r >= 2:
                        add_square(ni, m - 1, width)
                    dve.wait_ge(used, 2 * i + (n0 + r + 1))
                    for g, (a, b) in enumerate(groups_of(l, name)):
                        xk = flat(xT[:, bass.ds(m, 1), a:b])
                        ga = mvl[l][:, bass.ds(m + gate * 8, 1), g:g + 1].rearrange("p a c -> p (a c)")
                        ins = nc.vector.scalar_tensor_tensor(xk, G[(n0 + r) % 2][:, a:b], ga, xk, ALU.mult, ALU.add)
                    ins.then_inc(ev, 1)
                unit_loop(dve, l, name, add, head=2)

            nc.vector.memset(eps[:, :], EPS).then_inc(start_v, 1)
            nc.vector.memset(half[:, :], -0.5).then_inc(start_v, 1)
            dve.wait_ge(v_landed, 48)
            for l in range(LAYERS):
                link(nc.vector.tensor_scalar(nsink[:, 4 * l:4 * l + 4], vecs(l, SK, 4), -1.0, None, ALU.mult))
            lv = mraw[0][:, 0:512].rearrange("p (a b c) -> p a b c", a=4, b=2)
            lp = mraw[1][:, 0:256].rearrange("p (a c) -> p a c", a=4)
            link(nc.vector.tensor_tensor(lp, lv[:, :, 0, :], lv[:, :, 1, :], ALU.mult))
            link(nc.vector.reduce_sum(cst[:, 40:44], lp, AXX))
            for l in range(LAYERS):
                link(nc.vector.tensor_copy(cst[:, 70 + 10 * l:80 + 10 * l], vecs(l, DZ, 10)))
            z = cst[:, 70:90]
            link(nc.vector.tensor_scalar(cst[:, 50:70], z, -1.0, None, ALU.mult))
            link(nc.vector.tensor_scalar(lg[:, :], z, 0.0, None, ALU.min))
            nc.vector.tensor_tensor(cst[:, 0:20], z, cst[:, 50:70], ALU.max).then_inc(start_v, 1)
            dve.wait_ge(cb_ready, 2)
            dve.wait_ge(start_v, 3)
            for j in range(8):
                dve.wait_ge(m_first[j], 16)
                mod(first_mod[:, 2 * j + 1, :], 8 + j, 2, m_dv, (m_dv, j) if j else None)
            dve.wait_ge(start_a, 2)
            nc.vector.tensor_scalar(cst[:, 70:90], cst[:, 20:40], 1.0, None, ALU.add).then_inc(start_v, 1)
            lam_init = [0.8 - 0.6 * math.exp(-0.3 * l) for l in range(LAYERS)]
            for l in range(LAYERS):
                link(nc.vector.tensor_tensor(nlam[:, l:l + 1], cst[:, 45 + 2 * l:46 + 2 * l],
                                             cst[:, 44 + 2 * l:45 + 2 * l], ALU.subtract))
                link(nc.vector.tensor_scalar(nlam[:, l:l + 1], nlam[:, l:l + 1], -lam_init[l], None, ALU.add))
            dve.wait_ge(start_a, 3)
            link(nc.vector.tensor_tensor(lg[:, :], lg[:, :], cst[:, 50:70], ALU.subtract))
            for l in range(LAYERS):
                o = L[l]
                if l == 0:
                    dve.wait_ge(m_pe, 1)
                    modulation(0, G[0][:, 0:16].rearrange("p (m c) -> p m c", c=2), 0, 8)
                    dve.wait_ge(m_dv, 8)
                    modulation(0, msv[:, 8:16], 8, 16)
                    scales(0, 0, 2)
                norm(2 * l, 6)
                operand(2 * l, 0, [(0, LAT), (LAT, TOK)])
                if l == 0:
                    ring_mod(0, 0, 2)
                    ring_mod(1, 0, 2)
                    with dve.Fori(0, 17) as i:
                        ring_mod(2, i, 2)
                        ring_mod(3, i, 2)
                    dve.wait_ge(m_used, 36)
                    modulation(0, msv[:, 16:MODS], 16, MODS)
                    scales(0, 1, 2)
                dve.wait_ge(ropeld, 16 * (l + 1))
                for r in range(N_IN - N_KV):
                    for i in ROTARY_AT[l].get(r, []):
                        t, w = ROPED[i]
                        dve.wait_ge(o.rot, i + 1)
                        if i >= 2:
                            dve.wait_ge(o.rdone, i - 1)
                        c = R_S64 if w == HD else R_S32
                        nc.vector.tensor_tensor(ropeA[i % 2], X0[:, 512 * (i % 2):512 * (i % 2) + LAT],
                                                rope[:, c:c + LAT], ALU.mult).then_inc(o.rsin, 1)
                        dve.wait_ge(o.rsin, i + 1)
                        dve.wait_ge(o.rcos, i + 1)
                        nc.vector.tensor_tensor(pT[:, t, 0:LAT], ropeA[i % 2], ropeB[i % 2],
                                                ALU.add).then_inc(o.rdone, 1)
                    if r == 7:
                        dve.wait_ge(tabs_a, 13 * (l + 1))
                        link(nc.vector.tensor_scalar(kdec[:, :], kdec[:, :], CQ ** -0.5, None, ALU.mult))
                        for md, c in ((mdec, R_MG), (dback, R_ML)):
                            mv = md[:, :].rearrange("p (h c) -> p h c", h=4)
                            link(nc.vector.tensor_tensor(mv, mv, rope[:, c:c + P].unsqueeze(1).to_broadcast([P, 4, P]),
                                                         ALU.mult))
                        link(nc.vector.tensor_tensor(mdec[:, :], mdec[:, :], dback, ALU.add))
                        link(nc.vector.memset(fsc[:, :], 1.0))
                        nc.vector.tensor_scalar(fsc[:, 2:6], vecs(l, SG, 1).to_broadcast([P, 4]),
                                                1.0 - lam_init[l], None, ALU.mult).then_inc(o.tab, 1)
                dve.wait_ge(o.kt, 1)
                for d in range(2):
                    kb = kdec[:, 4 * d:4 * d + 4].unsqueeze(1).unsqueeze(3).to_broadcast([P, 6, 4, CQ])
                    nc.vector.tensor_tensor(kdk[:, d].rearrange("p n (h e) -> p n h e", h=4),
                                            X1[:, 0:TOK].rearrange("p (n h e) -> p n h e", n=6, h=4),
                                            kb, ALU.mult).then_inc(o.kd, 1)
                for i, (d, n, to, prev) in enumerate(STATE_CHAIN):
                    dve.wait_ge(o.kv, i + 1)
                    if i >= 2:
                        dve.wait_ge(o.st, i - 1)
                    dst = states[:, d, to, :] if prev is None else tm[:, 256 * (i % 2):256 * (i % 2) + 256]
                    src = (G[1] if i % 4 < 2 else X0)[:, 512 * (i % 2):512 * (i % 2) + 256]
                    if prev is not None:
                        link(nc.vector.tensor_tensor(dst, src, kc[:, K_BD:K_BD + 256], ALU.mult))
                        nc.vector.scalar_tensor_tensor(states[:, d, to, :], states[:, d, prev, :], gch[:, d:d + 1],
                                                       dst, ALU.mult, ALU.add).then_inc(o.st, 1)
                    else:
                        nc.vector.tensor_tensor(dst, src, kc[:, K_BD:K_BD + 256], ALU.mult).then_inc(o.st, 1)
                nt = tiles_of(l)
                for j in range(nt):
                    dve.wait_ge(o.at, j + 1)
                    if j >= 2:
                        dve.wait_ge(o.y, j - 1)
                    nc.vector.tensor_tensor(tm[:, 1024 + 512 * (j % 2):1536 + 512 * (j % 2)],
                                            X0[:, 512 * (j % 2):512 * (j % 2) + 512], mdec[:, :],
                                            ALU.mult).then_inc(o.ad, 1)
                steps = attention_steps(l)
                groups, ends = turn_groups(steps)
                windowed = [sum(st[0] == "A" for st in steps[:s + 1]) for s in range(len(steps))]
                last_b = max(s for s, st in enumerate(steps) if st[0] == "B")
                for s in range(len(steps) + 1):
                    if s >= 1:
                        kind, h, q, spans, keys = steps[s - 1]
                        p, nk, m = (s - 1) % 2, P * len(keys), 2 * (s - 1)
                        if kind == "B":
                            dve.wait_ge(o.ex[0], s)
                            dve.wait_ge(o.ex[1], s)
                            link(nc.vector.reciprocal(RC[:, m:m + 2], LS[:, m:m + 2]))
                            link(nc.vector.scalar_tensor_tensor(ES[:, m:m + 1], RC[:, m + 1:m + 2], LS[:, m:m + 1],
                                                                nlam[:, l:l + 1], ALU.mult, ALU.mult))
                            nc.vector.scalar_tensor_tensor(Pb[p][0][:, 0:nk], Pb[p][1][:, 0:nk], ES[:, m:m + 1],
                                                           Pb[p][0][:, 0:nk], ALU.mult, ALU.add).then_inc(o.wr, 1)
                        else:
                            for c in range(2):
                                dve.wait_ge(o.es[c], windowed[s - 1])
                            link(nc.vector.tensor_tensor(LS[:, m:m + 2], LS[:, m:m + 2], ES[:, m:m + 2], ALU.add))
                            nc.vector.reciprocal(RC[:, m:m + 2], LS[:, m:m + 2]).then_inc(o.wr, 2)
                    if s < len(steps):
                        kind, h, q, spans, keys = steps[s]
                        p, nk = s % 2, P * len(keys)
                        for c in range(2):
                            m = 2 * s + c
                            dve.wait_ge(o.sc[c], s + 1)
                            mx = nc.vector.reduce_max(NB[:, m:m + 1], G[c][:, 0:nk], AXX, negate=True)
                            if kind == "A":
                                link(mx)
                                mx = nc.vector.tensor_tensor(NB[:, m:m + 1], NB[:, m:m + 1],
                                                             nsink[:, 4 * l + 2 * h + c:][:, 0:1], ALU.min)
                            mx.then_inc(o.nb[c], 1)
                    if s == 1:
                        dve.wait_ge(o.yc, nt)
                        link(nc.vector.reduce_sum(cst[:, 48:48 + 4 * nt].rearrange("p (n h) -> p n h", h=4),
                                                  ysb[:, 0:nt], AXX))
                        nc.vector.tensor_scalar(cst[:, 48:48 + 4 * nt], cst[:, 48:48 + 4 * nt], 1.0 / 64, None,
                                                ALU.mult).then_inc(o.gd, 1)
                    if s == 5:
                        dve.wait_ge(o.gp, 2)
                        link(nc.vector.reduce_sum(cst[:, 72:72 + 4 * nt].rearrange("p (n h) -> p n h", h=4),
                                                  ysq[:, 0:nt], AXX))
                        nc.vector.tensor_scalar(cst[:, 72:72 + 4 * nt], cst[:, 72:72 + 4 * nt], 1.0 / 64, EPS,
                                                ALU.mult, ALU.add).then_inc(o.gd, 1)
                    if s == last_b + 2:
                        dve.wait_ge(o.oe, ends[last_b])
                        nc.vector.tensor_scalar(ssb[:, 0:4 * nt], ssb[:, 0:4 * nt], 1.0 / P, EPS,
                                                ALU.mult, ALU.add).then_inc(o.gd, 1)
                for i, f in enumerate(FMT):
                    dve.wait_ge(o.mh, i + 1)
                    nc.vector.scalar_tensor_tensor(hTv[:, 1, f, 0:nt * P], (X0, X1)[i % 2][:, 0:nt * P], fsc[:, f:f + 1],
                                                   hTv[:, 0, f, 0:nt * P].bitcast(F32), ALU.mult,
                                                   ALU.subtract).then_inc(o.ml, 1)
                residual(l, "out", 2, ni=2 * l + 1)
                norm(2 * l + 1, nt)
                gr = groups_of(l, "up0")
                operand(2 * l + 1, 1, gr)
                width = gr[-1][1]
                accs = (tm[:, 0:TOK], tm[:, TOK:2 * TOK])
                for hf in range(2):
                    n0 = seg_at[l, f"up{hf}"][0]
                    g0 = (2 * l + hf) * KH
                    if l == 0 and hf == 0:
                        dve.wait_ge(cb_ready, 3)
                    with dve.Fori(0, KH) as i:
                        for j in range(2):
                            u0 = 2 * g0 + j
                            dve.wait_ge(accr, 2 * i + (u0 + 1))
                            cw = vecs(l, CW, 176).rearrange("p (u w) -> p u w", w=4)[
                                :, bass.ds(2 * i + (hf * 22 + j), 1), :].rearrange("p a w -> p (a w)")
                            src = G[(n0 + j) % 2]
                            for a, b in gr:
                                ins = nc.vector.scalar_tensor_tensor(accs[j][:, a + 1:b], src[:, a:b - 1], cw[:, 0:1],
                                                                     accs[j][:, a + 1:b], ALU.mult, ALU.add)
                            ins.then_inc(convl, 1)
                            dve.wait_ge(convl, 2 * i + (u0 + 1))
                            for a, b in gr:
                                ins = nc.vector.scalar_tensor_tensor(accs[j][:, a:b - 1], src[:, a + 1:b], cw[:, 2:3],
                                                                     accs[j][:, a:b - 1], ALU.mult, ALU.add)
                            ins.then_inc(ev, 1)
                        dve.wait_ge(silud, i + (g0 + 1))
                        nc.vector.tensor_tensor(accs[0][:, 0:width], accs[0][:, 0:width], accs[1][:, 0:width],
                                                ALU.mult).then_inc(prodd, 1)
                        dve.wait_ge(ghi, i + (g0 + 1))
                        nc.vector.tensor_tensor(flat(gTv[:, 1, bass.ds(i, 1), 0:width]), accs[0][:, 0:width],
                                                flat(gTv[:, 0, bass.ds(i, 1), 0:width]).bitcast(F32),
                                                ALU.subtract).then_inc(glo, 1)
                        if l == 0:
                            ring_mod(36 + 22 * hf, i, 2 - hf)
                            ring_mod(37 + 22 * hf, i, 2 - hf)
                    if hf == 1 and l == 0:
                        dve.wait_ge(m_used, 80)
                        modulation(1, msv[:, MODS:MODS + 26], 0, 26)
                        modulation(1, msv[:, MODS + 26:2 * MODS, 0:1], 26, MODS, 1)
                        scales(1, 0, 2)
                        scales(1, 1, 1)
                    residual(l, f"down{hf}", 5, ni=2 * l + 2 if hf else None)
            norm(4, 4)
            dve.wait_ge(rbd, diags[4] + 1)
            for k in range(KD8):
                nc.vector.scalar_tensor_tensor(pT[:, 8 + k, 0:LAT], xT[:, k, 0:LAT], fing[:, k:k + 1], X0[:, 0:LAT],
                                               ALU.mult, ALU.mult).then_inc(fin, 1)

        @block.tensor
        def _(pe):
            def norm(ni, nt):
                pe.wait_ge(sqa, 6 * ni + 6)
                for part, src in enumerate((sacc, sq)):
                    if part:
                        pe.wait_ge(sqd, 8 * ni + 8)
                    for t in range(nt):
                        ins = nc.tensor.matmul(X1[:, t:t + 1], src[:, t * P:(t + 1) * P], ones[:, 0:1],
                                               start=(part == 0 and t == 0), stop=(part == 1 and t == nt - 1))
                ins.then_inc(ssd, 1)
                for g, (a, b) in enumerate(((0, LAT), (LAT, TOK))[:1 if nt == 4 else 2]):
                    pe.wait_ge(dgd, diags[ni] + g + 1)
                    nc.tensor.matmul(X0[:, a:b], ones, dg[:, a:b], start=True, stop=True).then_inc(rbd, 1)

            def start_unit(n, i=0):
                pe.wait_ge(w_lo, 2 * i + (n + 1))
                if n >= 2:
                    pe.wait_ge(ev, 2 * i + (n - 1))

            def k_tile(l, name, n, rhs, kk, first, last, lo=None):
                for pi, (ws, xs) in enumerate(((0, 0), (1, 0), (0, 1))):
                    if lo and xs:
                        pe.wait_ge(*lo)
                    for a, b in groups_of(l, name):
                        ins = nc.tensor.matmul(G[n % 2][:, a:b], Wv[n % 2][ws][:, kk, :], rhs[:, xs, kk, a:b],
                                               start=(first and pi == 0), stop=(last and pi == 2))
                if last:
                    ins.then_inc(used, 1)

            def multiply(l, name, r, i, rhs, gate=None, ks=None):
                n0, cnt, k, _ = seg_at[l, name]
                start_unit(n0 + r, i)
                for kn, kk in enumerate(ks or range(k)):
                    lo = None
                    if gate:
                        hi, lo = gate(kn)
                        pe.wait_ge(*hi)
                    k_tile(l, name, n0 + r, rhs, kk, kn == 0, kn == k - 1, lo)

            def segment(l, name, rhs, gate=None, ks=None):
                unit_loop(pe, l, name, lambda r, i: multiply(
                    l, name, r, i, rhs, gate if r == 0 and isinstance(i, int) else None, ks),
                    head=2 if gate else 0)

            def normed_segment(l, name, ni):
                n0, _, k, _ = seg_at[l, name]
                lag = LAG[groups_of(l, name)[-1][1]]
                start_unit(n0)
                for j in range(k + lag):
                    if j < k:
                        pe.wait_ge(hid, 8 * ni + j + 1)
                        k_tile(l, name, n0, hTv, j, j == 0, j == k - 1, lo_done(ni, j))
                    if j == lag:
                        start_unit(n0 + 1)
                    if j >= lag:
                        k_tile(l, name, n0 + 1, hTv, j - lag, j == lag, j == k + lag - 1)

                def rest(r, i):
                    if r >= 2:
                        multiply(l, name, r, i, hTv)
                unit_loop(pe, l, name, rest, head=2)

            pe.wait_ge(c_ready, 1)
            for c in range(2):
                for k in range(KD8):
                    ins = nc.tensor.matmul((X0, X1)[c][:, k * P:(k + 1) * P], csv[:, k, c:c + 1].to_broadcast([P, P]),
                                           ident, start=True, stop=True)
                ins.then_inc(c_spread, 1)
            for j in range(8):
                pe.wait_ge(m_first[j], 16)
                wj = first_mod[:, 2 * j, :].rearrange("p (k m) -> p k m", k=KD8)
                for k in range(KD8):
                    ins = nc.tensor.matmul(G[0][:, 2 * j:2 * j + 2], wj[:, k, :], csv[:, k, :],
                                           start=(k == 0), stop=(k == KD8 - 1))
            ins.then_inc(m_pe, 1)
            pe.wait_ge(m_dv, 8)
            pe.wait_ge(k_landed, 16)
            for l in range(LAYERS):
                o = L[l]
                nt = tiles_of(l)
                norm(2 * l, 6)
                normed_segment(l, "in_kv", 2 * l)
                for r in range(N_IN - N_KV):
                    multiply(l, "in_q", r, 0, hTv)
                    for i in ROTARY_AT[l].get(r, []):
                        t, w = ROPED[i]
                        pe.wait_ge(ev, in_sbuf(l, t))
                        if i >= 2:
                            pe.wait_ge(o.rsin, i - 1)
                        elif l == 0:
                            pe.wait_ge(m_used, 36)
                        sw = K_S64 if w == HD else K_S32
                        nc.tensor.matmul(X0[:, 512 * (i % 2):512 * (i % 2) + LAT], kc[:, sw:sw + P], pT[:, t, 0:LAT],
                                         start=True, stop=True).then_inc(o.rot, 1)

                def turn_values(i):
                    v = VALUE_ORDER[i]
                    if i == 2:
                        pe.wait_ge(o.kd, 2)
                    if i >= 3:
                        pe.wait_ge(o.vc, i - 1 if i > 3 else 1)
                    for t in range(6 if v < 7 else nt):
                        ins = nc.tensor.transpose(value_bank(i)[:, t * P:(t + 1) * P],
                                                  pT[:, T_VA + v, t * P:(t + 1) * P], ident)
                    ins.then_inc(o.vt, 1)

                pe.wait_ge(ev, seg_end[l, "in_q"])
                pe.wait_ge(o.rdone, 6)
                for n in range(6):
                    ins = nc.tensor.transpose(X1[:, n * P:(n + 1) * P], pT[:, T_KR, n * P:(n + 1) * P], ident)
                ins.then_inc(o.kt, 1)
                turn_values(0)
                turn_values(1)
                pe.wait_ge(o.kd, 2)
                pe.wait_ge(o.vc, 2)
                pe.wait_ge(o.rsin, len(ROPED))
                for i, (d, n, to, prev) in enumerate(STATE_CHAIN):
                    if i >= 4:
                        pe.wait_ge(o.st, i - 3)
                    nc.tensor.matmul((G[1] if i % 4 < 2 else X0)[:, 512 * (i % 2):512 * (i % 2) + 256],
                                     kdk[:, d, n, :], vt[:, n, V_C:V_C + 256], start=True, stop=True).then_inc(o.kv, 1)
                    if i + 2 < len(VALUE_ORDER):
                        turn_values(i + 2)
                pe.wait_ge(o.st, len(STATE_CHAIN))
                pe.wait_ge(o.rdone, len(ROPED))

                def ret_scores(j):
                    if j >= 2:
                        pe.wait_ge(o.ad, j - 1)
                    pe.wait_ge(o.qd, 3 * j + 1)
                    nc.tensor.matmul(X0[:, 512 * (j % 2):512 * (j % 2) + 512], pT[:, T_KR, j * P:(j + 1) * P],
                                     tm[:, 2048 + 512 * (j % 2):2560 + 512 * (j % 2)],
                                     start=True, stop=True).then_inc(o.at, 1)

                ret_scores(0)
                for j in range(nt):
                    if j + 1 < nt:
                        ret_scores(j + 1)
                    if j >= 2:
                        pe.wait_ge(o.yc, j - 1)
                    y = G[1][:, 512 * (j % 2):512 * (j % 2) + 256]
                    dirs = [d for d in range(2) if j != 4 + d]
                    pe.wait_ge(o.qd, 3 * j + 3)
                    for d in dirs:
                        nc.tensor.matmul(y, tm[:, 512 + 256 * (j % 2) + P * d:][:, 0:P], states[:, d, j, :],
                                         start=(d == dirs[0]), stop=False)
                    pe.wait_ge(o.ad, j + 1)
                    for h in range(4):
                        ins = nc.tensor.matmul(y[:, 64 * h:64 * h + 64], tm[:, 1024 + 512 * (j % 2) + h * P:][:, 0:P],
                                               vt[:, j, V_C + 64 * h:V_C + 64 * h + 64], start=False, stop=(h == 3))
                    ins.then_inc(o.y, 1)
                steps = attention_steps(l)
                groups, ends = turn_groups(steps)

                def mix_values(t):
                    s, c, vcol, w, _ = groups[t]
                    keys = steps[s][4]
                    pe.wait_ge(o.te, t + 1)
                    if t >= 2:
                        pe.wait_ge(o.oe, t - 1)
                    for i, kt in enumerate(keys):
                        ins = nc.tensor.matmul(X1[:, 512 * (t % 2):512 * (t % 2) + w],
                                               WT[t % 2][:, i * P:(i + 1) * P], vt[:, kt, vcol:vcol + w],
                                               start=(i == 0), stop=(i == len(keys) - 1))
                    ins.then_inc(o.pv, 1)

                pe.wait_ge(o.vc, len(VALUE_ORDER))
                for s in range(len(steps) + 1):
                    if s < len(steps):
                        kind, h, q, spans, keys = steps[s]
                        for c in range(2):
                            if s >= 1:
                                pe.wait_ge(o.ex[c], s)
                            elif c == 1:
                                pe.wait_ge(o.yc, nt)
                            b0 = HD * (c if kind == "B" else h)
                            tq, tk = (T_QB + h, T_KB + h) if kind == "B" else (T_QA + c, T_KA)
                            for sc0, k0, w, band in spans:
                                ins = nc.tensor.matmul(G[c][:, sc0:sc0 + w], pT[b0:b0 + HD, tq, q * P:(q + 1) * P],
                                                       pT[b0:b0 + HD, tk, k0:k0 + w], start=True, stop=band is None)
                                if band is not None:
                                    ins = nc.tensor.matmul(G[c][:, sc0:sc0 + w], ident, kc[:, band:band + w],
                                                           start=False, stop=True)
                            ins.then_inc(o.sc[c], 1)
                    if s >= 1:
                        for t in range(ends[s - 2] if s >= 2 else 0, ends[s - 1]):
                            _, c, _, _, _ = groups[t]
                            if steps[s - 1][0] == "B":
                                pe.wait_ge(o.wr, t + 1)
                            else:
                                pe.wait_ge(o.ex[c], s)
                            if t >= 1:
                                pe.wait_ge(o.te, t)
                            for i in range(len(steps[s - 1][4])):
                                ins = nc.tensor.transpose(X0[:, i * P:(i + 1) * P],
                                                          Pb[(s - 1) % 2][c][:, i * P:(i + 1) * P], ident)
                            ins.then_inc(o.tr, 1)
                            if t >= 1:
                                mix_values(t - 1)
                mix_values(len(groups) - 1)
                def turn_mixed(i):
                    f = FMT[i]
                    if i == 0:
                        pe.wait_ge(o.gp, 5)
                    elif i == 1:
                        pe.wait_ge(o.oe, len(groups))
                    else:
                        pe.wait_ge(o.ml, i - 1)
                    if i == 2:
                        pe.wait_ge(o.gp, 7)
                    for t in range(nt):
                        ins = nc.tensor.transpose((X0, X1)[i % 2][:, t * P:(t + 1) * P],
                                                  mix[:, t, f * P:(f + 1) * P], ident)
                    ins.then_inc(o.mt, 1)

                turn_mixed(0)
                turn_mixed(1)

                def mixed_ready(k):
                    if 1 <= k < KD8 - 1:
                        turn_mixed(k + 1)
                    return (o.mh, k + 1), (o.ml, k + 1)

                segment(l, "out", hTv, mixed_ready, FMT)
                norm(2 * l + 1, nt)
                for hf in range(2):
                    if hf == 0:
                        normed_segment(l, "up0", 2 * l + 1)
                    else:
                        segment(l, "up1", hTv)
                    segment(l, f"down{hf}", gTv, lambda k: [(g, (2 * l + hf) * KH + k + 1) for g in (ghi, glo)])
            norm(4, 4)


ROPED = ([(T_KA, HD)] + [(T_KB + h, HD) for h in range(4)] + [(T_KR, CQ)]
         + [(T_QA, HD), (T_QA + 1, HD)] + [(T_QB + h, HD) for h in range(4)] + [(T_QR, CQ)])
ROTARY_AT = [{4: [0, 1, 2], 5: [3, 4, 5], 6: [6, 7, 8], 7: [9, 10], 8: [11, 12]},
             {1: [0, 1], 2: [2, 3], 3: [4, 5], 4: [6, 7], 5: [8], 6: [9], 7: [10], 8: [11, 12]}]
VALUE_ORDER = [5, 6, 0, 1, 2, 3, 4, 7, 8]
POOL_LO = [1, 3, 5]
LAG = {TOK: 4, LAT: 5}
ATTN_SCALED = (T_QA, T_QA + 1, T_QB, T_QB + 1, T_QB + 2, T_QB + 3)
_F, _B = [4, 5, 0, 1, 2, 3], [5, 4, 3, 2, 1, 0]
STATE_CHAIN = []
for _i in range(5):
    STATE_CHAIN.append((0, _F[_i], _F[_i + 1], _F[_i] if _i else None))
    STATE_CHAIN.append((1, _B[_i], _B[_i + 1], _B[_i] if _i else None))


def kernel(**inputs):
    import numpy as _np
    import concourse.bacc as _bacc
    from concourse import mybir as _mybir
    from concourse.bass_utils import run_bass_kernel_spmd as _run

    a = {k: _np.asarray(v) for k, v in inputs.items()}
    cc = _np.concatenate
    xc = cc([a["x"][0], a["ctx"][0]], 0)
    xin = xc.T.reshape(8, 128, 768).transpose(1, 0, 2).reshape(128, -1)
    cin = _np.stack([a["c"][0], a["c_ctx"]], -1).reshape(8, 128, 2).transpose(1, 0, 2).reshape(128, -1)

    def unit(w, rows, cols):
        return w[rows][:, cols].reshape(-1, 128, 128).transpose(1, 0, 2).reshape(128, -1)

    A, dk = _np.arange, 64
    qa = cc([A(0, 64), A(128, 192), A(64, 128), A(192, 256)])
    cols = cc([A(256, 384), A(1024, 1536), A(2176, 2304), A(384, 512), A(1536, 2048), A(2304, 2560),
               A(2560, 2816), qa, A(512, 1024), A(2048, 2176)])
    k8, k11, wm, vin = [], [], [], []

    def row_unit(m):
        return a["w_mod"][m // MODS][:, 128 * (m % MODS):128 * (m % MODS) + 128].T

    for j in range(8):
        wm += [unit(a["w_mod"][0], slice(None), slice(128 * j, 128 * j + 128)), row_unit(8 + j)]
    wm += [row_unit(m) for m in range(16, 2 * MODS)]
    for l in range(LAYERS):
        full = slice(None)
        k8 += [unit(a["w_in"][l], full, cols[128 * t:128 * t + 128]) for t in range(N_IN)]
        k8 += [unit(a["w_out"][l], full, slice(128 * m, 128 * m + 128)) for m in range(8)]
        order = [s * 22 + j for j in range(22) for s in range(2)]
        k8 += [unit(a["w_up"][l], full, slice(128 * u, 128 * u + 128)) for u in order]
        for hf in range(2):
            rows = slice(KH * 128 * hf, KH * 128 * (hf + 1))
            k11 += [unit(a["w_down"][l], rows, slice(128 * m, 128 * m + 128)) for m in range(8)]

        def fm(v):
            return v.reshape(-1, 128).T

        conv = _np.stack([fm(a["conv_w"][l, 0]), fm(a["conv_w"][l, 1]), fm(a["conv_w"][l, 2]),
                          fm(a["conv_b"][l])], -1)[:, order].reshape(128, -1)
        z = a["ret_decay_logit"][l]
        vin += [_np.repeat(fm(a["b_mod"][l]), 2, 1), _np.repeat(fm(a["norm1_g"][l]), 2, 1),
                _np.repeat(fm(a["norm2_g"][l]), 2, 1), conv, a["diff_subln_g"][l][:, None],
                _np.broadcast_to(a["attn_sink"][l][None], (128, 4)),
                _np.broadcast_to(z.reshape(1, 8), (128, 8)), _np.repeat(z.T, 32, 0)]
    kin, rin = constants()
    cbin = _np.broadcast_to(cc([a["c"][0], a["c_ctx"]])[None], (128, 2048))
    arrays = {
        "x": xin, "c": cin, "cb": cbin, "wk8": _np.stack(k8), "wk11": _np.stack(k11), "wmod": _np.stack(wm),
        "vec": cc(vin, 1), "final_g": a["final_g"].reshape(8, 128).T,
        "lam": _np.broadcast_to(a["diff_lambda"].reshape(1, -1), (128, 512)), "consts": kin, "rope": rin,
    }
    arrays = {k: _np.ascontiguousarray(v) for k, v in arrays.items()}
    nc = _bacc.Bacc("TRN2", target_bir_lowering=False, num_devices=1)
    args = [nc.dram_tensor(f"in_{k}", v.shape, _mybir.dt.from_np(v.dtype), kind="ExternalInput").ap()
            for k, v in arrays.items()]
    args.append(nc.dram_tensor("out", (128, 8, 512), _mybir.dt.float32, kind="ExternalOutput").ap())
    trunk(nc, *args)
    r = _run(nc, [{f"in_{k}": v for k, v in arrays.items()}], core_ids=[0])
    return r.results[0]["out"].transpose(2, 1, 0).reshape(1, 512, 1024)
```
